# Optimizing a Trainium2 kernel written in Bass

```python
import jax
import jax.numpy as jnp
from jax import lax
import numpy as np
import math
import jax, jax.numpy as jnp

D_MODEL = 1024
BATCH = 1
SEQ = 256
DEPTH = 1

GRID_W = 64
CTX_LEN = 256
HEAD_DIM = 64
N_Q_HEADS = 8
N_KV_HEADS = 2
Q_PER_KV = N_Q_HEADS // N_KV_HEADS
ATTN_WIDTH = N_Q_HEADS * HEAD_DIM
KV_WIDTH = N_KV_HEADS * HEAD_DIM
WINDOW = 128
BLOCK = 128
ROPE_BASE = 10000.0
ROPE_PAIRS = HEAD_DIM // 4
CONV_WIDTH = D_MODEL // 2
CONV_K = 3
PEER_HEADS = 8
PEER_KEY_DIM = 256
PEER_N_KEYS = 128
PEER_N_EXPERTS = PEER_N_KEYS * PEER_N_KEYS
PEER_TOPK = 16
PEER_CHUNK = 128
N_MOD = 6
EPS = 1e-6
NEG_INF = -1e30

PROJ_SIZES = (ATTN_WIDTH, KV_WIDTH, KV_WIDTH, CONV_WIDTH, CONV_WIDTH, CONV_WIDTH, D_MODEL, D_MODEL)
PROJ_WIDTH = sum(PROJ_SIZES)
PROJ_SPLITS = tuple(int(s) for s in np.cumsum(PROJ_SIZES)[:-1])
KV_START = ATTN_WIDTH
KV_END = ATTN_WIDTH + 2 * KV_WIDTH


def rmsnorm(x, g):
    xf = x.astype(jnp.float32)
    y = xf * lax.rsqrt(jnp.mean(xf * xf, axis=-1, keepdims=True) + EPS)
    return (y * g.astype(jnp.float32)).astype(x.dtype)

def adaln_params(cond, w_mod, b_mod):
    m = jax.nn.silu(cond) @ w_mod + b_mod
    return jnp.split(m, N_MOD, axis=-1)

def axial_rope_tables(length):
    rows = length // GRID_W
    row = jnp.repeat(jnp.arange(rows, dtype=jnp.float32), GRID_W)
    col = jnp.tile(jnp.arange(GRID_W, dtype=jnp.float32), rows)
    inv_freq = ROPE_BASE ** (-jnp.arange(ROPE_PAIRS, dtype=jnp.float32) / ROPE_PAIRS)
    ang_r = row[:, None] * inv_freq
    ang_c = col[:, None] * inv_freq
    return (jnp.cos(ang_r), jnp.sin(ang_r), jnp.cos(ang_c), jnp.sin(ang_c))

def _rotate(xp, cos, sin):
    x1, x2 = jnp.split(xp, 2, axis=-1)
    c = cos[:, None, :]
    s = sin[:, None, :]
    return jnp.concatenate([x1 * c - x2 * s, x1 * s + x2 * c], axis=-1)

def apply_axial_rope(x, tables):
    cos_r, sin_r, cos_c, sin_c = tables
    xr, xc = jnp.split(x.astype(jnp.float32), 2, axis=-1)
    out = jnp.concatenate([_rotate(xr, cos_r, sin_r), _rotate(xc, cos_c, sin_c)], axis=-1)
    return out.astype(x.dtype)

def split_proj(z):
    return jnp.split(z, PROJ_SPLITS, axis=-1)

def windowed_attention(q, k, v, k_ctx, v_ctx, sink):
    B, L = q.shape[0], q.shape[1]
    nb = L // BLOCK
    scale = HEAD_DIM ** -0.5
    qb = q.reshape(B, nb, BLOCK, N_KV_HEADS, Q_PER_KV, HEAD_DIM)
    pad = ((0, 0), (BLOCK, BLOCK), (0, 0), (0, 0))
    kp = jnp.pad(k, pad).reshape(B, nb + 2, BLOCK, N_KV_HEADS, HEAD_DIM)
    vp = jnp.pad(v, pad).reshape(B, nb + 2, BLOCK, N_KV_HEADS, HEAD_DIM)
    kb = jnp.concatenate([kp[:, :-2], kp[:, 1:-1], kp[:, 2:]], axis=2)
    vb = jnp.concatenate([vp[:, :-2], vp[:, 1:-1], vp[:, 2:]], axis=2)
    s_loc = jnp.einsum('bnqhgd,bnkhd->bhgnqk', qb, kb, preferred_element_type=jnp.float32) * scale
    s_ctx = jnp.einsum('bnqhgd,bchd->bhgnqc', qb, k_ctx, preferred_element_type=jnp.float32) * scale
    blk = jnp.arange(nb)[:, None]
    qpos = blk * BLOCK + jnp.arange(BLOCK)[None, :]
    kpos = (blk - 1) * BLOCK + jnp.arange(3 * BLOCK)[None, :]
    valid = ((kpos[:, None, :] >= 0) & (kpos[:, None, :] < L)
             & (jnp.abs(qpos[:, :, None] - kpos[:, None, :]) <= WINDOW))
    s_loc = jnp.where(valid, s_loc, NEG_INF)
    sink_l = jnp.broadcast_to(
        sink.astype(jnp.float32).reshape(N_KV_HEADS, Q_PER_KV)[None, :, :, None, None, None],
        s_loc.shape[:-1] + (1,))
    p = jax.nn.softmax(jnp.concatenate([s_loc, s_ctx, sink_l], axis=-1), axis=-1)
    n_loc = 3 * BLOCK
    n_ctx = k_ctx.shape[1]
    p_loc = p[..., :n_loc].astype(v.dtype)
    p_ctx = p[..., n_loc:n_loc + n_ctx].astype(v.dtype)
    out = (jnp.einsum('bhgnqk,bnkhd->bnqhgd', p_loc, vb)
           + jnp.einsum('bhgnqc,bchd->bnqhgd', p_ctx, v_ctx))
    return out.reshape(B, L, ATTN_WIDTH)

def context_attention(q, k, v, sink):
    B, C = q.shape[0], q.shape[1]
    qg = q.reshape(B, C, N_KV_HEADS, Q_PER_KV, HEAD_DIM)
    s = jnp.einsum('bqhgd,bkhd->bhgqk', qg, k, preferred_element_type=jnp.float32) * HEAD_DIM ** -0.5
    sink_l = jnp.broadcast_to(
        sink.astype(jnp.float32).reshape(N_KV_HEADS, Q_PER_KV)[None, :, :, None, None],
        s.shape[:-1] + (1,))
    p = jax.nn.softmax(jnp.concatenate([s, sink_l], axis=-1), axis=-1)[..., :C].astype(v.dtype)
    out = jnp.einsum('bhgqk,bkhd->bqhgd', p, v)
    return out.reshape(B, C, ATTN_WIDTH)

def short_conv(z, w):
    L = z.shape[1]
    zp = jnp.pad(z, ((0, 0), (1, 1), (0, 0)))
    return zp[:, :L] * w[0] + zp[:, 1:L + 1] * w[1] + zp[:, 2:] * w[2]

def conv_branch(gate_b, gate_c, u, conv_w, w_conv_out):
    return (gate_b * short_conv(gate_c * u, conv_w)) @ w_conv_out

def merge_branches(y_attn, y_conv, ga, gc, w_mix_out):
    return (jax.nn.sigmoid(ga) * y_attn + jax.nn.sigmoid(gc) * y_conv) @ w_mix_out

def peer(h, w_q, sub_keys, u_tab, v_tab):
    B, L, D = h.shape
    tok = h.reshape(-1, PEER_CHUNK, D)

    def chunk(t):
        T = t.shape[0]
        qh = (t @ w_q).reshape(T, PEER_HEADS, 2, PEER_KEY_DIM // 2)
        s = jnp.einsum('thpd,hpnd->thpn', qh, sub_keys, preferred_element_type=jnp.float32)
        s_top, i_top = lax.top_k(s, PEER_TOPK)
        cand = s_top[:, :, 0, :, None] + s_top[:, :, 1, None, :]
        cand_idx = i_top[:, :, 0, :, None] * PEER_N_KEYS + i_top[:, :, 1, None, :]
        best, pos = lax.top_k(cand.reshape(T, PEER_HEADS, PEER_TOPK * PEER_TOPK), PEER_TOPK)
        idx = jnp.take_along_axis(cand_idx.reshape(T, PEER_HEADS, PEER_TOPK * PEER_TOPK), pos, axis=-1)
        g = jax.nn.softmax(best, axis=-1)
        ue = jnp.take(u_tab, idx, axis=0)
        ve = jnp.take(v_tab, idx, axis=0)
        act = jax.nn.gelu(jnp.einsum('thkd,td->thk', ue, t, preferred_element_type=jnp.float32),
                          approximate=False)
        return jnp.einsum('thk,thkd->td', (g * act).astype(t.dtype), ve)

    return lax.map(chunk, tok).reshape(B, L, D)

def trunk_layer(x, xc, c, c_ctx, w_mod, b_mod, n1, n2, w_in, sink, conv_w,
                w_attn_out, w_conv_out, w_mix_out, pw_q, p_keys, p_u, p_v, rope, update_ctx):
    B, L, _ = x.shape
    C = xc.shape[1]
    sh1, sc1, g1, sh2, sc2, g2 = [m[:, None, :] for m in adaln_params(c, w_mod, b_mod)]
    csh1, csc1, cg1, csh2, csc2, cg2 = adaln_params(c_ctx, w_mod, b_mod)

    hc = rmsnorm(xc, n1) * (1 + csc1) + csh1
    if update_ctx:
        qc, kc, vc, gbc, gcc, uc, gac, gvc = split_proj(hc @ w_in)
    else:
        kc, vc = jnp.split(hc @ w_in[:, KV_START:KV_END], 2, axis=-1)
    kc = kc.reshape(B, C, N_KV_HEADS, HEAD_DIM)
    vc = vc.reshape(B, C, N_KV_HEADS, HEAD_DIM)

    h = rmsnorm(x, n1) * (1 + sc1) + sh1
    q, k, v, gb, gcv, u, ga, gv = split_proj(h @ w_in)
    q = apply_axial_rope(q.reshape(B, L, N_Q_HEADS, HEAD_DIM), rope)
    k = apply_axial_rope(k.reshape(B, L, N_KV_HEADS, HEAD_DIM), rope)
    v = v.reshape(B, L, N_KV_HEADS, HEAD_DIM)
    y_attn = windowed_attention(q, k, v, kc, vc, sink) @ w_attn_out
    y_conv = conv_branch(gb, gcv, u, conv_w, w_conv_out)
    x = x + g1 * merge_branches(y_attn, y_conv, ga, gv, w_mix_out)
    h2 = rmsnorm(x, n2) * (1 + sc2) + sh2
    x = x + g2 * peer(h2, pw_q, p_keys, p_u, p_v)

    if update_ctx:
        yc_attn = context_attention(qc.reshape(B, C, N_Q_HEADS, HEAD_DIM), kc, vc, sink) @ w_attn_out
        yc_conv = conv_branch(gbc, gcc, uc, conv_w, w_conv_out)
        xc = xc + cg1 * merge_branches(yc_attn, yc_conv, gac, gvc, w_mix_out)
        hc2 = rmsnorm(xc, n2) * (1 + csc2) + csh2
        xc = xc + cg2 * peer(hc2, pw_q, p_keys, p_u, p_v)
    return x, xc

def first_inputs(seed: int = 0) -> dict:
    key = jax.random.key(seed)
    ks = jax.random.split(key, 19)

    def nrm(k, shape, s):
        return jax.random.normal(k, shape, jnp.float32) * s

    return {
        "x": nrm(ks[0], (BATCH, SEQ, D_MODEL), 1.0),
        "c": nrm(ks[1], (BATCH, D_MODEL), 1.0),
        "ctx": nrm(ks[2], (BATCH, CTX_LEN, D_MODEL), 1.0),
        "c_ctx": nrm(ks[3], (D_MODEL,), 1.0),
        "w_mod": nrm(ks[4], (DEPTH, D_MODEL, N_MOD * D_MODEL), D_MODEL ** -0.5),
        "b_mod": nrm(ks[5], (DEPTH, N_MOD * D_MODEL), 0.02),
        "norm1_g": 1.0 + nrm(ks[6], (DEPTH, D_MODEL), 0.02),
        "norm2_g": 1.0 + nrm(ks[7], (DEPTH, D_MODEL), 0.02),
        "w_in": nrm(ks[8], (DEPTH, D_MODEL, PROJ_WIDTH), D_MODEL ** -0.5),
        "attn_sink": nrm(ks[9], (DEPTH, N_Q_HEADS), 1.0),
        "conv_w": nrm(ks[10], (DEPTH, CONV_K, CONV_WIDTH), CONV_K ** -0.5),
        "w_attn_out": nrm(ks[11], (DEPTH, ATTN_WIDTH, D_MODEL), ATTN_WIDTH ** -0.5),
        "w_conv_out": nrm(ks[12], (DEPTH, CONV_WIDTH, D_MODEL), CONV_WIDTH ** -0.5),
        "w_mix_out": nrm(ks[13], (DEPTH, D_MODEL, D_MODEL), D_MODEL ** -0.5),
        "peer_w_q": nrm(ks[14], (DEPTH, D_MODEL, PEER_HEADS * PEER_KEY_DIM), D_MODEL ** -0.5),
        "peer_sub_keys": nrm(ks[15], (DEPTH, PEER_HEADS, 2, PEER_N_KEYS, PEER_KEY_DIM // 2),
                             (PEER_KEY_DIM // 2) ** -0.5),
        "peer_u": nrm(ks[16], (DEPTH, PEER_N_EXPERTS, D_MODEL), D_MODEL ** -0.5),
        "peer_v": nrm(ks[17], (DEPTH, PEER_N_EXPERTS, D_MODEL), 0.5),
        "final_g": 1.0 + nrm(ks[18], (D_MODEL,), 0.02),
    }

def first_block(x, c, ctx, c_ctx, w_mod, b_mod, norm1_g, norm2_g, w_in, attn_sink, conv_w,
              w_attn_out, w_conv_out, w_mix_out, peer_w_q, peer_sub_keys, peer_u, peer_v, final_g):
    rope = axial_rope_tables(x.shape[1])
    xc = ctx
    for l in range(DEPTH):
        x, xc = trunk_layer(x, xc, c, c_ctx, w_mod[l], b_mod[l], norm1_g[l], norm2_g[l], w_in[l],
                            attn_sink[l], conv_w[l], w_attn_out[l], w_conv_out[l], w_mix_out[l],
                            peer_w_q[l], peer_sub_keys[l], peer_u[l], peer_v[l], rope,
                            l < DEPTH - 1)
    return rmsnorm(x, final_g)


CHUNK = 64
N_META = 16
Q_BLOCK = 128

MLA_HEADS = 8
MLA_Q_RANK = 384
MLA_KV_RANK = 256
MLA_NOPE = 128
MLA_ROPE = 64
MLA_V = 128
ROPE_HALF = MLA_ROPE // 2
ROPE_THETA = 10000.0

GLA_HEADS = 4
GLA_DK = D_MODEL // 2
GLA_DV = D_MODEL
GLA_HK = GLA_DK // GLA_HEADS
GLA_HV = GLA_DV // GLA_HEADS
GLA_GATE_RANK = 16
GLA_TAU = 16.0
GLA_CHUNK = 16

PEER_NKEYS = 128
PEER_EXPERTS = PEER_NKEYS * PEER_NKEYS
PEER_QDIM = 256
PEER_HALF = PEER_QDIM // 2
PEER_BLOCK = 16

SPLITS = (MLA_Q_RANK, MLA_KV_RANK, MLA_ROPE, GLA_DK, GLA_DK, GLA_DV, GLA_GATE_RANK, GLA_DV, D_MODEL, D_MODEL)
D_IN = MLA_Q_RANK + MLA_KV_RANK + MLA_ROPE + 2 * GLA_DK + GLA_DV + GLA_GATE_RANK + GLA_DV + 2 * D_MODEL


def rmsnorm_2(x, g):
    x32 = x.astype(jnp.float32)
    y = x32 * lax.rsqrt(jnp.mean(x32 * x32, axis=-1, keepdims=True) + EPS)
    return (y * g.astype(jnp.float32)).astype(x.dtype)

def rope_tables(n):
    inv_freq = ROPE_THETA ** (-jnp.arange(ROPE_HALF, dtype=jnp.float32) / ROPE_HALF)
    ang = jnp.arange(n, dtype=jnp.float32)[:, None] * inv_freq[None, :]
    return jnp.cos(ang), jnp.sin(ang)

def rope(x, cos, sin):
    x32 = x.astype(jnp.float32)
    x1, x2 = x32[..., :ROPE_HALF], x32[..., ROPE_HALF:]
    return jnp.concatenate([x1 * cos - x2 * sin, x2 * cos + x1 * sin], axis=-1).astype(x.dtype)

def mla_branch(c_q, c_kv, k_pe, q_norm, w_uq, kv_norm, w_ukv, qn_nope, qn_pe, kn_nope, kn_pe, cos, sin, cid):
    B, L, _ = c_q.shape
    q = (rmsnorm_2(c_q, q_norm) @ w_uq).reshape(B, L, MLA_HEADS, MLA_NOPE + MLA_ROPE)
    kv = (rmsnorm_2(c_kv, kv_norm) @ w_ukv).reshape(B, L, MLA_HEADS, MLA_NOPE + MLA_V)
    q_nope = rmsnorm_2(q[..., :MLA_NOPE], qn_nope)
    q_pe = rope(rmsnorm_2(q[..., MLA_NOPE:], qn_pe), cos[:, None, :], sin[:, None, :])
    k_nope = rmsnorm_2(kv[..., :MLA_NOPE], kn_nope)
    v = kv[..., MLA_NOPE:]
    k_pe = rope(rmsnorm_2(k_pe, kn_pe), cos, sin)
    scale = (MLA_NOPE + MLA_ROPE) ** -0.5
    lp = cid.shape[0]
    nb = lp // Q_BLOCK
    pad = ((0, 0), (0, lp - L), (0, 0), (0, 0))
    qn_b = jnp.pad(q_nope, pad).reshape(B, nb, Q_BLOCK, MLA_HEADS, MLA_NOPE).transpose(1, 0, 2, 3, 4)
    qp_b = jnp.pad(q_pe, pad).reshape(B, nb, Q_BLOCK, MLA_HEADS, MLA_ROPE).transpose(1, 0, 2, 3, 4)
    cq_b = cid.reshape(nb, Q_BLOCK)
    cid_k = cid[:L]

    def attend(blk):
        qn, qp, cq = blk
        s = (jnp.einsum('bqhd,bkhd->bhqk', qn, k_nope) + jnp.einsum('bqhd,bkd->bhqk', qp, k_pe)).astype(jnp.float32) * scale
        mask = cid_k[None, :] <= cq[:, None]
        s = jnp.where(mask, s, -jnp.inf)
        w = jax.nn.softmax(s, axis=-1).astype(v.dtype)
        return jnp.einsum('bhqk,bkhd->bqhd', w, v)

    out = lax.map(attend, (qn_b, qp_b, cq_b))
    out = out.transpose(1, 0, 2, 3, 4).reshape(B, lp, MLA_HEADS * MLA_V)
    return out[:, :L]

def gla_branch(gq, gk, gv, ga, gg, w_a2, b_a, g_norm):
    B, L, _ = gq.shape
    nc = L // GLA_CHUNK
    q = gq.reshape(B, L, GLA_HEADS, GLA_HK) * (GLA_HK ** -0.5)
    k = gk.reshape(B, L, GLA_HEADS, GLA_HK)
    v = gv.reshape(B, L, GLA_HEADS, GLA_HV)
    log_a = jax.nn.log_sigmoid((ga @ w_a2 + b_a).astype(jnp.float32)) / GLA_TAU
    log_a = log_a.reshape(B, L, GLA_HEADS, GLA_HK)

    def to_chunks(t):
        return t.reshape(B, nc, GLA_CHUNK, GLA_HEADS, t.shape[-1]).transpose(1, 0, 3, 2, 4).astype(jnp.float32)

    tri = jnp.tril(jnp.ones((GLA_CHUNK, GLA_CHUNK), dtype=bool))

    def step(S, inp):
        qc, kc, vc, lac = inp
        bcum = jnp.cumsum(lac, axis=2)
        o_inter = jnp.einsum('bhcd,bhde->bhce', qc * jnp.exp(bcum), S)
        diff = bcum[:, :, :, None, :] - bcum[:, :, None, :, :]
        decay = jnp.exp(jnp.where(tri[None, None, :, :, None], diff, -jnp.inf))
        A = jnp.einsum('bhid,bhjd,bhijd->bhij', qc, kc, decay)
        o_intra = jnp.einsum('bhij,bhje->bhie', A, vc)
        b_last = bcum[:, :, -1]
        k_dec = kc * jnp.exp(b_last[:, :, None, :] - bcum)
        S = jnp.exp(b_last)[..., None] * S + jnp.einsum('bhcd,bhce->bhde', k_dec, vc)
        return S, o_inter + o_intra

    S0 = jnp.zeros((B, GLA_HEADS, GLA_HK, GLA_HV), jnp.float32)
    _, o = lax.scan(step, S0, (to_chunks(q), to_chunks(k), to_chunks(v), to_chunks(log_a)))
    o = o.transpose(1, 0, 3, 2, 4).reshape(B, L, GLA_HEADS, GLA_HV).astype(gq.dtype)
    o = rmsnorm_2(o, g_norm).reshape(B, L, GLA_DV)
    return o * jax.nn.silu(gg)

def peer_ffn(h, w_q, sub_keys, u_tab, v_tab):
    B, L, D = h.shape
    q = (h @ w_q).reshape(B, L, PEER_HEADS, 2, PEER_HALF)
    s = jnp.einsum('blhpd,pnd->blhpn', q, sub_keys).astype(jnp.float32)
    top_s, top_i = lax.top_k(s, PEER_TOPK)
    cand_s = top_s[..., 0, :, None] + top_s[..., 1, None, :]
    cand_i = top_i[..., 0, :, None] * PEER_NKEYS + top_i[..., 1, None, :]
    best_s, best_pos = lax.top_k(cand_s.reshape(B, L, PEER_HEADS, PEER_TOPK * PEER_TOPK), PEER_TOPK)
    idx = jnp.take_along_axis(cand_i.reshape(B, L, PEER_HEADS, PEER_TOPK * PEER_TOPK), best_pos, axis=-1)
    gate = jax.nn.softmax(best_s, axis=-1)
    nb = L // PEER_BLOCK

    def blocks(t):
        return t.reshape((B, nb, PEER_BLOCK) + t.shape[2:]).swapaxes(0, 1)

    def expert_block(inp):
        hb, ib, gb = inp
        u = u_tab[ib]
        act = jax.nn.gelu(jnp.einsum('bpd,bphkd->bphk', hb, u).astype(jnp.float32), approximate=False)
        coef = (act * gb).astype(hb.dtype)
        return jnp.einsum('bphk,bphkd->bpd', coef, v_tab[ib])

    out = lax.map(expert_block, (blocks(h), blocks(idx), blocks(gate)))
    return out.swapaxes(0, 1).reshape(B, L, D)

def second_inputs(seed: int = 0) -> dict:
    key = jax.random.key(seed)
    ks = jax.random.split(key, 24)
    f32 = jnp.float32

    def nrm(k, shape, fan_in):
        return jax.random.normal(k, shape, f32) * (fan_in ** -0.5)

    def gain(k, shape):
        return 1.0 + 0.02 * jax.random.normal(k, shape, f32)

    return {
        "x": jax.random.normal(ks[0], (BATCH, SEQ, D_MODEL), f32),
        "meta": jax.random.normal(ks[1], (N_META, D_MODEL), f32),
        "norm_mix": gain(ks[2], (DEPTH, D_MODEL)),
        "w_in": nrm(ks[3], (DEPTH, D_MODEL, D_IN), D_MODEL),
        "mla_q_norm": gain(ks[4], (DEPTH, MLA_Q_RANK)),
        "mla_w_uq": nrm(ks[5], (DEPTH, MLA_Q_RANK, MLA_HEADS * (MLA_NOPE + MLA_ROPE)), MLA_Q_RANK),
        "mla_kv_norm": gain(ks[6], (DEPTH, MLA_KV_RANK)),
        "mla_w_ukv": nrm(ks[7], (DEPTH, MLA_KV_RANK, MLA_HEADS * (MLA_NOPE + MLA_V)), MLA_KV_RANK),
        "qn_nope": gain(ks[8], (DEPTH, MLA_NOPE)),
        "qn_pe": gain(ks[9], (DEPTH, MLA_ROPE)),
        "kn_nope": gain(ks[10], (DEPTH, MLA_NOPE)),
        "kn_pe": gain(ks[11], (DEPTH, MLA_ROPE)),
        "gla_w_a2": nrm(ks[12], (DEPTH, GLA_GATE_RANK, GLA_DK), GLA_GATE_RANK),
        "gla_b_a": 0.1 * jax.random.normal(ks[13], (DEPTH, GLA_DK), f32),
        "gla_norm": gain(ks[14], (DEPTH, GLA_HV)),
        "w_o_mla": nrm(ks[15], (DEPTH, MLA_HEADS * MLA_V, D_MODEL), MLA_HEADS * MLA_V),
        "w_o_gla": nrm(ks[16], (DEPTH, GLA_DV, D_MODEL), GLA_DV),
        "w_out": nrm(ks[17], (DEPTH, D_MODEL, D_MODEL), D_MODEL),
        "norm_ffn": gain(ks[18], (DEPTH, D_MODEL)),
        "peer_w_q": nrm(ks[19], (DEPTH, D_MODEL, PEER_HEADS * PEER_QDIM), D_MODEL),
        "peer_keys": nrm(ks[20], (DEPTH, 2, PEER_NKEYS, PEER_HALF), PEER_HALF),
        "peer_u": nrm(ks[21], (DEPTH, PEER_EXPERTS, D_MODEL), D_MODEL),
        "peer_v": nrm(ks[22], (DEPTH, PEER_EXPERTS, D_MODEL), PEER_HEADS),
    }

def second_block(x, meta, norm_mix, w_in, mla_q_norm, mla_w_uq, mla_kv_norm, mla_w_ukv, qn_nope, qn_pe, kn_nope, kn_pe, gla_w_a2, gla_b_a, gla_norm, w_o_mla, w_o_gla, w_out, norm_ffn, peer_w_q, peer_keys, peer_u, peer_v):
    B = x.shape[0]
    h = jnp.concatenate([jnp.broadcast_to(meta.astype(x.dtype)[None], (B, N_META, D_MODEL)), x], axis=1)
    L = h.shape[1]
    lp = -(-L // Q_BLOCK) * Q_BLOCK
    pos = jnp.arange(lp)
    cid = jnp.where(pos < N_META, 0, 1 + (pos - N_META) // CHUNK)
    cos, sin = rope_tables(L)
    offsets = [int(o) for o in np.cumsum(SPLITS)[:-1]]
    for l in range(DEPTH):
        n = rmsnorm_2(h, norm_mix[l])
        parts = jnp.split(n @ w_in[l], offsets, axis=-1)
        c_q, c_kv, k_pe, gq, gk, gv, ga, gg, gate_a, gate_b = parts
        y_a = mla_branch(c_q, c_kv, k_pe, mla_q_norm[l], mla_w_uq[l], mla_kv_norm[l], mla_w_ukv[l], qn_nope[l], qn_pe[l], kn_nope[l], kn_pe[l], cos, sin, cid)
        y_b = gla_branch(gq, gk, gv, ga, gg, gla_w_a2[l], gla_b_a[l], gla_norm[l])
        mix = jax.nn.sigmoid(gate_a) * (y_a @ w_o_mla[l]) + jax.nn.sigmoid(gate_b) * (y_b @ w_o_gla[l])
        h = h + mix @ w_out[l]
        h = h + peer_ffn(rmsnorm_2(h, norm_ffn[l]), peer_w_q[l], peer_keys[l], peer_u[l], peer_v[l])
    return h[:, N_META:]


def setup_inputs(seed=0):
    out = dict(first_inputs(seed))
    for name, value in second_inputs(seed + 1).items():
        if name != "x":
            out[name + "_2"] = value
    return out


def reference(
    x, c, ctx, c_ctx, w_mod, b_mod, norm1_g, norm2_g, w_in, attn_sink, conv_w, w_attn_out,
    w_conv_out, w_mix_out, peer_w_q, peer_sub_keys, peer_u, peer_v, final_g, meta_2, norm_mix_2,
    w_in_2, mla_q_norm_2, mla_w_uq_2, mla_kv_norm_2, mla_w_ukv_2, qn_nope_2, qn_pe_2, kn_nope_2,
    kn_pe_2, gla_w_a2_2, gla_b_a_2, gla_norm_2, w_o_mla_2, w_o_gla_2, w_out_2, norm_ffn_2,
    peer_w_q_2, peer_keys_2, peer_u_2, peer_v_2,
):
    x = first_block(
        x, c, ctx, c_ctx, w_mod, b_mod, norm1_g, norm2_g, w_in, attn_sink, conv_w, w_attn_out,
        w_conv_out, w_mix_out, peer_w_q, peer_sub_keys, peer_u, peer_v, final_g,
    )
    return second_block(
        x, meta_2, norm_mix_2, w_in_2, mla_q_norm_2, mla_w_uq_2, mla_kv_norm_2, mla_w_ukv_2,
        qn_nope_2, qn_pe_2, kn_nope_2, kn_pe_2, gla_w_a2_2, gla_b_a_2, gla_norm_2, w_o_mla_2,
        w_o_gla_2, w_out_2, norm_ffn_2, peer_w_q_2, peer_keys_2, peer_u_2, peer_v_2,
    )


_drawn_inputs = setup_inputs


def setup_inputs(seed=0):
    import zlib

    import numpy as np

    out = dict(_drawn_inputs(seed))
    spreads = {}
    factors = {'attn_sink': 5.771,
     'mla_q_norm_2': 8.0,
     'mla_kv_norm_2': 7.13,
     'qn_nope_2': 8.0,
     'qn_pe_2': 8.0,
     'kn_nope_2': 8.0,
     'kn_pe_2': 8.0,
     'gla_norm_2': 30.064,
     'gla_b_a_2': 3.889,
     'norm_ffn_2': 8.0}
    for name, (base, spread) in spreads.items():
        noise = np.random.default_rng([zlib.crc32(name.encode()), seed]).standard_normal(out[name].shape)
        drawn = base * np.exp(spread * noise) if base else spread * noise
        out[name] = jnp.asarray(drawn.astype(out[name].dtype))
    for name, factor in factors.items():
        out[name] = (out[name] * factor).astype(out[name].dtype)
    return out
```

```python
import math

import numpy as np

import concourse.bass as bass
from concourse import mybir

F32 = mybir.dt.float32
F32R = mybir.dt.float32r
U32 = mybir.dt.uint32
ALU = mybir.AluOpType
ACT = mybir.ActivationFunctionType
AX_X = mybir.AxisListType.X

P = 128
D = 1024
KD = D // P
T = 256
NT = T // P
CTX = 256
META = 16
TM = T + META
EPS = 1e-6
NEG = -1.0e30
HEAD = 64
GROUP = 4
WINDOW = 128
HEADS = 8
TOPK = 16
NKEY = 128
TAU = 16.0
GLA_HEADS = 4
LEVELS = 7
RING = 4
UNIT = KD * P
HLRING = 2
OHRING = 4
NPROJ = 3
B_STAT = (3, 7)
B_SCORE = (4, 5)
B_PT = 6
B_OUT = 7



def stream_order():
    order = [("mod", 16), ("in_kvq", 6)]
    mods, fills = 32, 28
    plan = [("fill1", 1)] * fills
    out = []
    for i, p in enumerate(plan):
        out.append(p)
        out += [("mod", 1)] * ((mods * (i + 1)) // fills - (mods * i) // fills)
    order += out
    order += [("attn_out", 4), ("conv_out", 4), ("mix_out", 8), ("wq1", 16), ("u1", 128), ("v1", 128),
              ("cq", 3), ("ckv", 2), ("kpe", 1), ("uq", 6), ("ukv_k", 2), ("ukv_v", 2),
              ("gq", 4), ("gk", 4), ("ga", 1), ("gv", 8), ("gate_a", 8), ("gg", 8), ("gate_b", 8),
              ("wo_mla", 8), ("wo_gla", 8), ("w_out", 8), ("wq2", 16), ("u2", 128), ("v2", 128)]
    return order


def unit_table():
    at, n = {}, 0
    for key, count in stream_order():
        at.setdefault(key, []).extend(range(n, n + count))
        n += count
    return at, n


def pack_stream(a):
    def std(w):
        n = w.shape[1] // P
        return w.reshape(KD, P, n, P).transpose(2, 1, 0, 3).reshape(n, P, UNIT)

    def short(w, per):
        k, n = w.shape[0] // P, w.shape[1] // P
        u = w.reshape(k, P, n // per, per, P).transpose(2, 1, 3, 0, 4).reshape(n // per, P, per * k * P)
        return np.concatenate([u, np.zeros((n // per, P, UNIT - per * k * P), np.float32)], axis=2)

    w_in = a["w_in"][0]
    q = w_in[:, :512].reshape(D, 2, GROUP, HEAD).transpose(0, 2, 1, 3).reshape(D, 512)
    k, v = w_in[:, 512:640], w_in[:, 640:768]
    gb, gc, u = w_in[:, 768:1280], w_in[:, 1280:1792], w_in[:, 1792:2304]
    ga, gv = w_in[:, 2304:3328], w_in[:, 3328:4352]
    attn_out = a["w_attn_out"][0].reshape(2, GROUP, HEAD, D).transpose(1, 0, 2, 3).reshape(512, D)
    w2 = a["w_in_2"][0]
    c = np.cumsum([0, 384, 256, 64, 512, 512, 1024, 16, 1024, 1024, 1024])
    part = lambda i: w2[:, c[i]:c[i + 1]]
    uq = a["mla_w_uq_2"][0].reshape(384, 8, 192)
    uq = np.concatenate([uq[:, :, :128].reshape(384, 1024), uq[:, :, 128:].reshape(384, 512)], axis=1)
    ukv = a["mla_w_ukv_2"][0].reshape(256, 8, 256)
    ukv_v = ukv[:, :, 128:].reshape(2, P, 2, 512).transpose(2, 1, 0, 3).reshape(2, P, UNIT)

    def peer_u(t):
        return t.reshape(P, P, KD, P).transpose(1, 3, 2, 0).reshape(P, P, UNIT)

    def peer_v(t):
        return t.reshape(P, P, D).transpose(1, 0, 2)

    parts = {
        "mod": std(a["w_mod"][0]), "in_kvq": std(np.concatenate([k, v, q], axis=1)),
        "fill1": std(np.concatenate([gc, u, gb, ga, gv], axis=1)),
        "attn_out": short(attn_out, 2), "conv_out": short(a["w_conv_out"][0], 2),
        "mix_out": std(a["w_mix_out"][0]), "wq1": std(a["peer_w_q"][0]),
        "u1": peer_u(a["peer_u"][0]), "v1": peer_v(a["peer_v"][0]),
        "cq": std(part(0)), "ckv": std(part(1)), "kpe": std(np.concatenate([part(2), part(2)], axis=1)),
        "uq": short(uq, 2), "ukv_k": short(ukv[:, :, :128].reshape(256, 1024), 4), "ukv_v": ukv_v,
        "gq": std(part(3)), "gk": std(part(4)), "gv": std(part(5)),
        "ga": std(np.concatenate([part(6), np.zeros((D, P - 16), np.float32)], axis=1)),
        "gg": std(part(7)), "gate_a": std(part(8)), "gate_b": std(part(9)),
        "wo_mla": std(a["w_o_mla_2"][0]), "wo_gla": std(a["w_o_gla_2"][0]), "w_out": std(a["w_out_2"][0]),
        "wq2": std(a["peer_w_q_2"][0]), "u2": peer_u(a["peer_u_2"][0]), "v2": peer_v(a["peer_v_2"][0]),
    }
    at, n = unit_table()
    out = np.empty((n, P, UNIT), np.float32)
    for key, where in at.items():
        assert len(where) == len(parts[key]), (key, len(where), len(parts[key]))
        out[where] = parts[key]
    return out



VECS = [("b_mod", 48), ("norm1", 8), ("norm2", 8), ("final", 8), ("norm_mix", 8), ("q_norm", 3), ("kv_norm", 2),
        ("qn_nope", 1), ("qn_pe", 1), ("kn_nope", 1), ("kn_pe", 1), ("b_a", 4), ("gla_norm", 2), ("norm_ffn", 8),
        ("conv_w", 12), ("sink", 8), ("cond", 16)]
CONSTS = [("ident", 128), ("blk64", 128), ("iota", 128), ("delta", 8)]
CONSTS1 = [("rot", 128), ("cos", 256), ("sin", 256), ("mask", 1024)]
CONSTS2 = [("rot", 128), ("cos", 272), ("sin", 272), ("mask", 544), ("gla_mask", 128 * (LEVELS + 1))]


def offsets(table):
    at, n = {}, 0
    for key, size in table:
        at[key] = (n, size)
        n += size
    return at, n


def pack_vectors(a):
    col = lambda v: v.reshape(-1, P).T
    twice = lambda v: np.concatenate([v, v]).reshape(P, 1)
    parts = {
        "b_mod": col(a["b_mod"][0]), "norm1": col(a["norm1_g"][0]), "norm2": col(a["norm2_g"][0]),
        "final": col(a["final_g"]), "norm_mix": col(a["norm_mix_2"][0]), "q_norm": col(a["mla_q_norm_2"][0]),
        "kv_norm": col(a["mla_kv_norm_2"][0]), "qn_nope": col(a["qn_nope_2"][0]), "qn_pe": twice(a["qn_pe_2"][0]),
        "kn_nope": col(a["kn_nope_2"][0]), "kn_pe": twice(a["kn_pe_2"][0]), "b_a": col(a["gla_b_a_2"][0]),
        "gla_norm": col(a["gla_norm_2"][0]), "norm_ffn": col(a["norm_ffn_2"][0]),
        "conv_w": a["conv_w"][0].reshape(12, P).T, "sink": np.tile(a["attn_sink"][0], (P, 1)),
        "cond": np.stack([col(a["c"][0]), col(a["c_ctx"])], axis=2).reshape(P, 16),
    }
    return np.ascontiguousarray(np.concatenate([parts[k] for k, _ in VECS], axis=1))


def rotation(half):
    r = np.zeros((P, P), np.float32)
    for i in range(P):
        first = i % (2 * half) < half
        r[i, i + half if first else i - half] = -1.0 if first else 1.0
    return r.T


def shape_constants():
    i = np.arange(P)
    f32 = np.float32
    common = {
        "ident": np.eye(P), "blk64": i[:, None] // 64 == i[None, :] // 64,
        "iota": np.tile(np.arange(P), (P, 1)), "delta": i[:, None] // TOPK == np.arange(HEADS)[None, :],
    }
    pos = np.arange(T)
    freq = (f32(10000.0) ** (-(np.arange(16, dtype=f32)) / f32(16))).astype(f32)
    place = np.where((i % HEAD < 32)[:, None], pos[None, :] // 64, pos[None, :] % 64).astype(f32)
    angle = (place * freq[i % 16][:, None]).astype(f32)
    mask = np.zeros((NT, P, 512))
    for t in range(NT):
        far = np.abs(t * P + i[:, None] - np.arange(T)[None, :]) > WINDOW
        mask[t, :, :T] = np.where(far, NEG, 0.0)
    first = {"rot": rotation(16), "cos": np.cos(angle), "sin": np.sin(angle),
             "mask": mask.transpose(1, 0, 2).reshape(P, -1)}
    where = np.concatenate([np.arange(META, TM), np.arange(META)]).astype(f32)
    freq = (f32(10000.0) ** (-(np.arange(32, dtype=f32)) / f32(32))).astype(f32)
    angle = (where[None, :] * freq[i % 32][:, None]).astype(f32)
    mask = np.zeros((NT, P, TM))
    for t in range(NT):
        later = np.arange(T)[None, :] // 64 > (t * P + i[:, None]) // 64
        mask[t, :, :T] = np.where(later, NEG, 0.0)
    levels = np.zeros((LEVELS + 1, P, P))
    for n in range(LEVELS):
        size = 1 << n
        j, q = i[:, None] // size, i[None, :] // size
        levels[n] = (j % 2 == 0) & (q == j + 1)
    levels[LEVELS] = np.eye(P)
    second = {"rot": rotation(32), "cos": np.cos(angle), "sin": np.sin(angle),
              "mask": mask.transpose(1, 0, 2).reshape(P, -1), "gla_mask": levels.transpose(1, 0, 2).reshape(P, -1)}
    join = lambda parts, table: np.ascontiguousarray(
        np.concatenate([np.asarray(parts[k], np.float32).reshape(P, n) for k, n in table], axis=1))
    return join(common, CONSTS), join(first, CONSTS1), join(second, CONSTS2)


def feature_major(x):
    return np.ascontiguousarray(x.T.reshape(-1, P, x.shape[0]).transpose(1, 0, 2))



class Tile:

    def __init__(self, unit, ready, pairs, rows, cols, engine, take):
        self.unit, self.ready, self.pairs, self.rows, self.cols = unit, ready, pairs, rows, cols
        self.engine, self.take = engine, take


def build(nc, stream, xT, ctxT, metaT, vectors, common, consts1, consts2, keys1, keys2, w_a2, out):
    units, n_units = unit_table()

    top = [(nc.sbuf_base + 31) // 32 * 8]

    def place(name, shape, dtype=F32, at=None):
        size = math.prod(shape[1:])
        where = top[0] if at is None else at
        t = nc.alloc_sbuf_tensor_at(name, shape, dtype, offset=4 * where)
        if at is None:
            top[0] += (size + 7) // 8 * 8
        return t, where

    ring, _ = place("ring", [P, RING, UNIT])
    resid, _ = place("resid", [P, KD, T])
    s_area, _ = place("s_area", [P, NT * HEADS * 2 * P])
    arena, _ = place("arena", [P, P * T])
    gbuf, gbuf_at = place("gbuf", [P, 10240])
    hl, _ = place("hl", [P, HLRING, 2, UNIT], F32R, at=gbuf_at)
    hsplit, _ = place("hsplit", [P, 2, KD, T], F32R, at=gbuf_at + 2 * HLRING * UNIT)
    csplit, _ = place("csplit", [P, 2, 2, T], F32R, at=gbuf_at + 2 * HLRING * UNIT + 2 * KD * T)
    vec_at, n_vec = offsets(VECS)
    con_at, n_con = offsets(CONSTS)
    vec, _ = place("vec", [P, n_vec])
    con, _ = place("con", [P, n_con])
    mod, _ = place("mod", [P, 48, 2])
    scale1, _ = place("scale1", [P, KD, 2])
    scale2, _ = place("scale2", [P, KD])
    small, _ = place("small", [P, 32])
    gate_f, _ = place("gate_f", [P, 2, 2, P])
    onesbuf, _ = place("onesbuf", [P, P])
    topbuf, _ = place("topbuf", [P, 2, TOPK])
    idxbuf, _ = place("idxbuf", [P, 2, TOPK], U32)
    keybuf, _ = place("keybuf", [P, 2 * P])
    tmpbuf, _ = place("tmpbuf", [P, 2 * P])
    bestbuf, _ = place("bestbuf", [P, TOPK])
    zsum, _ = place("zsum", [P, 2, HEADS * NT])
    assert top[0] * 4 <= nc.sbuf_usable_end, (top[0] * 4, nc.sbuf_usable_end)

    def v_(name, i=0, n=1):
        a = vec_at[name][0] + i
        return vec[:, a:a + n]

    def c_(name):
        a, n = con_at[name]
        return con[:, a:a + n]

    ident, blk64, iota, delta, ones = c_("ident"), c_("blk64"), c_("iota"), c_("delta"), onesbuf[:, :]

    class Space:

        def __init__(self, tensor, size):
            self.t, self.n, self.at = tensor, size, 0

        def take(self, *shape):
            n = math.prod(shape)
            a = self.at
            self.at += n
            assert self.at <= self.n, (self.at, self.n)
            ap = self.t[:, a:a + n]
            if len(shape) == 2:
                ap = ap.rearrange("p (a b) -> p a b", a=shape[0])
            if len(shape) == 3:
                ap = ap.rearrange("p (a b c) -> p a b c", a=shape[0], b=shape[1])
            return ap

    ps = nc.alloc_psum_tensor("ps", [P, 8, 512], F32)

    sems = {}

    def S(name):
        if name not in sems:
            sems[name] = nc.alloc_semaphore(name)
        return sems[name]

    def wait(eng, name, value):
        if value > 0:
            eng.wait_ge(S(name), value)

    ring_full = [f"ring_full{s}" for s in range(RING)]

    def arrival(unit):
        return ring_full[unit % RING], 16 * (unit // RING + 1)

    def slot(unit):
        return ring[:, unit % RING, :]

    A1 = Space(arena, P * T)
    xin = A1.take(KD, T + CTX)
    sq1 = A1.take(KD, T + CTX)
    h1 = A1.take(KD, T + CTX)
    q_raw, q_rot = A1.take(4, T), A1.take(4, T)
    k_raw, k_rot = A1.take(T + CTX), A1.take(T + CTX)
    rope_tmp = A1.take(TM)
    v_tok = A1.take(4, P)
    gc_b, z_b, conv_b, cg_b = A1.take(4, T), A1.take(4, T), A1.take(4, T), A1.take(4, T)
    sga, sgv, mixed = A1.take(KD, T), A1.take(KD, T), A1.take(KD, T)
    attn1 = A1.take(4, T)
    G1 = Space(gbuf, 10240)
    con1_at, n_con1 = offsets(CONSTS1)
    con1 = G1.take(n_con1)
    probs1, pt1 = G1.take(2, 512), G1.take(2, 512)
    rs1 = G1.take(2, 512)
    cprod = G1.take(2, T)
    silu_c = G1.take(KD, 2)
    sig_c = G1.take(KD, 2)

    A2 = Space(arena, P * T)
    hin, n2, sq2 = A2.take(KD, TM), A2.take(KD, TM), A2.take(KD, TM)
    cq_b, cqn, ckv_b, ckvn = A2.take(3, T), A2.take(3, T), A2.take(2, TM), A2.take(2, TM)
    kpe_raw, kpe_n, kpe_rot = A2.take(TM), A2.take(TM), A2.take(TM)
    qnope, qnope_n = A2.take(HEADS, T), A2.take(HEADS, T)
    qpe, qpe_rot = A2.take(4, T), A2.take(4, T)
    knope, knope_n = A2.take(HEADS, TM), A2.take(HEADS, TM)
    v2_flat = A2.take(3 * D)
    v2 = v2_flat.rearrange("p (a d) -> p a d", a=3)
    attn2 = A2.take(HEADS, T)
    G2 = Space(gbuf, 10240)
    con2_at, n_con2 = offsets(CONSTS2)
    con2 = G2.take(n_con2)
    probs2, pt2 = G2.take(2, TM), G2.take(2, 3 * P)
    rs2 = G2.take(2, TM)
    ga_b, wa2_b = G2.take(TM), G2.take(512)
    la, lb = G2.take(GLA_HEADS, TM), G2.take(GLA_HEADS, TM)
    silu_g = G2.take(KD, T)
    SA = Space(s_area, NT * HEADS * 2 * P)
    sgate_a, sgate_b = SA.take(KD, T), SA.take(KD, T)
    gq, gk = A2.take(GLA_HEADS, T), A2.take(GLA_HEADS, TM)
    gv = A2.take(3, D)
    A3 = Space(arena, P * T)
    A3.take(3 * KD, TM)
    gd2 = [A3.take(GLA_HEADS, P) for _ in range(2)]
    gqd = [A3.take(GLA_HEADS, P) for _ in range(2)]
    gkd = [A3.take(GLA_HEADS, P) for _ in range(2)]
    amat = [A3.take(GLA_HEADS, P) for _ in range(NT)]
    atmp = A3.take(GLA_HEADS, P)
    qdec = A3.take(GLA_HEADS, T)
    kdec = [A3.take(GLA_HEADS, META), A3.take(GLA_HEADS, P)]
    kdecT = [A3.take(GLA_HEADS, P), A3.take(GLA_HEADS, P)]
    state = [A3.take(GLA_HEADS, 256), A3.take(GLA_HEADS, 256)]
    blast = A3.take(2, GLA_HEADS)
    o_gla = A3.take(KD, T)
    og_n = A3.take(KD, T)
    assert A3.at <= A2.at - 3 * D - GLA_HEADS * (T + TM) - HEADS * T
    mixed2 = v2_flat[:, 0:KD * T].rearrange("p (k t) -> p k t", k=KD)

    def con1_(name):
        a, n = con1_at[name]
        return con1[:, a:a + n]

    def con2_(name):
        a, n = con2_at[name]
        return con2[:, a:a + n]

    scores = s_area[:, :].rearrange("p (t h x) -> p t h x", t=NT, h=HEADS)
    q_area = arena[:, P * T - 16 * T:]
    keys_area = arena[:, P * T - 16 * T - 16 * P:P * T - 16 * T].rearrange("p (j n) -> p j n", j=16)
    acts = arena
    oh1 = gbuf[:, 0:4096].rearrange("p (r t i) -> p r t i", r=OHRING, t=8)
    oh2 = gbuf[:, 4096:6144].rearrange("p (r t i) -> p r t i", r=2, t=8)
    gbd = gbuf[:, 6144:8192].rearrange("p (r t i) -> p r t i", r=2, t=8)
    wrow = gbuf[:, 8192:10240].rearrange("p (r t i) -> p r t i", r=4, t=4)
    turned_tmp = gbuf[:, 8192:10240]

    tiles = []
    taken = {"act": 0, "dve": 0}
    group_of = {}

    def tile(group, unit, ready, pairs, rows, cols, engine, take):
        t = Tile(unit, ready, pairs, rows, cols, engine, take)
        taken[engine] += 1
        t.n, t.seq, t.bank = len(tiles), taken[engine], len(tiles) % NPROJ
        tiles.append(t)
        group_of.setdefault(group, []).append(t.n)

    def cols(unit, k, m=P, at=0):
        return slot(unit)[:, at + k * P:at + k * P + m]

    def std_pairs(unit, rhs, k=KD, at=0):
        return [(slot(unit)[:, at + i * P:at + (i + 1) * P], rhs[:, i]) for i in range(k)]

    def take_copy(dst):
        def f(kind, eng, src):
            return eng.copy(dst, src) if kind == "act" else eng.tensor_copy(dst, src)
        return f

    def take_func(dst, func):
        def f(kind, eng, src):
            return eng.activation(dst, src, func)
        return f

    def take_times(dst, other, scalar=None):
        def f(kind, eng, src):
            if scalar is None:
                return eng.tensor_tensor(dst, src, other, ALU.mult)
            return eng.scalar_tensor_tensor(dst, src, scalar, other, ALU.mult, ALU.mult)
        return f

    mod_units = units["mod"]

    def mod_tile(group, n):
        u = mod_units[n]
        tile(group, u, ("silu_ready", 1), std_pairs(u, silu_c), P, 2, "dve",
             lambda kind, eng, src: eng.tensor_scalar(mod[:, n, :], src, v_("b_mod", n), None, ALU.add))

    for n in range(16):
        mod_tile("mod_a", n)

    u0 = units["in_kvq"]
    tile("kvq1", u0[0], ("h1_ready", 1), std_pairs(u0[0], h1), P, T + CTX, "act", take_copy(k_raw))

    def v_pairs(u, src, t, n):
        return [(src[:, k, t:t + n], slot(u)[:, k * P:(k + 1) * P]) for k in range(KD)]

    for t in range(4):
        tile("kvq1", u0[1], ("h1_ready", 1), v_pairs(u0[1], h1, t * P, P), P, P, "act", take_copy(v_tok[:, t, :]))
    for j in range(4):
        tile("kvq1", u0[2 + j], ("h1_ready", 1), std_pairs(u0[2 + j], h1[:, :, 0:T]), P, T, "act",
             take_copy(q_raw[:, j, :]))
    kv1_taken = taken["act"]

    next_mod = 16
    f1 = units["fill1"]

    def conv_take(i):
        def f(kind, eng, src):
            chain(eng.tensor_tensor(z_b[:, i, :], src, gc_b[:, i, :], ALU.mult), eng)
            w = lambda tap: v_("conv_w", tap * 4 + i)
            chain(eng.tensor_scalar(conv_b[:, i, :], z_b[:, i, :], w(1), None, ALU.mult), eng)
            chain(eng.scalar_tensor_tensor(conv_b[:, i, 1:T], z_b[:, i, 0:T - 1], w(0), conv_b[:, i, 1:T],
                                           ALU.mult, ALU.add), eng)
            return eng.scalar_tensor_tensor(conv_b[:, i, 0:T - 1], z_b[:, i, 1:T], w(2), conv_b[:, i, 0:T - 1],
                                            ALU.mult, ALU.add)
        return f

    for i in range(28):
        u = f1[i]
        pairs = std_pairs(u, h1[:, :, 0:T])
        if i < 4:
            tile("fill1", u, None, pairs, P, T, "dve", take_copy(gc_b[:, i, :]))
        elif i < 8:
            tile("fill1", u, None, pairs, P, T, "dve", conv_take(i - 4))
        elif i < 12:
            tile("fill1", u, None, pairs, P, T, "dve", take_times(cg_b[:, i - 8, :], conv_b[:, i - 8, :]))
        elif i < 20:
            tile("fill1", u, None, pairs, P, T, "act", take_func(sga[:, i - 12, :], ACT.Sigmoid))
        else:
            tile("fill1", u, None, pairs, P, T, "act", take_func(sgv[:, i - 20, :], ACT.Sigmoid))
        while next_mod < 48 and (i == 27 or mod_units[next_mod] < f1[i + 1]):
            mod_tile("fill1", next_mod)
            next_mod += 1
    assert next_mod == 48

    sig1_taken = taken["act"]

    def ao_take(n):
        def f(kind, eng, src):
            if n == 0:
                wait(eng, "taken_act", sig1_taken)
            return eng.tensor_tensor(mixed[:, n, :], src, sga[:, n, :], ALU.mult)
        return f

    def add_take(dst, gate, tmp):
        def f(kind, eng, src):
            chain(eng.tensor_tensor(tmp, src, gate, ALU.mult), eng)
            return eng.tensor_tensor(dst, dst, tmp, ALU.add)
        return f

    for i, u in enumerate(units["attn_out"]):
        for s in range(2):
            tile("out1", u, ("attn_out_ready", 4), std_pairs(u, attn1, 4, at=s * 4 * P), P, T, "dve", ao_take(2 * i + s))
    for i, u in enumerate(units["conv_out"]):
        for s in range(2):
            n = 2 * i + s
            tile("out1", u, ("taken_dve", "conv"), std_pairs(u, cg_b, 4, at=s * 4 * P), P, T, "dve",
                 add_take(mixed[:, n, :], sgv[:, n, :], cprod[:, n % 2, :]))
    mixed_taken = taken["dve"]

    def resid_take(n, scalar):
        def f(kind, eng, src):
            dst = resid[:, n, :]
            if scalar is None:
                return eng.tensor_tensor(dst, src, dst, ALU.add)
            return eng.scalar_tensor_tensor(dst, src, scalar(n), dst, ALU.mult, ALU.add)
        return f

    for n, u in enumerate(units["mix_out"]):
        tile("out1", u, ("taken_dve", mixed_taken), std_pairs(u, mixed), P, T, "dve",
             resid_take(n, lambda n: mod[:, 16 + n, 0:1]))

    h_full = gbuf[:, 8192:10240].rearrange("p (k t) -> p k t", k=KD)

    def wq_tiles(b):
        for j, u in enumerate(units[f"wq{b}"]):
            tile(f"wq{b}", u, ("peer_in", b), std_pairs(u, h_full), P, T, "act" if j % 2 else "dve",
                 take_copy(q_area[:, j * T:(j + 1) * T]))
    wq_tiles(1)
    wq_taken = {1: dict(taken)}

    def group2(key, dst, ready, rhs, n, engine="act", k=KD, per=1, make=take_copy, width=None):
        for i, u in enumerate(units[key]):
            for s in range(per):
                m = i * per + s
                tile(key, u, ready, std_pairs(u, rhs, k, at=s * k * P), P, n, engine, make(dst[:, m, :]))

    nT = n2[:, :, 0:T]
    group2("cq", cq_b, ("n2_ready", 1), nT, T)
    group2("ckv", ckv_b, ("n2_ready", 1), n2, TM)
    tile("kpe", units["kpe"][0], ("n2_ready", 1), std_pairs(units["kpe"][0], n2), P, TM, "act", take_copy(kpe_raw))
    c_taken = taken["act"]
    for i, u in enumerate(units["uq"]):
        for s in range(2):
            m = 2 * i + s
            dst = qnope[:, m, :] if m < HEADS else qpe[:, m - HEADS, :]
            tile("uq", u, ("cq_ready", 1), std_pairs(u, cqn, 3, at=s * 3 * P), P, T, "act", take_copy(dst))
    uq_taken = taken["act"]
    group2("ukv_k", knope, ("ckv_ready", 1), ckvn, TM, k=2, per=4)
    uk_taken = taken["act"]
    KT2 = [(0, P), (P, P), (T, META)]
    for half, u in enumerate(units["ukv_v"]):
        for t, (a, n) in enumerate(KT2):
            pairs = [(ckvn[:, k, a:a + n], slot(u)[:, k * 512:(k + 1) * 512]) for k in range(2)]
            tile("ukv_v", u, None, pairs, n, 512, "act", take_copy(v2[0:n, t, half * 512:(half + 1) * 512]))
    v2_taken = taken["act"]

    def gq_take(dst):
        return lambda kind, eng, src: eng.activation(dst, src, ACT.Copy, scale=float(P) ** -0.5)
    group2("gq", gq, None, nT, T, make=gq_take)
    group2("gk", gk, None, n2, TM)
    tile("ga", units["ga"][0], None, std_pairs(units["ga"][0], n2), P, TM, "act", take_copy(ga_b))
    ga_taken = taken["act"]
    for i, u in enumerate(units["gv"]):
        for t, (a, n) in enumerate(KT2):
            tile("gv", u, None, v_pairs(u, n2, a, n), n, P, "act", take_copy(gv[0:n, t, i * P:(i + 1) * P]))
    gv_taken = taken["act"]
    group2("gate_a", sgate_a, None, nT, T, make=lambda d: take_func(d, ACT.Sigmoid))
    group2("gg", silu_g, None, nT, T, make=lambda d: take_func(d, ACT.Silu))
    group2("gate_b", sgate_b, None, nT, T, make=lambda d: take_func(d, ACT.Sigmoid))
    gates2_taken = taken["act"]

    def wo_mla_take(n):
        def f(kind, eng, src):
            if n == 0:
                wait(eng, "taken_act", gates2_taken)
            return eng.tensor_tensor(mixed2[:, n, :], src, sgate_a[:, n, :], ALU.mult)
        return f
    for n, u in enumerate(units["wo_mla"]):
        tile("wo_mla", u, ("attn_out_ready", 4 + HEADS), std_pairs(u, attn2), P, T, "dve", wo_mla_take(n))
    for n, u in enumerate(units["wo_gla"]):
        tile("wo_gla", u, ("gla_ready", 1), std_pairs(u, og_n), P, T, "dve",
             add_take(mixed2[:, n, :], sgate_b[:, n, :], rs2[:, n % 2, 0:T]))
    mixed2_taken = taken["dve"]
    for n, u in enumerate(units["w_out"]):
        tile("w_out", u, ("taken_dve", mixed2_taken), std_pairs(u, mixed2), P, T, "dve", resid_take(n, None))
    wq_tiles(2)
    wq_taken[2] = dict(taken)

    conv_taken = max(tiles[n].seq for n in group_of["fill1"] if tiles[n].engine == "dve" and tiles[n].cols == T)
    for t in tiles:
        if t.ready and t.ready[1] == "conv":
            t.ready = (t.ready[0], conv_taken)
    last_tile = {t.unit: t.n for t in tiles}

    chained = {}

    def chain(ins, eng):
        key = "dve_chain" if eng is dve_eng[0] else "act_chain"
        chained[key] = chained.get(key, 0) + 1
        ins.then_inc(S(key), 1)
        eng.wait_ge(S(key), chained[key])

    dve_eng = [None]

    def pe_tiles(pe, numbers):
        for n in numbers:
            t = tiles[n]
            pe.wait_ge(S(arrival(t.unit)[0]), arrival(t.unit)[1])
            if t.ready:
                wait(pe, *t.ready)
            if n >= NPROJ:
                before = tiles[n - NPROJ]
                wait(pe, "taken_" + before.engine, before.seq)
            last = len(t.pairs) - 1
            for i, (lhs, rhs) in enumerate(t.pairs):
                mm = pe.matmul(ps[0:t.rows, t.bank, 0:t.cols], lhs, rhs, start=(i == 0), stop=(i == last))
            mm.then_inc(S("tile_done"), 1)

    def take_tiles(kind, eng, numbers):
        for n in numbers:
            t = tiles[n]
            if t.engine == kind:
                wait(eng, "tile_done", n + 1)
                t.take(kind, eng, ps[0:t.rows, t.bank, 0:t.cols]).then_inc(S("taken_" + kind), 1)

    def pieces(group, parts):
        n = group_of[group] if isinstance(group, str) else [m for g in group for m in group_of[g]]
        return [n[len(n) * i // parts:len(n) * (i + 1) // parts] for i in range(parts)]

    norm_count = [0, 0]

    class Norm:

        def __init__(self, src, squares, n, cols, groups, lhs, width, root, ready, gain, dst=None, done=None, apply=None):
            self.src = src
            self.squares = squares
            self.n = n
            self.cols = cols
            self.groups = groups
            self.lhs = lhs
            self.width = width
            self.root = root
            self.ready = ready
            self.gain = gain
            self.dst = dst
            self.done = done
            self.apply = apply
            self.id, self.g0 = norm_count[0], norm_count[1]
            norm_count[0] += 1
            norm_count[1] += len(groups)

        def act(self, eng):
            for r in self.ready:
                wait(eng, *r)
            eng.activation(self.squares[:, 0:self.n, 0:self.cols], self.src, ACT.Square).then_inc(S("norm_squared"), 1)
            for g in range(len(self.groups)):
                wait(eng, "norm_inverted", self.g0 + g + 1)
                r = self.root[:, (self.g0 + g) % 2, 0:self.cols]
                eng.sqrt(r, r).then_inc(S("norm_rooted"), 1)

        def pe(self, eng):
            wait(eng, "norm_squared", self.id + 1)
            for g, group in enumerate(self.groups):
                wait(eng, "norm_inverted", self.g0 + g - 1)
                bank = B_STAT[(self.g0 + g) % 2]
                for i, k in enumerate(group):
                    mm = eng.matmul(ps[:, bank, 0:self.cols], self.lhs, self.squares[:, k, 0:self.cols],
                                    start=(i == 0), stop=(i == len(group) - 1))
                mm.then_inc(S("norm_summed"), 1)

        def dve(self, eng):
            def invert(g):
                r = self.root[:, (self.g0 + g) % 2, 0:self.cols]
                wait(eng, "norm_summed", self.g0 + g + 1)
                chain(eng.tensor_scalar(r, ps[:, B_STAT[(self.g0 + g) % 2], 0:self.cols], 1.0 / self.width, EPS,
                                        ALU.mult, ALU.add), eng)
                eng.reciprocal(r, r).then_inc(S("norm_inverted"), 1)

            for r in self.ready:
                wait(eng, *r)
            n = len(self.groups)
            invert(0)
            for g in range(n):
                if g + 1 < n:
                    invert(g + 1)
                wait(eng, "norm_rooted", self.g0 + g + 1)
                root = self.root[:, (self.g0 + g) % 2, 0:self.cols]
                if self.apply:
                    self.apply(eng, root)
                    continue
                for k in self.groups[g]:
                    ins = eng.scalar_tensor_tensor(self.dst(k), self.src[:, k, :], self.gain(k), root, ALU.mult, ALU.mult)
                if g == n - 1 and self.done:
                    ins.then_inc(S(self.done), 1)
                else:
                    chain(ins, eng)

    def flat_groups(n):
        return [[k] for k in range(n)]

    def apply_h1(eng, root):
        for half in range(2):
            for k in range(KD):
                a = slice(half * T, (half + 1) * T)
                ins = eng.scalar_tensor_tensor(h1[:, k, a], xin[:, k, a], scale1[:, k, half:half + 1], root[:, a],
                                               ALU.mult, ALU.mult)
        chain(ins, eng)
        for half in range(2):
            for k in range(KD):
                a = slice(half * T, (half + 1) * T)
                ins = eng.tensor_scalar(h1[:, k, a], h1[:, k, a], mod[:, k, half:half + 1], None, ALU.add)
        ins.then_inc(S("h1_ready"), 1)

    def apply_h2(eng, root):
        for k in range(KD):
            ins = eng.scalar_tensor_tensor(h_full[:, k, :], resid[:, k, :], scale2[:, k:k + 1], root, ALU.mult, ALU.mult)
        chain(ins, eng)
        for k in range(KD):
            ins = eng.tensor_scalar(h_full[:, k, :], h_full[:, k, :], mod[:, 24 + k, 0:1], None, ALU.add)
        ins.then_inc(S("peer_in"), 1)

    norm_x = Norm(xin, sq1, KD, T + CTX, [list(range(KD))], ones, D, rs1,
                  [("x_loaded", 32), ("ones_ready", 1)], None, apply=apply_h1)
    out1_taken = tiles[group_of["out1"][-1]].seq
    norm_h2 = Norm(resid[:, :, :], sq1, KD, T, [list(range(KD))], ones, D, rs1, [("taken_dve", out1_taken)], None,
                   apply=apply_h2)
    norm_final = Norm(resid[:, :, :], sq2, KD, T, [list(range(KD))], ones, D, rs2, [("peer_out", 1)],
                      lambda k: v_("final", k), dst=lambda k: hin[:, k, 0:T], done="x1_ready")
    norm_n2 = Norm(hin, sq2, KD, TM, [list(range(KD))], ones, D, rs2, [("x1_ready", 1), ("meta_loaded", 16)],
                   lambda k: v_("norm_mix", k), dst=lambda k: n2[:, k, :], done="n2_ready")
    norm_cq = Norm(cq_b, sq2, 3, T, [[0, 1, 2]], ones, 384, rs2, [("taken_act", c_taken)],
                   lambda k: v_("q_norm", k), dst=lambda k: cqn[:, k, :], done="cq_ready")
    norm_ckv = Norm(ckv_b, sq2, 2, TM, [[0, 1]], ones, 256, rs2, [("norm_summed", 5)],
                    lambda k: v_("kv_norm", k), dst=lambda k: ckvn[:, k, :], done="ckv_ready")
    kpe3 = kpe_raw.rearrange("p (a t) -> p a t", a=1)
    norm_kpe = Norm(kpe3, sq2, 1, TM, [[0]], blk64, 64, rs2, [("norm_summed", 6)],
                    lambda k: v_("kn_pe"), dst=lambda k: kpe_n, done="kpe_ready")
    norm_qn = Norm(qnope, sq2, HEADS, T, flat_groups(HEADS), ones, P, rs2, [("taken_act", uq_taken), ("norm_summed", 7)],
                   lambda k: v_("qn_nope"), dst=lambda k: qnope_n[:, k, :], done="qn_ready")
    norm_qpe = Norm(qpe, sq2, 4, T, flat_groups(4), blk64, 64, rs2, [("norm_summed", 15)],
                    lambda k: v_("qn_pe"), dst=lambda k: qpe[:, k, :], done="qpe_ready")
    norm_kn = Norm(knope, sq2, HEADS, TM, flat_groups(HEADS), ones, P, rs2, [("taken_act", uk_taken), ("norm_summed", 19)],
                   lambda k: v_("kn_nope"), dst=lambda k: knope_n[:, k, :], done="kn_ready")
    norm_gla = Norm(o_gla, sq2, KD, T, [[2 * h, 2 * h + 1] for h in range(GLA_HEADS)], ones, 256, rs2,
                    [("o_gla_ready", 4), ("norm_summed", 27)], lambda k: v_("gla_norm", k % 2),
                    dst=lambda k: og_n[:, k, :], done="og_normed")
    norm_ffn = Norm(resid[:, :, :], sq2, KD, T, [list(range(KD))], ones, D, rs2,
                    [("taken_dve", tiles[group_of["w_out"][-1]].seq)],
                    lambda k: v_("norm_ffn", k), dst=lambda k: h_full[:, k, :], done="peer_in")

    rope_count = [0]

    class Rope:

        def __init__(self, items, n, rot, cos, sin, ready, tmp, done):
            self.items = items
            self.n = n
            self.rot = rot
            self.cos = cos
            self.sin = sin
            self.ready = ready
            self.tmp = tmp
            self.done = done
            self.r0 = rope_count[0]
            rope_count[0] += len(items)

        def pe(self, eng):
            for r in self.ready:
                wait(eng, *r)
            for i, (src, _) in enumerate(self.items):
                m = self.r0 + i
                wait(eng, "rope_read", m - 1)
                eng.matmul(ps[:, B_STAT[m % 2], 0:self.n], self.rot, src, start=True, stop=True).then_inc(S("rope_swapped"), 1)

        def dve(self, eng):
            for r in self.ready:
                wait(eng, *r)
            for i, (src, dst) in enumerate(self.items):
                m = self.r0 + i
                eng.tensor_tensor(dst, src, self.cos, ALU.mult)
                wait(eng, "rope_swapped", m + 1)
                ins = eng.tensor_tensor(self.tmp, ps[:, B_STAT[m % 2], 0:self.n], self.sin, ALU.mult)
                ins.then_inc(S("rope_read"), 1)
                wait(eng, "rope_read", m + 1)
                ins = eng.tensor_tensor(dst, dst, self.tmp, ALU.add)
                if i == len(self.items) - 1:
                    ins.then_inc(S(self.done), 1)
                else:
                    chain(ins, eng)

    rope_q1 = Rope([(k_raw[:, 0:T], k_rot[:, 0:T])] + [(q_raw[:, j, :], q_rot[:, j, :]) for j in range(4)], T,
                   con1_("rot"), con1_("cos"), con1_("sin"), [("taken_act", kv1_taken), ("norm_inverted", 1)],
                   rope_tmp[:, 0:T], "rope1_ready")
    rope_q2 = Rope([(qpe[:, j, :], qpe_rot[:, j, :]) for j in range(4)], T, con2_("rot"),
                   con2_("cos")[:, 0:T], con2_("sin")[:, 0:T], [("qpe_ready", 1), ("norm_inverted", 27), ("kn_ready", 1)],
                   rs2[:, 0, 0:T], "rope2_ready")
    rope_k2 = Rope([(kpe_n, kpe_rot)], TM, con2_("rot"), con2_("cos"), con2_("sin"), [("kpe_ready", 1)],
                   rs2[:, 1, :], "rope2_ready")

    att_count = [0, 0]

    class Attention:

        def __init__(self, items, n_keys, key_tiles, scale, probs, pt, fill, ready, outs):
            self.items = items
            self.n_keys = n_keys
            self.key_tiles = key_tiles
            self.scale = scale
            self.probs = probs
            self.pt = pt
            self.fill = fill
            self.ready = ready
            self.outs = outs
            self.i0, self.o0 = att_count
            att_count[0] += len(items)
            att_count[1] += len(outs)

        def pe(self, eng):
            for r in self.ready:
                wait(eng, *r)
            n = len(self.items)

            def scores_of(i):
                it, m = self.items[i], self.i0 + i
                wait(eng, "att_masked", m - 1)
                for x, (lhs, rhs) in enumerate(it["scores"]):
                    mm = eng.matmul(ps[:, B_SCORE[m % 2], 0:self.n_keys], lhs, rhs, start=(x == 0),
                                    stop=(x == len(it["scores"]) - 1))
                mm.then_inc(S("att_scored"), 1)

            scores_of(0)
            scores_of(1)
            for i, it in enumerate(self.items):
                m = self.i0 + i
                pe_tiles(eng, self.fill[i])
                wait(eng, "att_prob", m + 1)
                wait(eng, "att_pt", m)
                for x, (a, w) in enumerate(self.key_tiles):
                    mm = eng.transpose(ps[0:w, B_PT, x * P:x * P + P], self.probs[:, m % 2, a:a + w], ident)
                mm.then_inc(S("att_turned"), 1)
                if i + 2 < n:
                    scores_of(i + 2)
                wait(eng, "att_pt", m + 1)
                if it["wait_out"] > 0:
                    wait(eng, "attn_out_ready", self.o0 + it["wait_out"])
                for x, (a, w) in enumerate(self.key_tiles):
                    mm = eng.matmul(it["out"], it["v"](x), self.pt[0:w, m % 2, x * P:(x + 1) * P], start=(x == 0),
                                    stop=(x == len(self.key_tiles) - 1))
                mm.then_inc(S("att_summed"), 1)

        def dve(self, eng):
            n = len(self.items)
            for r in self.ready:
                wait(eng, *r)

            def mask(i):
                it, m = self.items[i], self.i0 + i
                p = self.probs[:, m % 2, 0:self.n_keys]
                b = (m % 2) * 8
                wait(eng, "att_scored", m + 1)
                wait(eng, "att_turned", m - 1)
                ins = eng.scalar_tensor_tensor(p, ps[:, B_SCORE[m % 2], 0:self.n_keys], self.scale, it["mask"],
                                               ALU.mult, ALU.add)
                ins.then_inc(S("att_masked"), 1)
                wait(eng, "att_masked", m + 1)
                chain(eng.tensor_reduce(small[:, b:b + 1], p, AX_X, ALU.max), eng)
                if it["sink"] is None:
                    ins = eng.tensor_scalar(small[:, b + 1:b + 2], small[:, b:b + 1], -1.0, None, ALU.mult)
                else:
                    ins = eng.tensor_scalar(small[:, b + 1:b + 2], small[:, b:b + 1], v_("sink", it["sink"]), -1.0,
                                            ALU.max, ALU.mult)
                ins.then_inc(S("att_max"), 1)

            def normalise(i):
                it, m = self.items[i], self.i0 + i
                b = (m % 2) * 8
                p = self.probs[:, m % 2, 0:self.n_keys]
                wait(eng, "att_exp", m + 1)
                if it["sink"] is not None:
                    chain(eng.tensor_tensor(small[:, b + 2:b + 3], small[:, b + 2:b + 3], small[:, b + 3:b + 4], ALU.add), eng)
                chain(eng.reciprocal(small[:, b + 4:b + 5], small[:, b + 2:b + 3]), eng)
                eng.tensor_scalar(p, p, small[:, b + 4:b + 5], None, ALU.mult).then_inc(S("att_prob"), 1)

            mask(0)
            for i in range(n):
                take_tiles("dve", eng, self.fill[i])
                normalise(i)
                if i + 1 < n:
                    mask(i + 1)

        def act(self, eng):
            for i, it in enumerate(self.items):
                m = self.i0 + i
                b = (m % 2) * 8
                p = self.probs[:, m % 2, 0:self.n_keys]
                wait(eng, "att_max", m + 1)
                if it["sink"] is not None:
                    eng.activation(small[:, b + 3:b + 4], v_("sink", it["sink"]), ACT.Exp, bias=small[:, b + 1:b + 2])
                eng.activation(p, p, ACT.Exp, bias=small[:, b + 1:b + 2],
                               accum_out=small[:, b + 2:b + 3]).then_inc(S("att_exp"), 1)
                take_tiles("act", eng, self.fill[i])
                wait(eng, "att_turned", m + 1)
                wait(eng, "att_summed", m - 1)
                w = len(self.key_tiles) * P
                full = [x for x, (_, k) in enumerate(self.key_tiles) if k == P]
                ins = eng.copy(self.pt[:, m % 2, 0:len(full) * P], ps[:, B_PT, 0:len(full) * P])
                if len(full) < len(self.key_tiles):
                    k = self.key_tiles[-1][1]
                    ins = eng.copy(self.pt[0:k, m % 2, len(full) * P:w], ps[0:k, B_PT, len(full) * P:w])
                ins.then_inc(S("att_pt"), 1)
                if it["copy"] is not None:
                    wait(eng, "att_summed", m + 1)
                    src, dst = self.outs[it["copy"]]
                    eng.copy(dst, src).then_inc(S("attn_out_ready"), 1)

    def region(x):
        return ps[:, B_OUT, (x % 2) * T:(x % 2 + 1) * T]

    items1, outs1 = [], []
    for j in range(4):
        outs1.append((region(j), attn1[:, j, :]))
        for g in range(2):
            for t in range(NT):
                rows = slice(g * HEAD, (g + 1) * HEAD)
                last = g == 1 and t == NT - 1
                items1.append(dict(
                    scores=[(q_rot[rows, j, t * P:(t + 1) * P], k_rot[rows, :])],
                    mask=con1_("mask")[:, t * 512:(t + 1) * 512], sink=g * GROUP + j,
                    v=lambda x, g=g: v_tok[:, x, g * HEAD:(g + 1) * HEAD],
                    out=ps[rows, B_OUT, (j % 2) * T + t * P:(j % 2) * T + (t + 1) * P],
                    copy=j if last else None, wait_out=j - 1))
    att1 = Attention(items1, T + CTX, [(i * P, P) for i in range(4)], HEAD ** -0.5, probs1, pt1,
                     pieces("fill1", len(items1)), [("rope1_ready", 1)], outs1)
    items2, outs2 = [], []
    for h in range(HEADS):
        outs2.append((region(h), attn2[:, h, :]))
        rows = slice((h % 2) * 64, (h % 2) * 64 + 64)
        for t in range(NT):
            q = slice(t * P, (t + 1) * P)
            items2.append(dict(
                scores=[(qnope_n[:, h, q], knope_n[:, h, :]), (qpe_rot[rows, h // 2, q], kpe_rot[rows, :])],
                mask=con2_("mask")[:, t * TM:(t + 1) * TM], sink=None,
                v=lambda x, h=h: v2[0:KT2[x][1], x, h * P:(h + 1) * P],
                out=ps[:, B_OUT, (h % 2) * T + t * P:(h % 2) * T + (t + 1) * P],
                copy=h if t == NT - 1 else None, wait_out=h - 1))
    att2 = Attention(items2, TM, KT2, 192 ** -0.5, probs2, pt2,
                     pieces(["gq", "gk", "ga", "gv", "gate_a", "gg", "gate_b"], len(items2)),
                     [("kn_ready", 1), ("rope2_ready", 2), ("taken_act", v2_taken)], outs2)

    def gla_bank(m):
        return B_SCORE[m % 2]

    def pe_gla_decay(pe):
        wait(pe, "taken_act", ga_taken)
        wait(pe, "wa2_loaded", 16)
        wait(pe, "att_summed", 32)
        wait(pe, "attn_out_ready", 4 + HEADS)
        for h in range(GLA_HEADS):
            bank = [3, 4, 5, 6][h]
            pe.matmul(ps[:, bank, 0:TM], wa2_b[0:16, h * P:(h + 1) * P], ga_b[0:16, :], start=True,
                      stop=True).then_inc(S("gla_logit"), 1)

    def dve_gla_decay(dve):
        wait(dve, "taken_act", gates2_taken)
        for h in range(GLA_HEADS):
            wait(dve, "gla_logit", h + 1)
            ins = dve.tensor_scalar(la[:, h, :], ps[:, [3, 4, 5, 6][h], 0:TM], v_("b_a", h), None, ALU.add)
        chain(ins, dve)
        dve.scalar_tensor_tensor(lb, la, -1.0, la, ALU.mult, ALU.max).then_inc(S("gla_abs"), 1)
        wait(dve, "gla_log", 1)
        chain(dve.tensor_scalar(la, la, 0.0, None, ALU.min), dve)
        chain(dve.tensor_tensor(la, la, lb, ALU.subtract), dve)
        chain(dve.tensor_scalar(la, la, 1.0 / TAU, None, ALU.mult), dve)
        for h in range(GLA_HEADS):
            for a, w in KT2:
                ins = dve.tensor_tensor_scan(lb[:, h, a:a + w], ones[:, 0:w], la[:, h, a:a + w], 0.0, ALU.mult, ALU.add)
        chain(ins, dve)
        for n, (a, w) in enumerate([KT2[2], KT2[0]]):
            dve.tensor_tensor(kdec[n], lb[:, :, a + w - 1:a + w].broadcast_to([P, GLA_HEADS, w]), lb[:, :, a:a + w], ALU.subtract)
        dve.tensor_copy(blast[:, 1, :], lb[:, :, P - 1]).then_inc(S("gla_ends"), 1)
        wait(dve, "gla_ends_exp", 1)
        for n, (a, w) in enumerate([KT2[2], KT2[0]]):
            dve.tensor_tensor(kdec[n], kdec[n], gk[:, :, a:a + w], ALU.mult)
        dve.tensor_tensor(qdec, qdec, gq, ALU.mult).then_inc(S("gla_dec"), 1)

    def act_gla_decay(act):
        wait(act, "gla_abs", 1)
        act.activation(lb, lb, ACT.Exp, scale=-1.0).then_inc(S("gla_e"), 1)
        wait(act, "gla_e", 1)
        act.activation(lb, lb, ACT.Ln, bias=1.0).then_inc(S("gla_log"), 1)
        wait(act, "gla_ends", 1)
        act.activation(qdec, lb[:, :, 0:T], ACT.Exp)
        act.activation(kdec[0], kdec[0], ACT.Exp)
        act.activation(kdec[1], kdec[1], ACT.Exp)
        act.activation(blast[:, 1, :], blast[:, 1, :], ACT.Exp).then_inc(S("gla_ends_exp"), 1)

    gla_steps = [(t, n) for t in range(NT) for n in range(LEVELS + 1)]

    def dve_gla_levels(dve):
        def prepare(m):
            t, n = gla_steps[m]
            if n == LEVELS:
                return
            size = 1 << n
            a = t * P
            gd = gd2[(t * LEVELS + n) % 2]
            for h in range(GLA_HEADS):
                bh = lb[:, h, a:a + P].rearrange("p (m s) -> p m s", s=2 * size)
                dh = gd[:, h, :].rearrange("p (m s) -> p m s", s=2 * size)
                r = bh[:, :, size - 1:size].broadcast_to([P, P // (2 * size), 2 * size])
                ins = dve.tensor_tensor(dh, bh, r, ALU.subtract)
            chain(ins, dve)
            dve.scalar_tensor_tensor(gd, gd, -1.0, gd, ALU.mult, ALU.max).then_inc(S("gla_dist"), 1)

        dist = 0
        for m, (t, n) in enumerate(gla_steps):
            a = t * P
            gd = gd2[(t * LEVELS + n) % 2]
            prepare(m)
            if n < LEVELS:
                dist += 1
                wait(dve, "gla_fade", dist)
            wait(dve, "gla_pair", m - 1)
            if n < LEVELS:
                dve.tensor_tensor(gqd[m % 2], gd, gq[:, :, a:a + P], ALU.mult)
                ins = dve.tensor_tensor(gkd[m % 2], gd, gk[:, :, a:a + P], ALU.mult)
            else:
                dve.tensor_copy(gqd[m % 2], gq[:, :, a:a + P])
                ins = dve.tensor_copy(gkd[m % 2], gk[:, :, a:a + P])
            ins.then_inc(S("gla_faded"), 1)
            if m:
                collect(dve, m - 1)
        collect(dve, len(gla_steps) - 1)

    def collect(dve, m):
        t, n = gla_steps[m]
        wait(dve, "gla_pair", m + 1)
        mask = con2_("gla_mask")[:, n * P:(n + 1) * P].rearrange("p (a i) -> p a i", a=1).broadcast_to([P, GLA_HEADS, P])
        src = ps[:, gla_bank(m), :].rearrange("p (h i) -> p h i", h=GLA_HEADS)
        if n == 0:
            dve.tensor_tensor(amat[t], src, mask, ALU.mult).then_inc(S("gla_kept"), 1)
            return
        ins = dve.tensor_tensor(atmp, src, mask, ALU.mult)
        chain(ins, dve)
        dve.tensor_tensor(amat[t], amat[t], atmp, ALU.add).then_inc(S("gla_kept"), 1)
        wait(dve, "gla_kept", m + 1)

    def act_gla_levels(act):
        for n in range(NT * LEVELS):
            wait(act, "gla_dist", n + 1)
            gd = gd2[n % 2]
            act.activation(gd, gd, ACT.Exp, scale=-1.0).then_inc(S("gla_fade"), 1)

    def pe_gla_levels(pe):
        wait(pe, "gla_abs", 1)
        for m in range(len(gla_steps)):
            wait(pe, "gla_faded", m + 1)
            wait(pe, "gla_kept", m - 1)
            for h in range(GLA_HEADS):
                mm = pe.matmul(ps[:, gla_bank(m), h * P:(h + 1) * P], gkd[m % 2][:, h, :], gqd[m % 2][:, h, :],
                               start=True, stop=True)
            mm.then_inc(S("gla_pair"), 1)

    def pe_gla_out(pe):
        wait(pe, "gla_dec", 1)
        for h in range(GLA_HEADS):
            pe.transpose(ps[0:META, 3, h * P:(h + 1) * P], kdec[0][:, h, :], ident)
        for h in range(GLA_HEADS):
            mm = pe.transpose(ps[:, 6, h * P:(h + 1) * P], kdec[1][:, h, :], ident)
        mm.then_inc(S("gla_turned"), 1)
        wait(pe, "gla_turned_copied", 1)
        wait(pe, "taken_act", gv_taken)
        wait(pe, "norm_inverted", 27)
        for n in range(2):
            rows = META if n == 0 else P
            src = 2 if n == 0 else 0
            for h in range(GLA_HEADS):
                bank = 3 if h < 2 else 7
                mm = pe.matmul(ps[:, bank, (h % 2) * 256:(h % 2 + 1) * 256], kdecT[n][0:rows, h, :],
                               gv[0:rows, src, h * 256:(h + 1) * 256], start=True, stop=True)
            mm.then_inc(S("gla_state"), 1)
            wait(pe, "gla_state_kept", n + 1)
        wait(pe, "gla_kept", len(gla_steps))
        for t in range(NT):
            for h in range(GLA_HEADS):
                for e in range(2):
                    x = h * 2 + e
                    bank = [[4, 5], [6, 3]][t][x // 4]
                    dst = ps[:, bank, (x % 4) * P:(x % 4 + 1) * P]
                    pe.matmul(dst, gv[:, t, h * 256 + e * P:h * 256 + (e + 1) * P], amat[t][:, h, :], start=True, stop=False)
                    mm = pe.matmul(dst, state[t][:, h, e * P:(e + 1) * P], qdec[:, h, t * P:(t + 1) * P], start=False, stop=True)
                    if x % 4 == 3:
                        mm.then_inc(S("gla_o"), 1)

    def dve_gla_state(dve):
        for n in range(2):
            wait(dve, "gla_state", n + 1)
            for h in range(GLA_HEADS):
                bank = 3 if h < 2 else 7
                src = ps[:, bank, (h % 2) * 256:(h % 2 + 1) * 256]
                if n == 0:
                    ins = dve.tensor_copy(state[0][:, h, :], src)
                else:
                    ins = dve.scalar_tensor_tensor(state[1][:, h, :], state[0][:, h, :], blast[:, 1, h:h + 1], src,
                                                   ALU.mult, ALU.add)
            ins.then_inc(S("gla_state_kept"), 1)
            wait(dve, "gla_state_kept", n + 1)

    def act_gla_out(act):
        wait(act, "gla_turned", 1)
        act.copy(kdecT[0][0:META, :, :], ps[0:META, 3, :].rearrange("p (h d) -> p h d", h=GLA_HEADS))
        act.copy(kdecT[1], ps[:, 6, :].rearrange("p (h d) -> p h d", h=GLA_HEADS)).then_inc(S("gla_turned_copied"), 1)
        for m in range(4):
            t, half = m // 2, m % 2
            bank = [[4, 5], [6, 3]][t][half]
            wait(act, "gla_o", m + 1)
            act.copy(o_gla[:, half * 4:half * 4 + 4, t * P:(t + 1) * P],
                     ps[:, bank, :].rearrange("p (x i) -> p x i", x=4)).then_inc(S("o_gla_ready"), 1)

    def passes(pe, out_ap, w, m, start, stop):
        pe.matmul(out_ap, w[0], m[0], start=start, stop=False)
        pe.matmul(out_ap, w[1], m[0], start=False, stop=False)
        return pe.matmul(out_ap, w[0], m[1], start=False, stop=stop)

    UB = 4
    N_IT = P // UB
    SEG = (16, 4, 12)
    assert sum(SEG) == N_IT

    def split_count(b, table):
        return ((b - 1) * 2 + table) * P

    def peer_pe_scores(pe, b):
        wait(pe, "taken_act", wq_taken[b]["act"])
        wait(pe, "taken_dve", wq_taken[b]["dve"])
        wait(pe, f"keys_loaded{b}", 16)
        for t in range(NT):
            for j in range(16):
                bank = (4 if t == 0 else 0) + j // 4
                mm = pe.matmul(ps[:, bank, (j % 4) * P:(j % 4 + 1) * P],
                               q_area[:, j * T + t * P:j * T + (t + 1) * P], keys_area[:, j, :], start=True, stop=True)
                if j % 4 == 3:
                    mm.then_inc(S("peer_scored"), 1)

    def peer_act_scores(act, b):
        for m in range(8):
            t, n = m // 4, m % 4
            wait(act, "peer_scored", (b - 1) * 8 + m + 1)
            act.copy(s_area[:, t * 2048 + n * 512:t * 2048 + (n + 1) * 512],
                     ps[:, (4 if t == 0 else 0) + n, :]).then_inc(S("peer_s_copied"), 1)

    def u_loop(kind, eng, b, it0, n_it, extra=None):
        u_first = units[f"u{b}"][0]
        s0 = split_count(b, 0)
        done0 = (b - 1) * P
        with eng.Fori(it0, it0 + n_it) as i:
            for s in range(UB):
                unit = u_first + s
                raw = slot(unit)
                hslot = (s0 + s) % HLRING
                if kind == "pe":
                    eng.wait_ge(S("split_hi"), i * UB + (s0 + s + 1))
                    eng.wait_ge(S("split_lo"), i * UB + (s0 + s + 1))
                    eng.wait_ge(S("u_bank_free"), i * UB + (done0 + 4 * b - 4 + s + 1))
                    for k in range(KD):
                        w = [hl[:, hslot, x, k * P:(k + 1) * P] for x in range(2)]
                        m = [hsplit[:, x, k, :] for x in range(2)]
                        mm = passes(eng, ps[:, s, 0:T], w, m, k == 0, k == KD - 1)
                    mm.then_inc(S("split_used"), 1)
                if kind == "act":
                    eng.wait_ge(S(ring_full[unit % RING]), i * 16 + 16 * (unit // RING + 1))
                    eng.wait_ge(S("split_used"), i * UB + (s0 + s + 2 * b - HLRING + 1))
                    eng.copy(hl[:, hslot, 0, :], raw).then_inc(S("split_hi"), 1)
                    if s >= 2:
                        gelu(eng, b, i, s - 2)
                if kind == "dve":
                    eng.wait_ge(S("split_hi"), i * UB + (s0 + s + 1))
                    eng.tensor_tensor(hl[:, hslot, 1, :], raw, hl[:, hslot, 0, :].bitcast(F32), ALU.subtract)\
                       .then_inc(S("split_lo"), 1)
                    if extra:
                        extra(eng, i, s)
            if kind == "act":
                gelu(eng, b, i, 2)
                gelu(eng, b, i, 3)

    def gelu(eng, b, i, s):
        eng.wait_ge(S("split_used"), i * UB + (split_count(b, 0) + 2 * b + s + 1))
        eng.activation(acts[:, bass.ds(i * (UB * T) + s * T, T)], ps[:, s, 0:T], ACT.Gelu).then_inc(S("u_bank_free"), 1)

    def topk_step(dve, b):
        def f(eng, i, s):
            if s == 0:
                chain_in(eng, eng.tensor_copy(keybuf[:, :], s_area[:, bass.ds(i * 256, 256)]))
                for x in range(2):
                    half = keybuf[:, x * P:(x + 1) * P]
                    ins = eng.max(topbuf[:, x, 0:8], half)
                chain_in(eng, ins)
                for x in range(2):
                    eng.max_index(idxbuf[:, x, 0:8], topbuf[:, x, 0:8], keybuf[:, x * P:(x + 1) * P])
                    ins = eng.match_replace(tmpbuf[:, x * P:(x + 1) * P], topbuf[:, x, 0:8], keybuf[:, x * P:(x + 1) * P], NEG)
                chain_in(eng, ins)
            if s == 1:
                for x in range(2):
                    ins = eng.max(topbuf[:, x, 8:16], tmpbuf[:, x * P:(x + 1) * P])
                chain_in(eng, ins)
                for x in range(2):
                    ins = eng.max_index(idxbuf[:, x, 8:16], topbuf[:, x, 8:16], tmpbuf[:, x * P:(x + 1) * P])
                chain_in(eng, ins)
                for x in range(2):
                    eng.tensor_copy(index_f[:, bass.ds(i * 16 + x * 256, 16)], idxbuf[:, x, :])
                ins = eng.tensor_tensor(keybuf[:, :].rearrange("p (a b) -> p a b", a=TOPK),
                                        topbuf[:, 0, :].rearrange("p (a o) -> p a o", o=1).broadcast_to([P, TOPK, TOPK]),
                                        topbuf[:, 1, :].rearrange("p (o b) -> p o b", o=1).broadcast_to([P, TOPK, TOPK]),
                                        ALU.add)
                chain_in(eng, ins)
            if s == 2:
                chain_in(eng, eng.max(bestbuf[:, 0:8], keybuf[:, :]))
                chain_in(eng, eng.match_replace(tmpbuf[:, :], bestbuf[:, 0:8], keybuf[:, :], NEG))
                chain_in(eng, eng.max(bestbuf[:, 8:16], tmpbuf[:, :]))
            if s == 3:
                chain_in(eng, eng.match_replace(tmpbuf[:, :], bestbuf[:, 8:16], tmpbuf[:, :], NEG))
                eng.tensor_scalar(keybuf[:, :], keybuf[:, :], bestbuf[:, 0:1], None, ALU.subtract)
                chain_in(eng, eng.tensor_scalar(tmpbuf[:, :], tmpbuf[:, :], NEG, NEG, ALU.not_equal, ALU.mult))
                chain_in(eng, eng.tensor_tensor(s_area[:, bass.ds(i * 256, 256)], keybuf[:, :], tmpbuf[:, :], ALU.add))
        def chain_in(eng, ins):
            eng.drain()
        return f

    index_f = gate_f[:, :, :, :].rearrange("p x t r -> p (x t r)")

    def dve_gates(dve, b):
        wait(dve, "gates_exp", b)
        g3 = s_area[:, :].rearrange("p (h x) -> p h x", x=2 * P)
        chain(dve.tensor_reduce(zsum[:, 0, :], g3, AX_X, ALU.add), dve)
        chain(dve.reciprocal(zsum[:, 1, :], zsum[:, 0, :]), dve)
        for t in range(NT):
            for h in range(HEADS):
                m = t * HEADS + h
                src = g3[:, m, :].rearrange("p (a b) -> p a b", a=TOPK)
                dst = turned_tmp.rearrange("p (a h b) -> p a h b", a=TOPK, h=HEADS)[:, :, h, :]
                ins = dve.tensor_scalar(dst, src, zsum[:, 1, m:m + 1], None, ALU.mult)
            chain(ins, dve)
            ins = dve.tensor_copy(s_area[:, t * 2048:(t + 1) * 2048], turned_tmp)
            if t == 0:
                chain(ins, dve)
        ins.then_inc(S("gates_ready"), 1)

    def pe_gate_turns(pe, b):
        wait(pe, "gates_ready", b)
        for x in range(2):
            for t in range(NT):
                mm = pe.transpose(ps[:, 4, (x * NT + t) * P:(x * NT + t + 1) * P], gate_f[:, x, t, :], ident)
        mm.then_inc(S("gates_turned"), 1)
        for t in range(NT):
            for a in range(TOPK):
                m = (t * TOPK + a) // 4
                if a % 4 == 0:
                    wait(pe, "turns_copied", (b - 1) * 9 + 1 + m - 2 if m >= 3 else 0)
                bank = 5 + m % 3
                src = s_area[:, t * 2048 + a * P:t * 2048 + (a + 1) * P]
                mm = pe.transpose(ps[:, bank, (a % 4) * P:(a % 4 + 1) * P], src, ident)
                if a % 4 == 3:
                    mm.then_inc(S("gates_turned"), 1)

    def dve_gate_turns(dve, b):
        wait(dve, "gates_turned", (b - 1) * 9 + 1)
        dve.tensor_copy(index_f, ps[:, 4, :]).then_inc(S("turns_copied"), 1)
        for t in range(NT):
            for n in range(4):
                m = t * 4 + n
                wait(dve, "gates_turned", (b - 1) * 9 + 2 + m)
                bank = 5 + m % 3
                dst = turned_tmp[:, :].rearrange("p (t a) -> p a t", a=TOPK)[:, n * 4:(n + 1) * 4, :]
                dve.tensor_copy(dst, ps[:, bank, :].rearrange("p (a t) -> p a t", a=4)).then_inc(S("turns_copied"), 1)
            wait(dve, "turns_copied", (b - 1) * 9 + 1 + 4 * (t + 1))
            chain(dve.tensor_copy(s_area[:, t * 2048:(t + 1) * 2048], turned_tmp[:, :]), dve)

    NG = T // 8

    def act_group(act, b, g, buf):
        gate_t = s_area
        act.wait_ge(S("w_ready"), g * 2 + (base(b, 4) + 2))
        for h in range(HEADS):
            src = gate_t[:, ds(g * 128, 128)].rearrange("p (t a) -> p t a", t=8)
            ins = act.activation(gbd[:, buf, :, h * TOPK:(h + 1) * TOPK], src, ACT.Copy, scale=delta[:, h:h + 1])
        ins.then_inc(S("bd_ready"), 1)

    def act_rows(act, b, g, buf):
        for half in range(2):
            act.wait_ge(S("w_ready"), g * 2 + (base(b, 4) + 4 + half + 1))
            act.wait_ge(S("e_ready"), g * 2 + (base(b, 8) + 6))
            act.copy(wrow[:, buf * 2 + half, :, :],
                     ps[:, buf * 2 + half, :].rearrange("p (t i) -> p t i", t=4)).then_inc(S("w_copied"), 1)

    def base(b, free):
        return (b - 1) * (2 * NG + free)

    def ds(a, n):
        return bass.ds(a, n) if not isinstance(a, int) else slice(a, a + n)

    def dve_onehots(dve, b, g, buf, buf1):
        def hot(dst, x):
            col = index_f[:, ds(g * 8 + x * T, 8)].rearrange("p (t o) -> p t o", o=1).broadcast_to([P, 8, P])
            row = iota.rearrange("p (o i) -> p o i", o=1).broadcast_to([P, 8, P])
            return dve.tensor_tensor(dst, col, row, ALU.is_equal)
        dve.wait_ge(S("w_ready"), g * 2 + (base(b, 4) + 2))
        hot(oh2[:, buf, :, :], 1).then_inc(S("oh2_ready"), 1)
        dve.wait_ge(S("e_ready"), g * 2 + (base(b, 8) + 2))
        hot(oh1[:, buf1, :, :], 0).then_inc(S("oh1_ready"), 1)

    def dve_multiply(dve, b, g, buf):
        for half in range(2):
            dve.wait_ge(S("e_ready"), g * 2 + (base(b, 8) + 8 + half + 1))
            a4 = acts[:, :].rearrange("p (i t) -> p i t", t=T)[:, :, ds(g * 8 + half * 4, 4)]
            src = ps[:, 4 + buf * 2 + half, :].rearrange("p (t i) -> p i t", t=4)
            dve.tensor_tensor(a4, a4, src, ALU.mult).then_inc(S("e_used"), 1)

    def pe_w(pe, b, g, buf):
        pe.wait_ge(S("oh2_ready"), g + ((b - 1) * NG + 1))
        pe.wait_ge(S("bd_ready"), g + ((b - 1) * NG + 1))
        for half in range(2):
            pe.wait_ge(S("w_copied"), g * 2 + (base(b, 4) + half + 1))
            for t in range(4):
                mm = pe.matmul(ps[:, buf * 2 + half, t * P:(t + 1) * P], gbd[:, buf, half * 4 + t, :],
                               oh2[:, buf, half * 4 + t, :], start=True, stop=True)
            mm.then_inc(S("w_ready"), 1)

    def pe_e(pe, b, g, buf, buf1):
        pe.wait_ge(S("oh1_ready"), g + ((b - 1) * NG + 1))
        for half in range(2):
            pe.wait_ge(S("w_copied"), g * 2 + (base(b, 4) + 4 + half + 1))
            pe.wait_ge(S("e_used"), g * 2 + (base(b, 4) + half + 1))
            for t in range(4):
                mm = pe.matmul(ps[:, 4 + buf * 2 + half, t * P:(t + 1) * P], oh1[:, buf1, half * 4 + t, :],
                               wrow[:, buf * 2 + half, t, :], start=True, stop=True)
            mm.then_inc(S("e_ready"), 1)

    def v_loop(kind, eng, b):
        v_first = units[f"v{b}"][0]
        s0 = split_count(b, 1)

        def body(i, first, last):
            for s in range(UB):
                unit = v_first + s
                hslot, cslot = (s0 + s) % HLRING, s % 2
                c = ds(i * (UB * T) + s * T, T)
                if kind == "act":
                    eng.wait_ge(S(ring_full[unit % RING]), i * 16 + 16 * (unit // RING + 1))
                    eng.wait_ge(S("split_used"), i * UB + (s0 + s + 2 * b - HLRING + 1))
                    eng.copy(csplit[:, cslot, 0, :], acts[:, c]).then_inc(S("csplit_hi"), 1)
                    eng.copy(hl[:, hslot, 0, :], slot(unit)).then_inc(S("split_hi"), 1)
                if kind == "dve":
                    eng.wait_ge(S("csplit_hi"), i * UB + ((b - 1) * P + s + 1))
                    eng.tensor_tensor(csplit[:, cslot, 1, :], acts[:, c], csplit[:, cslot, 0, :].bitcast(F32), ALU.subtract)
                    eng.wait_ge(S("split_hi"), i * UB + (s0 + s + 1))
                    eng.tensor_tensor(hl[:, hslot, 1, :], slot(unit), hl[:, hslot, 0, :].bitcast(F32), ALU.subtract)\
                       .then_inc(S("split_lo"), 1)
                if kind == "pe":
                    eng.wait_ge(S("split_hi"), i * UB + (s0 + s + 1))
                    eng.wait_ge(S("split_lo"), i * UB + (s0 + s + 1))
                    for d in range(KD):
                        w = [hl[:, hslot, x, d * P:(d + 1) * P] for x in range(2)]
                        m = [csplit[:, cslot, x, :] for x in range(2)]
                        mm = passes(eng, ps[:, d, 0:T], w, m, first and s == 0, last and s == UB - 1)
                    mm.then_inc(S("split_used"), 1)

        body(0, True, False)
        with eng.Fori(1, N_IT - 1) as i:
            body(i, False, False)
        body(N_IT - 1, False, True)

    def peer_pe(pe, b):
        pe_tiles(pe, group_of[f"wq{b}"])
        peer_pe_scores(pe, b)
        pe.wait_ge(S("peer_s_copied"), 8 * b)
        pe.drain().then_inc(S("split_used"), 2)
        pe.wait_ge(S("hsplit_ready"), b)
        u_loop("pe", pe, b, 0, SEG[0])
        u_loop("pe", pe, b, SEG[0], SEG[1])
        pe_gate_turns(pe, b)
        u_loop("pe", pe, b, SEG[0] + SEG[1], SEG[2])
        pe.wait_ge(S("u_bank_free"), b * (P + 4))
        pe.wait_ge(S("turns_copied"), 9 * b)
        pe.wait_ge(S("split_used"), split_count(b, 0) + P + 2 * b)
        for name, free in (("w_ready", 4), ("e_ready", 8), ("w_copied", 4), ("e_used", 4)):
            pe.drain().then_inc(S(name), free)
        pe_w(pe, b, 0, 0)

        def step(g, n):
            pe_w(pe, b, g + 1, (n + 1) % 2)
            pe_e(pe, b, g, n % 2, n % OHRING)
        with pe.Fori(0, NG // OHRING - 1) as i:
            for n in range(OHRING):
                step(i * OHRING + n, n)
        for n in range(OHRING - 1):
            step(NG - OHRING + n, n)
        pe_e(pe, b, NG - 1, 1, OHRING - 1)
        pe.wait_ge(S("e_used"), b * (2 * NG + 4))
        v_loop("pe", pe, b)

    def peer_act(act, b):
        take_tiles("act", act, group_of[f"wq{b}"])
        peer_act_scores(act, b)
        act.wait_ge(S("peer_scored"), 8 * b)
        act.copy(hsplit[:, 0, :, :], h_full).then_inc(S("hsplit_hi"), 1)
        act.wait_ge(S("peer_s_copied"), 8 * b)
        act.drain().then_inc(S("u_bank_free"), 4)
        u_loop("act", act, b, 0, SEG[0])
        wait(act, "topk_done", b)
        act.activation(s_area[:, :], s_area[:, :], ACT.Exp).then_inc(S("gates_exp"), 1)
        u_loop("act", act, b, SEG[0], SEG[1] + SEG[2])
        act.wait_ge(S("turns_copied"), 9 * b)
        act_group(act, b, 0, 0)

        def step(g, n):
            act_group(act, b, g + 1, (n + 1) % 2)
            act_rows(act, b, g, n % 2)
        with act.Fori(0, NG // OHRING - 1) as i:
            for n in range(OHRING):
                step(i * OHRING + n, n)
        for n in range(OHRING - 1):
            step(NG - OHRING + n, n)
        act_rows(act, b, NG - 1, 1)
        act.wait_ge(S("e_used"), b * (2 * NG + 4))
        v_loop("act", act, b)

    def peer_dve(dve, b):
        take_tiles("dve", dve, group_of[f"wq{b}"])
        dve.wait_ge(S("hsplit_hi"), b)
        dve.tensor_tensor(hsplit[:, 1, :, :], h_full, hsplit[:, 0, :, :].bitcast(F32), ALU.subtract)\
           .then_inc(S("hsplit_ready"), 1)
        dve.wait_ge(S("peer_s_copied"), 8 * b)
        u_loop("dve", dve, b, 0, SEG[0], topk_step(dve, b))
        dve.drain().then_inc(S("topk_done"), 1)
        dve_gates(dve, b)
        u_loop("dve", dve, b, SEG[0], SEG[1])
        dve_gate_turns(dve, b)
        u_loop("dve", dve, b, SEG[0] + SEG[1], SEG[2])
        dve_onehots(dve, b, 0, 0, 0)

        def step(g, n):
            dve_onehots(dve, b, g + 1, (n + 1) % 2, (n + 1) % OHRING)
            dve_multiply(dve, b, g, n % 2)
        with dve.Fori(0, NG // OHRING - 1) as i:
            for n in range(OHRING):
                step(i * OHRING + n, n)
        for n in range(OHRING - 1):
            step(NG - OHRING + n, n)
        dve_multiply(dve, b, NG - 1, 1)
        dve.wait_ge(S("e_used"), b * (2 * NG + 4))
        v_loop("dve", dve, b)
        dve.wait_ge(S("split_used"), 2 * b * P + 2 * b)
        for k in range(KD):
            if b == 1:
                ins = dve.scalar_tensor_tensor(resid[:, k, :], ps[:, k, 0:T], mod[:, 40 + k, 0:1], resid[:, k, :],
                                               ALU.mult, ALU.add)
            else:
                ins = dve.tensor_tensor(resid[:, k, :], ps[:, k, 0:T], resid[:, k, :], ALU.add)
        ins.then_inc(S("peer_out"), 1)

    with nc.Block() as block:
        @block.sync
        def _(sp):
            peer_units = {u: n for n, u in enumerate(units["u1"] + units["v1"] + units["u2"] + units["v2"])}

            def load(u):
                sp.dma_start(slot(u), stream[u, :, :]).then_inc(S(arrival(u)[0]), 16)

            u = 0
            while u < n_units:
                old = u - RING
                if u in peer_units and old in peer_units:
                    end = u
                    while end < n_units and end in peer_units:
                        end += 1
                    rounds = (end - u) // RING
                    n0 = peer_units[old]
                    with sp.Fori(0, rounds) as i:
                        for s in range(RING):
                            sp.wait_ge(S("split_lo"), i * RING + (n0 + s + 1))
                            sp.dma_start(slot(u + s), stream[bass.ds(i * RING + (u + s), 1), :, :]
                                         .rearrange("a p n -> (a p) n")).then_inc(S(ring_full[(u + s) % RING]), 16)
                    u += rounds * RING
                    while u < end:
                        wait(sp, "split_lo", peer_units[u - RING] + 1)
                        load(u)
                        u += 1
                    continue
                if old in peer_units:
                    wait(sp, "split_lo", peer_units[old] + 1)
                elif old >= 0:
                    wait(sp, "tile_done", last_tile[old] + 1)
                load(u)
                u += 1
            sp.wait_ge(S("peer_out"), 2)
            sp.dma_start(out, resid[:, :, :]).then_inc(S("out_stored"), 16)
            sp.wait_ge(S("out_stored"), 16)

        @block.gpsimd
        def _(pool):
            pool.memset(ones, 1.0).then_inc(S("ones_ready"), 1)

        @block.scalar
        def _(act):
            act.dma_start(vec[:, :], vectors).then_inc(S("vec_loaded"), 16)
            act.dma_start(xin[:, :, 0:T], xT).then_inc(S("x_loaded"), 16)
            act.dma_start(xin[:, :, T:], ctxT).then_inc(S("x_loaded"), 16)
            act.dma_start(resid[:, :, :], xT).then_inc(S("consts_loaded"), 16)
            act.dma_start(con[:, :], common).then_inc(S("consts_loaded"), 16)
            act.dma_start(con1, consts1).then_inc(S("consts_loaded"), 16)
            wait(act, "vec_loaded", 16)
            cond = vec[:, vec_at["cond"][0]:vec_at["cond"][0] + 16].rearrange("p (k c) -> p k c", k=KD)
            act.activation(silu_c, cond, ACT.Silu).then_inc(S("silu_ready"), 1)
            norm_x.act(act)
            wait(act, "consts_loaded", 48)
            take_tiles("act", act, group_of["kvq1"])
            att1.act(act)
            take_tiles("act", act, group_of["out1"])
            norm_h2.act(act)
            act.dma_start(keys_area, keys1).then_inc(S("keys_loaded1"), 16)
            peer_act(act, 1)
            wait(act, "peer_out", 1)
            act.dma_start(con2, consts2).then_inc(S("consts2_loaded"), 16)
            act.dma_start(hin[:, :, T:TM], metaT).then_inc(S("meta_loaded"), 16)
            act.dma_start(wa2_b[0:16, :], w_a2).then_inc(S("wa2_loaded"), 16)
            norm_final.act(act)
            norm_n2.act(act)
            for g in ("cq", "ckv", "kpe"):
                take_tiles("act", act, group_of[g])
            norm_cq.act(act)
            norm_ckv.act(act)
            norm_kpe.act(act)
            take_tiles("act", act, group_of["uq"])
            norm_qn.act(act)
            norm_qpe.act(act)
            take_tiles("act", act, group_of["ukv_k"])
            norm_kn.act(act)
            take_tiles("act", act, group_of["ukv_v"])
            wait(act, "consts2_loaded", 16)
            att2.act(act)
            act_gla_decay(act)
            act_gla_levels(act)
            act_gla_out(act)
            norm_gla.act(act)
            norm_ffn.act(act)
            wait(act, "peer_in", 2)
            act.dma_start(keys_area, keys2).then_inc(S("keys_loaded2"), 16)
            peer_act(act, 2)

        @block.vector
        def _(dve):
            dve_eng[0] = dve
            wait(dve, "vec_loaded", 16)
            take_tiles("dve", dve, group_of["mod_a"])
            wait(dve, "taken_dve", 16)
            for c in range(2):
                ins = dve.scalar_tensor_tensor(scale1[:, :, c], mod[:, 8:16, c], 1.0, v_("norm1", 0, 8), ALU.add, ALU.mult)
            chain(ins, dve)
            norm_x.dve(dve)
            wait(dve, "consts_loaded", 48)
            rope_q1.dve(dve)
            dve.tensor_copy(k_rot[:, T:T + CTX], k_raw[:, T:T + CTX]).then_inc(S("rope1_ready"), 1)
            att1.dve(dve)
            take_tiles("dve", dve, group_of["out1"])
            chain(dve.scalar_tensor_tensor(scale2[:, :], mod[:, 32:40, 0], 1.0, v_("norm2", 0, 8), ALU.add, ALU.mult), dve)
            norm_h2.dve(dve)
            peer_dve(dve, 1)
            norm_final.dve(dve)
            wait(dve, "x1_ready", 1)
            chain(dve.tensor_copy(resid[:, :, :], hin[:, :, 0:T]), dve)
            norm_n2.dve(dve)
            norm_cq.dve(dve)
            norm_ckv.dve(dve)
            norm_kpe.dve(dve)
            norm_qn.dve(dve)
            norm_qpe.dve(dve)
            norm_kn.dve(dve)
            wait(dve, "consts2_loaded", 16)
            rope_q2.dve(dve)
            rope_k2.dve(dve)
            att2.dve(dve)
            dve_gla_decay(dve)
            dve_gla_levels(dve)
            dve_gla_state(dve)
            norm_gla.dve(dve)
            wait(dve, "og_normed", 1)
            wait(dve, "taken_act", gates2_taken)
            dve.tensor_tensor(og_n, og_n, silu_g, ALU.mult).then_inc(S("gla_ready"), 1)
            for g in ("wo_mla", "wo_gla", "w_out"):
                take_tiles("dve", dve, group_of[g])
            norm_ffn.dve(dve)
            peer_dve(dve, 2)

        @block.tensor
        def _(pe):
            pe_tiles(pe, group_of["mod_a"])
            norm_x.pe(pe)
            pe_tiles(pe, group_of["kvq1"])
            wait(pe, "consts_loaded", 48)
            rope_q1.pe(pe)
            wait(pe, "rope1_ready", 2)
            att1.pe(pe)
            pe_tiles(pe, group_of["out1"])
            norm_h2.pe(pe)
            peer_pe(pe, 1)
            norm_final.pe(pe)
            norm_n2.pe(pe)
            for g in ("cq", "ckv", "kpe"):
                pe_tiles(pe, group_of[g])
            norm_cq.pe(pe)
            norm_ckv.pe(pe)
            norm_kpe.pe(pe)
            pe_tiles(pe, group_of["uq"])
            norm_qn.pe(pe)
            norm_qpe.pe(pe)
            pe_tiles(pe, group_of["ukv_k"])
            norm_kn.pe(pe)
            pe_tiles(pe, group_of["ukv_v"])
            wait(pe, "consts2_loaded", 16)
            rope_q2.pe(pe)
            rope_k2.pe(pe)
            att2.pe(pe)
            pe_gla_decay(pe)
            pe_gla_levels(pe)
            pe_gla_out(pe)
            norm_gla.pe(pe)
            for g in ("wo_mla", "wo_gla", "w_out"):
                pe_tiles(pe, group_of[g])
            norm_ffn.pe(pe)
            peer_pe(pe, 2)


def kernel(**inputs):
    import concourse.bacc as bacc
    from concourse.bass_utils import run_bass_kernel_spmd

    a = {k: np.asarray(v) for k, v in inputs.items()}
    common, consts1, consts2 = shape_constants()
    keys1 = a["peer_sub_keys"][0].reshape(16, P, P).transpose(2, 0, 1)
    keys2 = np.tile(a["peer_keys_2"][0].transpose(2, 0, 1)[:, None], (1, HEADS, 1, 1)).reshape(P, 16, P)
    arrays = {
        "stream": pack_stream(a), "xT": feature_major(a["x"][0]), "ctxT": feature_major(a["ctx"][0]),
        "metaT": feature_major(a["meta_2"]), "vectors": pack_vectors(a), "common": common,
        "consts1": consts1, "consts2": consts2, "keys1": keys1, "keys2": keys2, "w_a2": a["gla_w_a2_2"][0],
    }
    arrays = {k: np.ascontiguousarray(v) for k, v in arrays.items()}
    nc = bacc.Bacc("TRN2", target_bir_lowering=False, num_devices=1, dynamic_dma_scratch_size=1024)
    args = [nc.dram_tensor(k, v.shape, F32, kind="ExternalInput").ap() for k, v in arrays.items()]
    out = nc.dram_tensor("out", (P, KD, T), F32, kind="ExternalOutput").ap()
    build(nc, *args, out)
    result = run_bass_kernel_spmd(nc, [arrays], core_ids=[0]).results[0]["out"]
    return np.ascontiguousarray(np.asarray(result).transpose(2, 1, 0).reshape(1, T, D))
```

```python
import math

import numpy as np

import concourse.bass as bass
from concourse import mybir

F32 = mybir.dt.float32
F32R = mybir.dt.float32r
U32 = mybir.dt.uint32
ALU = mybir.AluOpType
ACT = mybir.ActivationFunctionType
AX_X = mybir.AxisListType.X

P = 128
D = 1024
KD = D // P
T = 256
NT = T // P
CTX = 256
META = 16
TM = T + META
EPS = 1e-6
NEG = -1.0e30
HEAD = 64
GROUP = 4
WINDOW = 128
HEADS = 8
TOPK = 16
NKEY = 128
TAU = 16.0
GLA_HEADS = 4
LEVELS = 7
RING = 4
UNIT = KD * P
HALF = UNIT // 2
HLRING = 4
CRING = 4
GRING = 4
ACT_HOT = 5
NPROJ = 3
B_STAT = (3, 7)
B_SCORE = (4, 5)
B_PT = 6
B_OUT = 7



def stream_order():
    order = [("mod", 16), ("in_kvq", 6)]
    mods, fills = 32, 28
    plan = [("fill1", 1)] * fills
    out = []
    for i, p in enumerate(plan):
        out.append(p)
        out += [("mod", 1)] * ((mods * (i + 1)) // fills - (mods * i) // fills)
    order += out
    order += [("attn_out", 4), ("conv_out", 4), ("mix_out", 8), ("wq1", 16), ("u1", 128), ("v1", 128),
              ("cq", 3), ("ckv", 2), ("kpe", 1), ("uq", 6), ("ukv_k", 2), ("ukv_v", 2),
              ("gq", 4), ("gk", 4), ("ga", 1), ("gv", 8), ("gate_a", 8), ("gg", 8), ("gate_b", 8),
              ("wo_mla", 8), ("wo_gla", 8), ("w_out", 8), ("wq2", 16), ("u2", 128), ("v2", 128)]
    return order


def unit_table():
    at, n = {}, 0
    for key, count in stream_order():
        at.setdefault(key, []).extend(range(n, n + count))
        n += count
    return at, n


def pack_stream(a):
    def std(w):
        n = w.shape[1] // P
        return w.reshape(KD, P, n, P).transpose(2, 1, 0, 3).reshape(n, P, UNIT)

    def short(w, per):
        k, n = w.shape[0] // P, w.shape[1] // P
        u = w.reshape(k, P, n // per, per, P).transpose(2, 1, 3, 0, 4).reshape(n // per, P, per * k * P)
        return np.concatenate([u, np.zeros((n // per, P, UNIT - per * k * P), np.float32)], axis=2)

    w_in = a["w_in"][0]
    q = w_in[:, :512].reshape(D, 2, GROUP, HEAD).transpose(0, 2, 1, 3).reshape(D, 512)
    k, v = w_in[:, 512:640], w_in[:, 640:768]
    gb, gc, u = w_in[:, 768:1280], w_in[:, 1280:1792], w_in[:, 1792:2304]
    ga, gv = w_in[:, 2304:3328], w_in[:, 3328:4352]
    attn_out = a["w_attn_out"][0].reshape(2, GROUP, HEAD, D).transpose(1, 0, 2, 3).reshape(512, D)
    w2 = a["w_in_2"][0]
    c = np.cumsum([0, 384, 256, 64, 512, 512, 1024, 16, 1024, 1024, 1024])
    part = lambda i: w2[:, c[i]:c[i + 1]]
    uq = a["mla_w_uq_2"][0].reshape(384, 8, 192)
    uq = np.concatenate([uq[:, :, :128].reshape(384, 1024), uq[:, :, 128:].reshape(384, 512)], axis=1)
    ukv = a["mla_w_ukv_2"][0].reshape(256, 8, 256)
    ukv_v = ukv[:, :, 128:].reshape(2, P, 2, 512).transpose(2, 1, 0, 3).reshape(2, P, UNIT)

    def peer_u(t):
        return t.reshape(P, P, KD, P).transpose(1, 3, 2, 0).reshape(P, P, UNIT)

    def peer_v(t):
        return t.reshape(P, P, D).transpose(1, 0, 2)

    parts = {
        "mod": std(a["w_mod"][0]), "in_kvq": std(np.concatenate([k, v, q], axis=1)),
        "fill1": std(np.concatenate([gc, u, gb, ga, gv], axis=1)),
        "attn_out": short(attn_out, 2), "conv_out": short(a["w_conv_out"][0], 2),
        "mix_out": std(a["w_mix_out"][0]), "wq1": std(a["peer_w_q"][0]),
        "u1": peer_u(a["peer_u"][0]), "v1": peer_v(a["peer_v"][0]),
        "cq": std(part(0)), "ckv": std(part(1)), "kpe": std(np.concatenate([part(2), part(2)], axis=1)),
        "uq": short(uq, 2), "ukv_k": short(ukv[:, :, :128].reshape(256, 1024), 4), "ukv_v": ukv_v,
        "gq": std(part(3)), "gk": std(part(4)), "gv": std(part(5)),
        "ga": std(np.concatenate([part(6), np.zeros((D, P - 16), np.float32)], axis=1)),
        "gg": std(part(7)), "gate_a": std(part(8)), "gate_b": std(part(9)),
        "wo_mla": std(a["w_o_mla_2"][0]), "wo_gla": std(a["w_o_gla_2"][0]), "w_out": std(a["w_out_2"][0]),
        "wq2": std(a["peer_w_q_2"][0]), "u2": peer_u(a["peer_u_2"][0]), "v2": peer_v(a["peer_v_2"][0]),
    }
    at, n = unit_table()
    out = np.empty((n, P, UNIT), np.float32)
    for key, where in at.items():
        assert len(where) == len(parts[key]), (key, len(where), len(parts[key]))
        out[where] = parts[key]
    return out



VECS = [("b_mod", 48), ("norm1", 8), ("norm2", 8), ("final", 8), ("norm_mix", 8), ("q_norm", 3), ("kv_norm", 2),
        ("qn_nope", 1), ("qn_pe", 1), ("kn_nope", 1), ("kn_pe", 1), ("b_a", 4), ("gla_norm", 2), ("norm_ffn", 8),
        ("conv_w", 12), ("sink", 8), ("cond", 16)]
CONSTS = [("ident", 128), ("blk64", 128), ("iota", 128)]
CONSTS1 = [("rot", 128), ("cos", 256), ("sin", 256), ("mask", 1024)]
CONSTS2 = [("rot", 128), ("cos", 272), ("sin", 272), ("mask", 544), ("gla_mask", 128 * (LEVELS + 1))]


def offsets(table):
    at, n = {}, 0
    for key, size in table:
        at[key] = (n, size)
        n += size
    return at, n


def pack_vectors(a):
    col = lambda v: v.reshape(-1, P).T
    twice = lambda v: np.concatenate([v, v]).reshape(P, 1)
    parts = {
        "b_mod": col(a["b_mod"][0]), "norm1": col(a["norm1_g"][0]), "norm2": col(a["norm2_g"][0]),
        "final": col(a["final_g"]), "norm_mix": col(a["norm_mix_2"][0]), "q_norm": col(a["mla_q_norm_2"][0]),
        "kv_norm": col(a["mla_kv_norm_2"][0]), "qn_nope": col(a["qn_nope_2"][0]), "qn_pe": twice(a["qn_pe_2"][0]),
        "kn_nope": col(a["kn_nope_2"][0]), "kn_pe": twice(a["kn_pe_2"][0]), "b_a": col(a["gla_b_a_2"][0]),
        "gla_norm": col(a["gla_norm_2"][0]), "norm_ffn": col(a["norm_ffn_2"][0]),
        "conv_w": a["conv_w"][0].reshape(12, P).T, "sink": np.tile(a["attn_sink"][0], (P, 1)),
        "cond": np.stack([col(a["c"][0]), col(a["c_ctx"])], axis=2).reshape(P, 16),
    }
    return np.ascontiguousarray(np.concatenate([parts[k] for k, _ in VECS], axis=1))


def rotation(half):
    r = np.zeros((P, P), np.float32)
    for i in range(P):
        first = i % (2 * half) < half
        r[i, i + half if first else i - half] = -1.0 if first else 1.0
    return r.T


def shape_constants():
    i = np.arange(P)
    f32 = np.float32
    common = {
        "ident": np.eye(P), "blk64": i[:, None] // 64 == i[None, :] // 64,
        "iota": np.tile(np.arange(P), (P, 1)),
    }
    pos = np.arange(T)
    freq = (f32(10000.0) ** (-(np.arange(16, dtype=f32)) / f32(16))).astype(f32)
    place = np.where((i % HEAD < 32)[:, None], pos[None, :] // 64, pos[None, :] % 64).astype(f32)
    angle = (place * freq[i % 16][:, None]).astype(f32)
    mask = np.zeros((NT, P, 512))
    for t in range(NT):
        far = np.abs(t * P + i[:, None] - np.arange(T)[None, :]) > WINDOW
        mask[t, :, :T] = np.where(far, NEG, 0.0)
    first = {"rot": rotation(16), "cos": np.cos(angle), "sin": np.sin(angle),
             "mask": mask.transpose(1, 0, 2).reshape(P, -1)}
    where = np.concatenate([np.arange(META, TM), np.arange(META)]).astype(f32)
    freq = (f32(10000.0) ** (-(np.arange(32, dtype=f32)) / f32(32))).astype(f32)
    angle = (where[None, :] * freq[i % 32][:, None]).astype(f32)
    mask = np.zeros((NT, P, TM))
    for t in range(NT):
        later = np.arange(T)[None, :] // 64 > (t * P + i[:, None]) // 64
        mask[t, :, :T] = np.where(later, NEG, 0.0)
    levels = np.zeros((LEVELS + 1, P, P))
    for n in range(LEVELS):
        size = 1 << n
        j, q = i[:, None] // size, i[None, :] // size
        levels[n] = (j % 2 == 0) & (q == j + 1)
    levels[LEVELS] = np.eye(P)
    second = {"rot": rotation(32), "cos": np.cos(angle), "sin": np.sin(angle),
              "mask": mask.transpose(1, 0, 2).reshape(P, -1), "gla_mask": levels.transpose(1, 0, 2).reshape(P, -1)}
    join = lambda parts, table: np.ascontiguousarray(
        np.concatenate([np.asarray(parts[k], np.float32).reshape(P, n) for k, n in table], axis=1))
    return join(common, CONSTS), join(first, CONSTS1), join(second, CONSTS2)


def feature_major(x):
    return np.ascontiguousarray(x.T.reshape(-1, P, x.shape[0]).transpose(1, 0, 2))



class Tile:

    def __init__(self, unit, ready, pairs, rows, cols, engine, take):
        self.unit, self.ready, self.pairs, self.rows, self.cols = unit, ready, pairs, rows, cols
        self.engine, self.take = engine, take


def build(nc, stream, xT, ctxT, metaT, vectors, common, consts1, consts2, keys1, keys2, w_a2, out):
    units, n_units = unit_table()

    top = [(nc.sbuf_base + 31) // 32 * 8]

    def place(name, shape, dtype=F32, at=None):
        size = math.prod(shape[1:])
        where = top[0] if at is None else at
        t = nc.alloc_sbuf_tensor_at(name, shape, dtype, offset=4 * where)
        if at is None:
            top[0] += (size + 7) // 8 * 8
        return t, where

    ring, _ = place("ring", [P, RING, UNIT])
    resid, _ = place("resid", [P, KD, T])
    s_area, _ = place("s_area", [P, NT * HEADS * 2 * P])
    arena, _ = place("arena", [P, P * T])
    gbuf, gbuf_at = place("gbuf", [P, 10240])
    hl, _ = place("hl", [P, HLRING, 2, HALF], F32R, at=gbuf_at)
    hsplit, _ = place("hsplit", [P, 2, KD, T], F32R, at=gbuf_at + 2 * HLRING * HALF)
    csplit, _ = place("csplit", [P, CRING, 2, T], F32R, at=gbuf_at + 2 * HLRING * HALF + 2 * KD * T)
    vec_at, n_vec = offsets(VECS)
    con_at, n_con = offsets(CONSTS)
    vec, _ = place("vec", [P, n_vec])
    con, _ = place("con", [P, n_con])
    mod, _ = place("mod", [P, 48, 2])
    scale1, _ = place("scale1", [P, KD, 2])
    scale2, _ = place("scale2", [P, KD])
    small, _ = place("small", [P, 32])
    gate_f, _ = place("gate_f", [P, 2, 2, P])
    onesbuf, _ = place("onesbuf", [P, P])
    topbuf, _ = place("topbuf", [P, 2, TOPK])
    idxbuf, _ = place("idxbuf", [P, 2, TOPK], U32)
    keybuf, _ = place("keybuf", [P, 2 * P])
    tmpbuf, _ = place("tmpbuf", [P, 2 * P])
    bestbuf, _ = place("bestbuf", [P, TOPK])
    posbuf, _ = place("posbuf", [P, TOPK], U32)
    assert top[0] * 4 <= nc.sbuf_usable_end, (top[0] * 4, nc.sbuf_usable_end)

    def v_(name, i=0, n=1):
        a = vec_at[name][0] + i
        return vec[:, a:a + n]

    def c_(name):
        a, n = con_at[name]
        return con[:, a:a + n]

    ident, blk64, iota, ones = c_("ident"), c_("blk64"), c_("iota"), onesbuf[:, :]

    class Space:

        def __init__(self, tensor, size):
            self.t, self.n, self.at = tensor, size, 0

        def take(self, *shape):
            n = math.prod(shape)
            a = self.at
            self.at += n
            assert self.at <= self.n, (self.at, self.n)
            ap = self.t[:, a:a + n]
            if len(shape) == 2:
                ap = ap.rearrange("p (a b) -> p a b", a=shape[0])
            if len(shape) == 3:
                ap = ap.rearrange("p (a b c) -> p a b c", a=shape[0], b=shape[1])
            return ap

    ps = nc.alloc_psum_tensor("ps", [P, 8, 512], F32)

    sems = {}

    def S(name):
        if name not in sems:
            sems[name] = nc.alloc_semaphore(name)
        return sems[name]

    def wait(eng, name, value):
        if value > 0:
            eng.wait_ge(S(name), value)

    ring_full = [f"ring_full{s}" for s in range(RING)]

    def arrival(unit):
        return ring_full[unit % RING], 16 * (unit // RING + 1)

    def slot(unit):
        return ring[:, unit % RING, :]

    A1 = Space(arena, P * T)
    xin = A1.take(KD, T + CTX)
    sq1 = A1.take(KD, T + CTX)
    h1 = A1.take(KD, T + CTX)
    q_raw, q_rot = A1.take(4, T), A1.take(4, T)
    k_raw, k_rot = A1.take(T + CTX), A1.take(T + CTX)
    rope_tmp = A1.take(TM)
    v_tok = A1.take(4, P)
    gc_b, z_b, conv_b, cg_b = A1.take(4, T), A1.take(4, T), A1.take(4, T), A1.take(4, T)
    sga, sgv, mixed = A1.take(KD, T), A1.take(KD, T), A1.take(KD, T)
    attn1 = A1.take(4, T)
    G1 = Space(gbuf, 10240)
    con1_at, n_con1 = offsets(CONSTS1)
    con1 = G1.take(n_con1)
    probs1, pt1 = G1.take(2, 512), G1.take(2, 512)
    rs1 = G1.take(2, 512)
    cprod = G1.take(2, T)
    silu_c = G1.take(KD, 2)
    sig_c = G1.take(KD, 2)

    A2 = Space(arena, P * T)
    hin, n2, sq2 = A2.take(KD, TM), A2.take(KD, TM), A2.take(KD, TM)
    cq_b, cqn, ckv_b, ckvn = A2.take(3, T), A2.take(3, T), A2.take(2, TM), A2.take(2, TM)
    kpe_raw, kpe_n, kpe_rot = A2.take(TM), A2.take(TM), A2.take(TM)
    qnope, qnope_n = A2.take(HEADS, T), A2.take(HEADS, T)
    qpe, qpe_rot = A2.take(4, T), A2.take(4, T)
    knope, knope_n = A2.take(HEADS, TM), A2.take(HEADS, TM)
    v2_flat = A2.take(3 * D)
    v2 = v2_flat.rearrange("p (a d) -> p a d", a=3)
    attn2 = A2.take(HEADS, T)
    G2 = Space(gbuf, 10240)
    con2_at, n_con2 = offsets(CONSTS2)
    con2 = G2.take(n_con2)
    probs2, pt2 = G2.take(2, TM), G2.take(2, 3 * P)
    rs2 = G2.take(2, TM)
    ga_b, wa2_b = G2.take(TM), G2.take(512)
    la, lb = G2.take(GLA_HEADS, TM), G2.take(GLA_HEADS, TM)
    silu_g = G2.take(KD, T)
    SA = Space(s_area, NT * HEADS * 2 * P)
    sgate_a, sgate_b = SA.take(KD, T), SA.take(KD, T)
    gq, gk = A2.take(GLA_HEADS, T), A2.take(GLA_HEADS, TM)
    gv = A2.take(3, D)
    A3 = Space(arena, P * T)
    A3.take(3 * KD, TM)
    gd2 = [A3.take(GLA_HEADS, P) for _ in range(2)]
    gqd = [A3.take(GLA_HEADS, P) for _ in range(2)]
    gkd = [A3.take(GLA_HEADS, P) for _ in range(2)]
    amat = [A3.take(GLA_HEADS, P) for _ in range(NT)]
    atmp = A3.take(GLA_HEADS, P)
    qdec = A3.take(GLA_HEADS, T)
    kdec = [A3.take(GLA_HEADS, META), A3.take(GLA_HEADS, P)]
    kdecT = [A3.take(GLA_HEADS, P), A3.take(GLA_HEADS, P)]
    state = [A3.take(GLA_HEADS, 256), A3.take(GLA_HEADS, 256)]
    blast = A3.take(2, GLA_HEADS)
    o_gla = A3.take(KD, T)
    og_n = A3.take(KD, T)
    assert A3.at <= A2.at - 3 * D - GLA_HEADS * (T + TM) - HEADS * T
    mixed2 = v2_flat[:, 0:KD * T].rearrange("p (k t) -> p k t", k=KD)

    def con1_(name):
        a, n = con1_at[name]
        return con1[:, a:a + n]

    def con2_(name):
        a, n = con2_at[name]
        return con2[:, a:a + n]

    q_area = arena[:, P * T - 16 * T:]
    keys_area = arena[:, P * T - 16 * T - 16 * P:P * T - 16 * T].rearrange("p (j n) -> p j n", j=16)
    acts = arena
    K = Space(gbuf, 10240)
    K.take(8192)
    sum_pos, sum_best = K.take(NT * P), K.take(NT * P)
    rank1, rank2 = K.take(NT, P), K.take(NT, P)
    chosen = K.take(3, NT * P)
    gate_sum = K.take(2, NT * HEADS)
    lookup = s_area[:, 0:2048].rearrange("p (c n) -> p c n", c=2)
    KINDS = 5
    sel = s_area[:, 2048:2048 + KINDS * T].rearrange("p (c t) -> p c t", c=KINDS)
    hot1 = gbuf[:, 0:GRING * 8 * P].rearrange("p (r t i) -> p r t i", r=GRING, t=8)
    hot2 = gbuf[:, GRING * 8 * P:2 * GRING * 8 * P].rearrange("p (r t i) -> p r t i", r=GRING, t=8)
    H = Space(gbuf, 10240)
    H.take(8192)
    stage = [H.take(KINDS, 8) for _ in range(GRING)]
    hot_dist = [H.take(ACT_HOT, P) for _ in range(2)]

    tiles = []
    taken = {"act": 0, "dve": 0}
    group_of = {}

    def tile(group, unit, ready, pairs, rows, cols, engine, take):
        t = Tile(unit, ready, pairs, rows, cols, engine, take)
        taken[engine] += 1
        t.n, t.seq, t.bank = len(tiles), taken[engine], len(tiles) % NPROJ
        tiles.append(t)
        group_of.setdefault(group, []).append(t.n)

    def std_pairs(unit, rhs, k=KD, at=0):
        return [(slot(unit)[:, at + i * P:at + (i + 1) * P], rhs[:, i]) for i in range(k)]

    def take_copy(dst):
        def f(kind, eng, src):
            return eng.copy(dst, src) if kind == "act" else eng.tensor_copy(dst, src)
        return f

    def take_func(dst, func):
        def f(kind, eng, src):
            return eng.activation(dst, src, func)
        return f

    def take_times(dst, other, scalar=None):
        def f(kind, eng, src):
            if scalar is None:
                return eng.tensor_tensor(dst, src, other, ALU.mult)
            return eng.scalar_tensor_tensor(dst, src, scalar, other, ALU.mult, ALU.mult)
        return f

    mod_units = units["mod"]

    def mod_tile(group, n):
        u = mod_units[n]
        tile(group, u, ("silu_ready", 1), std_pairs(u, silu_c), P, 2, "dve",
             lambda kind, eng, src: eng.tensor_scalar(mod[:, n, :], src, v_("b_mod", n), None, ALU.add))

    for n in range(16):
        mod_tile("mod_a", n)

    u0 = units["in_kvq"]
    tile("kvq1", u0[0], ("h1_ready", 1), std_pairs(u0[0], h1), P, T + CTX, "act", take_copy(k_raw))

    def v_pairs(u, src, t, n):
        return [(src[:, k, t:t + n], slot(u)[:, k * P:(k + 1) * P]) for k in range(KD)]

    for t in range(4):
        tile("kvq1", u0[1], ("h1_ready", 1), v_pairs(u0[1], h1, t * P, P), P, P, "act", take_copy(v_tok[:, t, :]))
    for j in range(4):
        tile("kvq1", u0[2 + j], ("h1_ready", 1), std_pairs(u0[2 + j], h1[:, :, 0:T]), P, T, "act",
             take_copy(q_raw[:, j, :]))
    kv1_taken = taken["act"]

    next_mod = 16
    f1 = units["fill1"]

    def conv_take(i):
        def f(kind, eng, src):
            chain(eng.tensor_tensor(z_b[:, i, :], src, gc_b[:, i, :], ALU.mult), eng)
            w = lambda tap: v_("conv_w", tap * 4 + i)
            chain(eng.tensor_scalar(conv_b[:, i, :], z_b[:, i, :], w(1), None, ALU.mult), eng)
            chain(eng.scalar_tensor_tensor(conv_b[:, i, 1:T], z_b[:, i, 0:T - 1], w(0), conv_b[:, i, 1:T],
                                           ALU.mult, ALU.add), eng)
            return eng.scalar_tensor_tensor(conv_b[:, i, 0:T - 1], z_b[:, i, 1:T], w(2), conv_b[:, i, 0:T - 1],
                                            ALU.mult, ALU.add)
        return f

    for i in range(28):
        u = f1[i]
        pairs = std_pairs(u, h1[:, :, 0:T])
        if i < 4:
            tile("fill1", u, None, pairs, P, T, "dve", take_copy(gc_b[:, i, :]))
        elif i < 8:
            tile("fill1", u, None, pairs, P, T, "dve", conv_take(i - 4))
        elif i < 12:
            tile("fill1", u, None, pairs, P, T, "dve", take_times(cg_b[:, i - 8, :], conv_b[:, i - 8, :]))
        elif i < 20:
            tile("fill1", u, None, pairs, P, T, "act", take_func(sga[:, i - 12, :], ACT.Sigmoid))
        else:
            tile("fill1", u, None, pairs, P, T, "act", take_func(sgv[:, i - 20, :], ACT.Sigmoid))
        while next_mod < 48 and (i == 27 or mod_units[next_mod] < f1[i + 1]):
            mod_tile("fill1", next_mod)
            next_mod += 1
    assert next_mod == 48

    sig1_taken = taken["act"]

    def ao_take(n):
        def f(kind, eng, src):
            if n == 0:
                wait(eng, "taken_act", sig1_taken)
            return eng.tensor_tensor(mixed[:, n, :], src, sga[:, n, :], ALU.mult)
        return f

    def add_take(dst, gate, tmp):
        def f(kind, eng, src):
            chain(eng.tensor_tensor(tmp, src, gate, ALU.mult), eng)
            return eng.tensor_tensor(dst, dst, tmp, ALU.add)
        return f

    for i, u in enumerate(units["attn_out"]):
        for s in range(2):
            tile("out1", u, ("attn_out_ready", 4), std_pairs(u, attn1, 4, at=s * 4 * P), P, T, "dve", ao_take(2 * i + s))
    for i, u in enumerate(units["conv_out"]):
        for s in range(2):
            n = 2 * i + s
            tile("out1", u, ("taken_dve", "conv"), std_pairs(u, cg_b, 4, at=s * 4 * P), P, T, "dve",
                 add_take(mixed[:, n, :], sgv[:, n, :], cprod[:, n % 2, :]))
    mixed_taken = taken["dve"]

    def resid_take(n, scalar):
        def f(kind, eng, src):
            dst = resid[:, n, :]
            if scalar is None:
                return eng.tensor_tensor(dst, src, dst, ALU.add)
            return eng.scalar_tensor_tensor(dst, src, scalar(n), dst, ALU.mult, ALU.add)
        return f

    for n, u in enumerate(units["mix_out"]):
        tile("out1", u, ("taken_dve", mixed_taken), std_pairs(u, mixed), P, T, "dve",
             resid_take(n, lambda n: mod[:, 16 + n, 0:1]))

    h_full = gbuf[:, 8192:10240].rearrange("p (k t) -> p k t", k=KD)

    def wq_tiles(b):
        for j, u in enumerate(units[f"wq{b}"]):
            tile(f"wq{b}", u, ("peer_in", b), std_pairs(u, h_full), P, T, "act" if j % 2 else "dve",
                 take_copy(q_area[:, j * T:(j + 1) * T]))
    wq_tiles(1)
    wq_taken = {1: dict(taken)}

    def group2(key, dst, ready, rhs, n, engine="act", k=KD, per=1, make=take_copy, width=None):
        for i, u in enumerate(units[key]):
            for s in range(per):
                m = i * per + s
                tile(key, u, ready, std_pairs(u, rhs, k, at=s * k * P), P, n, engine, make(dst[:, m, :]))

    nT = n2[:, :, 0:T]
    group2("cq", cq_b, ("n2_ready", 1), nT, T)
    group2("ckv", ckv_b, ("n2_ready", 1), n2, TM)
    tile("kpe", units["kpe"][0], ("n2_ready", 1), std_pairs(units["kpe"][0], n2), P, TM, "act", take_copy(kpe_raw))
    c_taken = taken["act"]
    for i, u in enumerate(units["uq"]):
        for s in range(2):
            m = 2 * i + s
            dst = qnope[:, m, :] if m < HEADS else qpe[:, m - HEADS, :]
            tile("uq", u, ("cq_ready", 1), std_pairs(u, cqn, 3, at=s * 3 * P), P, T, "act", take_copy(dst))
    uq_taken = taken["act"]
    group2("ukv_k", knope, ("ckv_ready", 1), ckvn, TM, k=2, per=4)
    uk_taken = taken["act"]
    KT2 = [(0, P), (P, P), (T, META)]
    for half, u in enumerate(units["ukv_v"]):
        for t, (a, n) in enumerate(KT2):
            pairs = [(ckvn[:, k, a:a + n], slot(u)[:, k * 512:(k + 1) * 512]) for k in range(2)]
            tile("ukv_v", u, None, pairs, n, 512, "act", take_copy(v2[0:n, t, half * 512:(half + 1) * 512]))
    v2_taken = taken["act"]

    def gq_take(dst):
        return lambda kind, eng, src: eng.activation(dst, src, ACT.Copy, scale=float(P) ** -0.5)
    group2("gq", gq, None, nT, T, make=gq_take)
    group2("gk", gk, None, n2, TM)
    tile("ga", units["ga"][0], None, std_pairs(units["ga"][0], n2), P, TM, "act", take_copy(ga_b))
    ga_taken = taken["act"]
    for i, u in enumerate(units["gv"]):
        for t, (a, n) in enumerate(KT2):
            tile("gv", u, None, v_pairs(u, n2, a, n), n, P, "act", take_copy(gv[0:n, t, i * P:(i + 1) * P]))
    gv_taken = taken["act"]
    group2("gate_a", sgate_a, None, nT, T, make=lambda d: take_func(d, ACT.Sigmoid))
    group2("gg", silu_g, None, nT, T, make=lambda d: take_func(d, ACT.Silu))
    group2("gate_b", sgate_b, None, nT, T, make=lambda d: take_func(d, ACT.Sigmoid))
    gates2_taken = taken["act"]

    def wo_mla_take(n):
        def f(kind, eng, src):
            if n == 0:
                wait(eng, "taken_act", gates2_taken)
            return eng.tensor_tensor(mixed2[:, n, :], src, sgate_a[:, n, :], ALU.mult)
        return f
    for n, u in enumerate(units["wo_mla"]):
        tile("wo_mla", u, ("attn_out_ready", 4 + HEADS), std_pairs(u, attn2), P, T, "dve", wo_mla_take(n))
    for n, u in enumerate(units["wo_gla"]):
        tile("wo_gla", u, ("gla_ready", 1), std_pairs(u, og_n), P, T, "dve",
             add_take(mixed2[:, n, :], sgate_b[:, n, :], rs2[:, n % 2, 0:T]))
    mixed2_taken = taken["dve"]
    for n, u in enumerate(units["w_out"]):
        tile("w_out", u, ("taken_dve", mixed2_taken), std_pairs(u, mixed2), P, T, "dve", resid_take(n, None))
    wq_tiles(2)
    wq_taken[2] = dict(taken)

    conv_taken = max(tiles[n].seq for n in group_of["fill1"] if tiles[n].engine == "dve" and tiles[n].cols == T)
    for t in tiles:
        if t.ready and t.ready[1] == "conv":
            t.ready = (t.ready[0], conv_taken)
    last_tile = {t.unit: t.n for t in tiles}

    chained = {}

    def chain(ins, eng):
        key = "dve_chain" if eng is dve_eng[0] else "act_chain"
        chained[key] = chained.get(key, 0) + 1
        ins.then_inc(S(key), 1)
        eng.wait_ge(S(key), chained[key])

    dve_eng = [None]

    def pe_tiles(pe, numbers):
        for n in numbers:
            t = tiles[n]
            pe.wait_ge(S(arrival(t.unit)[0]), arrival(t.unit)[1])
            if t.ready:
                wait(pe, *t.ready)
            if n >= NPROJ:
                before = tiles[n - NPROJ]
                wait(pe, "taken_" + before.engine, before.seq)
            last = len(t.pairs) - 1
            for i, (lhs, rhs) in enumerate(t.pairs):
                mm = pe.matmul(ps[0:t.rows, t.bank, 0:t.cols], lhs, rhs, start=(i == 0), stop=(i == last))
            mm.then_inc(S("tile_done"), 1)

    def take_tiles(kind, eng, numbers):
        for n in numbers:
            t = tiles[n]
            if t.engine == kind:
                wait(eng, "tile_done", n + 1)
                t.take(kind, eng, ps[0:t.rows, t.bank, 0:t.cols]).then_inc(S("taken_" + kind), 1)

    def pieces(group, parts):
        n = group_of[group] if isinstance(group, str) else [m for g in group for m in group_of[g]]
        return [n[len(n) * i // parts:len(n) * (i + 1) // parts] for i in range(parts)]

    norm_count = [0, 0]

    class Norm:

        def __init__(self, src, squares, n, cols, groups, lhs, width, root, ready, gain, dst=None, done=None, apply=None):
            self.src = src
            self.squares = squares
            self.n = n
            self.cols = cols
            self.groups = groups
            self.lhs = lhs
            self.width = width
            self.root = root
            self.ready = ready
            self.gain = gain
            self.dst = dst
            self.done = done
            self.apply = apply
            self.id, self.g0 = norm_count[0], norm_count[1]
            norm_count[0] += 1
            norm_count[1] += len(groups)

        def act(self, eng):
            for r in self.ready:
                wait(eng, *r)
            eng.activation(self.squares[:, 0:self.n, 0:self.cols], self.src, ACT.Square).then_inc(S("norm_squared"), 1)
            for g in range(len(self.groups)):
                wait(eng, "norm_inverted", self.g0 + g + 1)
                r = self.root[:, (self.g0 + g) % 2, 0:self.cols]
                eng.sqrt(r, r).then_inc(S("norm_rooted"), 1)

        def pe(self, eng):
            wait(eng, "norm_squared", self.id + 1)
            for g, group in enumerate(self.groups):
                wait(eng, "norm_inverted", self.g0 + g - 1)
                bank = B_STAT[(self.g0 + g) % 2]
                for i, k in enumerate(group):
                    mm = eng.matmul(ps[:, bank, 0:self.cols], self.lhs, self.squares[:, k, 0:self.cols],
                                    start=(i == 0), stop=(i == len(group) - 1))
                mm.then_inc(S("norm_summed"), 1)

        def dve(self, eng):
            def invert(g):
                r = self.root[:, (self.g0 + g) % 2, 0:self.cols]
                wait(eng, "norm_summed", self.g0 + g + 1)
                chain(eng.tensor_scalar(r, ps[:, B_STAT[(self.g0 + g) % 2], 0:self.cols], 1.0 / self.width, EPS,
                                        ALU.mult, ALU.add), eng)
                eng.reciprocal(r, r).then_inc(S("norm_inverted"), 1)

            for r in self.ready:
                wait(eng, *r)
            n = len(self.groups)
            invert(0)
            for g in range(n):
                if g + 1 < n:
                    invert(g + 1)
                wait(eng, "norm_rooted", self.g0 + g + 1)
                root = self.root[:, (self.g0 + g) % 2, 0:self.cols]
                if self.apply:
                    self.apply(eng, root)
                    continue
                for k in self.groups[g]:
                    ins = eng.scalar_tensor_tensor(self.dst(k), self.src[:, k, :], self.gain(k), root, ALU.mult, ALU.mult)
                if g == n - 1 and self.done:
                    ins.then_inc(S(self.done), 1)
                else:
                    chain(ins, eng)

    def flat_groups(n):
        return [[k] for k in range(n)]

    def apply_h1(eng, root):
        for half in range(2):
            for k in range(KD):
                a = slice(half * T, (half + 1) * T)
                ins = eng.scalar_tensor_tensor(h1[:, k, a], xin[:, k, a], scale1[:, k, half:half + 1], root[:, a],
                                               ALU.mult, ALU.mult)
        chain(ins, eng)
        for half in range(2):
            for k in range(KD):
                a = slice(half * T, (half + 1) * T)
                ins = eng.tensor_scalar(h1[:, k, a], h1[:, k, a], mod[:, k, half:half + 1], None, ALU.add)
        ins.then_inc(S("h1_ready"), 1)

    def apply_h2(eng, root):
        for k in range(KD):
            ins = eng.scalar_tensor_tensor(h_full[:, k, :], resid[:, k, :], scale2[:, k:k + 1], root, ALU.mult, ALU.mult)
        chain(ins, eng)
        for k in range(KD):
            ins = eng.tensor_scalar(h_full[:, k, :], h_full[:, k, :], mod[:, 24 + k, 0:1], None, ALU.add)
        ins.then_inc(S("peer_in"), 1)

    norm_x = Norm(xin, sq1, KD, T + CTX, [list(range(KD))], ones, D, rs1,
                  [("x_loaded", 32), ("ones_ready", 1)], None, apply=apply_h1)
    out1_taken = tiles[group_of["out1"][-1]].seq
    norm_h2 = Norm(resid[:, :, :], sq1, KD, T, [list(range(KD))], ones, D, rs1, [("taken_dve", out1_taken)], None,
                   apply=apply_h2)
    norm_final = Norm(resid[:, :, :], sq2, KD, T, [list(range(KD))], ones, D, rs2, [("peer_out", 1)],
                      lambda k: v_("final", k), dst=lambda k: hin[:, k, 0:T], done="x1_ready")
    norm_n2 = Norm(hin, sq2, KD, TM, [list(range(KD))], ones, D, rs2, [("x1_ready", 1), ("meta_loaded", 16)],
                   lambda k: v_("norm_mix", k), dst=lambda k: n2[:, k, :], done="n2_ready")
    norm_cq = Norm(cq_b, sq2, 3, T, [[0, 1, 2]], ones, 384, rs2, [("taken_act", c_taken)],
                   lambda k: v_("q_norm", k), dst=lambda k: cqn[:, k, :], done="cq_ready")
    norm_ckv = Norm(ckv_b, sq2, 2, TM, [[0, 1]], ones, 256, rs2, [("norm_summed", 5)],
                    lambda k: v_("kv_norm", k), dst=lambda k: ckvn[:, k, :], done="ckv_ready")
    kpe3 = kpe_raw.rearrange("p (a t) -> p a t", a=1)
    norm_kpe = Norm(kpe3, sq2, 1, TM, [[0]], blk64, 64, rs2, [("norm_summed", 6)],
                    lambda k: v_("kn_pe"), dst=lambda k: kpe_n, done="kpe_ready")
    norm_qn = Norm(qnope, sq2, HEADS, T, flat_groups(HEADS), ones, P, rs2, [("taken_act", uq_taken), ("norm_summed", 7)],
                   lambda k: v_("qn_nope"), dst=lambda k: qnope_n[:, k, :], done="qn_ready")
    norm_qpe = Norm(qpe, sq2, 4, T, flat_groups(4), blk64, 64, rs2, [("norm_summed", 15)],
                    lambda k: v_("qn_pe"), dst=lambda k: qpe[:, k, :], done="qpe_ready")
    norm_kn = Norm(knope, sq2, HEADS, TM, flat_groups(HEADS), ones, P, rs2, [("taken_act", uk_taken), ("norm_summed", 19)],
                   lambda k: v_("kn_nope"), dst=lambda k: knope_n[:, k, :], done="kn_ready")
    norm_gla = Norm(o_gla, sq2, KD, T, [[2 * h, 2 * h + 1] for h in range(GLA_HEADS)], ones, 256, rs2,
                    [("o_gla_ready", 4), ("norm_summed", 27)], lambda k: v_("gla_norm", k % 2),
                    dst=lambda k: og_n[:, k, :], done="og_normed")
    norm_ffn = Norm(resid[:, :, :], sq2, KD, T, [list(range(KD))], ones, D, rs2,
                    [("taken_dve", tiles[group_of["w_out"][-1]].seq)],
                    lambda k: v_("norm_ffn", k), dst=lambda k: h_full[:, k, :], done="peer_in")

    rope_count = [0]

    class Rope:

        def __init__(self, items, n, rot, cos, sin, ready, tmp, done):
            self.items = items
            self.n = n
            self.rot = rot
            self.cos = cos
            self.sin = sin
            self.ready = ready
            self.tmp = tmp
            self.done = done
            self.r0 = rope_count[0]
            rope_count[0] += len(items)

        def pe(self, eng):
            for r in self.ready:
                wait(eng, *r)
            for i, (src, _) in enumerate(self.items):
                m = self.r0 + i
                wait(eng, "rope_read", m - 1)
                eng.matmul(ps[:, B_STAT[m % 2], 0:self.n], self.rot, src, start=True, stop=True).then_inc(S("rope_swapped"), 1)

        def dve(self, eng):
            for r in self.ready:
                wait(eng, *r)
            for i, (src, dst) in enumerate(self.items):
                m = self.r0 + i
                eng.tensor_tensor(dst, src, self.cos, ALU.mult)
                wait(eng, "rope_swapped", m + 1)
                ins = eng.tensor_tensor(self.tmp, ps[:, B_STAT[m % 2], 0:self.n], self.sin, ALU.mult)
                ins.then_inc(S("rope_read"), 1)
                wait(eng, "rope_read", m + 1)
                ins = eng.tensor_tensor(dst, dst, self.tmp, ALU.add)
                if i == len(self.items) - 1:
                    ins.then_inc(S(self.done), 1)
                else:
                    chain(ins, eng)

    rope_q1 = Rope([(k_raw[:, 0:T], k_rot[:, 0:T])] + [(q_raw[:, j, :], q_rot[:, j, :]) for j in range(4)], T,
                   con1_("rot"), con1_("cos"), con1_("sin"), [("taken_act", kv1_taken), ("norm_inverted", 1)],
                   rope_tmp[:, 0:T], "rope1_ready")
    rope_q2 = Rope([(qpe[:, j, :], qpe_rot[:, j, :]) for j in range(4)], T, con2_("rot"),
                   con2_("cos")[:, 0:T], con2_("sin")[:, 0:T], [("qpe_ready", 1), ("norm_inverted", 27), ("kn_ready", 1)],
                   rs2[:, 0, 0:T], "rope2_ready")
    rope_k2 = Rope([(kpe_n, kpe_rot)], TM, con2_("rot"), con2_("cos"), con2_("sin"), [("kpe_ready", 1)],
                   rs2[:, 1, :], "rope2_ready")

    att_count = [0, 0]

    class Attention:

        def __init__(self, items, n_keys, key_tiles, scale, probs, pt, fill, ready, outs):
            self.items = items
            self.n_keys = n_keys
            self.key_tiles = key_tiles
            self.scale = scale
            self.probs = probs
            self.pt = pt
            self.fill = fill
            self.ready = ready
            self.outs = outs
            self.i0, self.o0 = att_count
            att_count[0] += len(items)
            att_count[1] += len(outs)

        def pe(self, eng):
            for r in self.ready:
                wait(eng, *r)
            n = len(self.items)

            def scores_of(i):
                it, m = self.items[i], self.i0 + i
                wait(eng, "att_masked", m - 1)
                for x, (lhs, rhs) in enumerate(it["scores"]):
                    mm = eng.matmul(ps[:, B_SCORE[m % 2], 0:self.n_keys], lhs, rhs, start=(x == 0),
                                    stop=(x == len(it["scores"]) - 1))
                mm.then_inc(S("att_scored"), 1)

            scores_of(0)
            scores_of(1)
            for i, it in enumerate(self.items):
                m = self.i0 + i
                pe_tiles(eng, self.fill[i])
                wait(eng, "att_prob", m + 1)
                wait(eng, "att_pt", m)
                for x, (a, w) in enumerate(self.key_tiles):
                    mm = eng.transpose(ps[0:w, B_PT, x * P:x * P + P], self.probs[:, m % 2, a:a + w], ident)
                mm.then_inc(S("att_turned"), 1)
                if i + 2 < n:
                    scores_of(i + 2)
                wait(eng, "att_pt", m + 1)
                if it["wait_out"] > 0:
                    wait(eng, "attn_out_ready", self.o0 + it["wait_out"])
                for x, (a, w) in enumerate(self.key_tiles):
                    mm = eng.matmul(it["out"], it["v"](x), self.pt[0:w, m % 2, x * P:(x + 1) * P], start=(x == 0),
                                    stop=(x == len(self.key_tiles) - 1))
                mm.then_inc(S("att_summed"), 1)

        def dve(self, eng):
            n = len(self.items)
            for r in self.ready:
                wait(eng, *r)

            def mask(i):
                it, m = self.items[i], self.i0 + i
                p = self.probs[:, m % 2, 0:self.n_keys]
                b = (m % 2) * 8
                wait(eng, "att_scored", m + 1)
                wait(eng, "att_turned", m - 1)
                ins = eng.scalar_tensor_tensor(p, ps[:, B_SCORE[m % 2], 0:self.n_keys], self.scale, it["mask"],
                                               ALU.mult, ALU.add)
                ins.then_inc(S("att_masked"), 1)
                wait(eng, "att_masked", m + 1)
                chain(eng.tensor_reduce(small[:, b:b + 1], p, AX_X, ALU.max), eng)
                if it["sink"] is None:
                    ins = eng.tensor_scalar(small[:, b + 1:b + 2], small[:, b:b + 1], -1.0, None, ALU.mult)
                else:
                    ins = eng.tensor_scalar(small[:, b + 1:b + 2], small[:, b:b + 1], v_("sink", it["sink"]), -1.0,
                                            ALU.max, ALU.mult)
                ins.then_inc(S("att_max"), 1)

            def normalise(i):
                it, m = self.items[i], self.i0 + i
                b = (m % 2) * 8
                p = self.probs[:, m % 2, 0:self.n_keys]
                wait(eng, "att_exp", m + 1)
                if it["sink"] is not None:
                    chain(eng.tensor_tensor(small[:, b + 2:b + 3], small[:, b + 2:b + 3], small[:, b + 3:b + 4], ALU.add), eng)
                chain(eng.reciprocal(small[:, b + 4:b + 5], small[:, b + 2:b + 3]), eng)
                eng.tensor_scalar(p, p, small[:, b + 4:b + 5], None, ALU.mult).then_inc(S("att_prob"), 1)

            mask(0)
            for i in range(n):
                take_tiles("dve", eng, self.fill[i])
                normalise(i)
                if i + 1 < n:
                    mask(i + 1)

        def act(self, eng):
            for i, it in enumerate(self.items):
                m = self.i0 + i
                b = (m % 2) * 8
                p = self.probs[:, m % 2, 0:self.n_keys]
                wait(eng, "att_max", m + 1)
                if it["sink"] is not None:
                    eng.activation(small[:, b + 3:b + 4], v_("sink", it["sink"]), ACT.Exp, bias=small[:, b + 1:b + 2])
                eng.activation(p, p, ACT.Exp, bias=small[:, b + 1:b + 2],
                               accum_out=small[:, b + 2:b + 3]).then_inc(S("att_exp"), 1)
                take_tiles("act", eng, self.fill[i])
                wait(eng, "att_turned", m + 1)
                wait(eng, "att_summed", m - 1)
                w = len(self.key_tiles) * P
                full = [x for x, (_, k) in enumerate(self.key_tiles) if k == P]
                ins = eng.copy(self.pt[:, m % 2, 0:len(full) * P], ps[:, B_PT, 0:len(full) * P])
                if len(full) < len(self.key_tiles):
                    k = self.key_tiles[-1][1]
                    ins = eng.copy(self.pt[0:k, m % 2, len(full) * P:w], ps[0:k, B_PT, len(full) * P:w])
                ins.then_inc(S("att_pt"), 1)
                if it["copy"] is not None:
                    wait(eng, "att_summed", m + 1)
                    src, dst = self.outs[it["copy"]]
                    eng.copy(dst, src).then_inc(S("attn_out_ready"), 1)

    def region(x):
        return ps[:, B_OUT, (x % 2) * T:(x % 2 + 1) * T]

    items1, outs1 = [], []
    for j in range(4):
        outs1.append((region(j), attn1[:, j, :]))
        for g in range(2):
            for t in range(NT):
                rows = slice(g * HEAD, (g + 1) * HEAD)
                last = g == 1 and t == NT - 1
                items1.append(dict(
                    scores=[(q_rot[rows, j, t * P:(t + 1) * P], k_rot[rows, :])],
                    mask=con1_("mask")[:, t * 512:(t + 1) * 512], sink=g * GROUP + j,
                    v=lambda x, g=g: v_tok[:, x, g * HEAD:(g + 1) * HEAD],
                    out=ps[rows, B_OUT, (j % 2) * T + t * P:(j % 2) * T + (t + 1) * P],
                    copy=j if last else None, wait_out=j - 1))
    att1 = Attention(items1, T + CTX, [(i * P, P) for i in range(4)], HEAD ** -0.5, probs1, pt1,
                     pieces("fill1", len(items1)), [("rope1_ready", 1)], outs1)
    items2, outs2 = [], []
    for h in range(HEADS):
        outs2.append((region(h), attn2[:, h, :]))
        rows = slice((h % 2) * 64, (h % 2) * 64 + 64)
        for t in range(NT):
            q = slice(t * P, (t + 1) * P)
            items2.append(dict(
                scores=[(qnope_n[:, h, q], knope_n[:, h, :]), (qpe_rot[rows, h // 2, q], kpe_rot[rows, :])],
                mask=con2_("mask")[:, t * TM:(t + 1) * TM], sink=None,
                v=lambda x, h=h: v2[0:KT2[x][1], x, h * P:(h + 1) * P],
                out=ps[:, B_OUT, (h % 2) * T + t * P:(h % 2) * T + (t + 1) * P],
                copy=h if t == NT - 1 else None, wait_out=h - 1))
    att2 = Attention(items2, TM, KT2, 192 ** -0.5, probs2, pt2,
                     pieces(["gq", "gk", "ga", "gv", "gate_a", "gg", "gate_b"], len(items2)),
                     [("kn_ready", 1), ("rope2_ready", 2), ("taken_act", v2_taken)], outs2)

    def gla_bank(m):
        return B_SCORE[m % 2]

    def pe_gla_decay(pe):
        wait(pe, "taken_act", ga_taken)
        wait(pe, "wa2_loaded", 16)
        wait(pe, "att_summed", 32)
        wait(pe, "attn_out_ready", 4 + HEADS)
        for h in range(GLA_HEADS):
            bank = [3, 4, 5, 6][h]
            pe.matmul(ps[:, bank, 0:TM], wa2_b[0:16, h * P:(h + 1) * P], ga_b[0:16, :], start=True,
                      stop=True).then_inc(S("gla_logit"), 1)

    def dve_gla_decay(dve):
        wait(dve, "taken_act", gates2_taken)
        for h in range(GLA_HEADS):
            wait(dve, "gla_logit", h + 1)
            ins = dve.tensor_scalar(la[:, h, :], ps[:, [3, 4, 5, 6][h], 0:TM], v_("b_a", h), None, ALU.add)
        chain(ins, dve)
        dve.scalar_tensor_tensor(lb, la, -1.0, la, ALU.mult, ALU.max).then_inc(S("gla_abs"), 1)
        wait(dve, "gla_log", 1)
        chain(dve.tensor_scalar(la, la, 0.0, None, ALU.min), dve)
        chain(dve.tensor_tensor(la, la, lb, ALU.subtract), dve)
        chain(dve.tensor_scalar(la, la, 1.0 / TAU, None, ALU.mult), dve)
        for h in range(GLA_HEADS):
            for a, w in KT2:
                ins = dve.tensor_tensor_scan(lb[:, h, a:a + w], ones[:, 0:w], la[:, h, a:a + w], 0.0, ALU.mult, ALU.add)
        chain(ins, dve)
        for n, (a, w) in enumerate([KT2[2], KT2[0]]):
            dve.tensor_tensor(kdec[n], lb[:, :, a + w - 1:a + w].broadcast_to([P, GLA_HEADS, w]), lb[:, :, a:a + w], ALU.subtract)
        dve.tensor_copy(blast[:, 1, :], lb[:, :, P - 1]).then_inc(S("gla_ends"), 1)
        wait(dve, "gla_ends_exp", 1)
        for n, (a, w) in enumerate([KT2[2], KT2[0]]):
            dve.tensor_tensor(kdec[n], kdec[n], gk[:, :, a:a + w], ALU.mult)
        dve.tensor_tensor(qdec, qdec, gq, ALU.mult).then_inc(S("gla_dec"), 1)

    def act_gla_decay(act):
        wait(act, "gla_abs", 1)
        act.activation(lb, lb, ACT.Exp, scale=-1.0).then_inc(S("gla_e"), 1)
        wait(act, "gla_e", 1)
        act.activation(lb, lb, ACT.Ln, bias=1.0).then_inc(S("gla_log"), 1)
        wait(act, "gla_ends", 1)
        act.activation(qdec, lb[:, :, 0:T], ACT.Exp)
        act.activation(kdec[0], kdec[0], ACT.Exp)
        act.activation(kdec[1], kdec[1], ACT.Exp)
        act.activation(blast[:, 1, :], blast[:, 1, :], ACT.Exp).then_inc(S("gla_ends_exp"), 1)

    gla_steps = [(t, n) for t in range(NT) for n in range(LEVELS + 1)]

    def dve_gla_levels(dve):
        def prepare(m):
            t, n = gla_steps[m]
            if n == LEVELS:
                return
            size = 1 << n
            a = t * P
            gd = gd2[(t * LEVELS + n) % 2]
            for h in range(GLA_HEADS):
                bh = lb[:, h, a:a + P].rearrange("p (m s) -> p m s", s=2 * size)
                dh = gd[:, h, :].rearrange("p (m s) -> p m s", s=2 * size)
                r = bh[:, :, size - 1:size].broadcast_to([P, P // (2 * size), 2 * size])
                ins = dve.tensor_tensor(dh, bh, r, ALU.subtract)
            chain(ins, dve)
            dve.scalar_tensor_tensor(gd, gd, -1.0, gd, ALU.mult, ALU.max).then_inc(S("gla_dist"), 1)

        dist = 0
        for m, (t, n) in enumerate(gla_steps):
            a = t * P
            gd = gd2[(t * LEVELS + n) % 2]
            prepare(m)
            if n < LEVELS:
                dist += 1
                wait(dve, "gla_fade", dist)
            wait(dve, "gla_pair", m - 1)
            if n < LEVELS:
                dve.tensor_tensor(gqd[m % 2], gd, gq[:, :, a:a + P], ALU.mult)
                ins = dve.tensor_tensor(gkd[m % 2], gd, gk[:, :, a:a + P], ALU.mult)
            else:
                dve.tensor_copy(gqd[m % 2], gq[:, :, a:a + P])
                ins = dve.tensor_copy(gkd[m % 2], gk[:, :, a:a + P])
            ins.then_inc(S("gla_faded"), 1)
            if m:
                collect(dve, m - 1)
        collect(dve, len(gla_steps) - 1)

    def collect(dve, m):
        t, n = gla_steps[m]
        wait(dve, "gla_pair", m + 1)
        mask = con2_("gla_mask")[:, n * P:(n + 1) * P].rearrange("p (a i) -> p a i", a=1).broadcast_to([P, GLA_HEADS, P])
        src = ps[:, gla_bank(m), :].rearrange("p (h i) -> p h i", h=GLA_HEADS)
        if n == 0:
            dve.tensor_tensor(amat[t], src, mask, ALU.mult).then_inc(S("gla_kept"), 1)
            return
        ins = dve.tensor_tensor(atmp, src, mask, ALU.mult)
        chain(ins, dve)
        dve.tensor_tensor(amat[t], amat[t], atmp, ALU.add).then_inc(S("gla_kept"), 1)
        wait(dve, "gla_kept", m + 1)

    def act_gla_levels(act):
        for n in range(NT * LEVELS):
            wait(act, "gla_dist", n + 1)
            gd = gd2[n % 2]
            act.activation(gd, gd, ACT.Exp, scale=-1.0).then_inc(S("gla_fade"), 1)

    def pe_gla_levels(pe):
        wait(pe, "gla_abs", 1)
        for m in range(len(gla_steps)):
            wait(pe, "gla_faded", m + 1)
            wait(pe, "gla_kept", m - 1)
            for h in range(GLA_HEADS):
                mm = pe.matmul(ps[:, gla_bank(m), h * P:(h + 1) * P], gkd[m % 2][:, h, :], gqd[m % 2][:, h, :],
                               start=True, stop=True)
            mm.then_inc(S("gla_pair"), 1)

    def pe_gla_out(pe):
        wait(pe, "gla_dec", 1)
        for h in range(GLA_HEADS):
            pe.transpose(ps[0:META, 3, h * P:(h + 1) * P], kdec[0][:, h, :], ident)
        for h in range(GLA_HEADS):
            mm = pe.transpose(ps[:, 6, h * P:(h + 1) * P], kdec[1][:, h, :], ident)
        mm.then_inc(S("gla_turned"), 1)
        wait(pe, "gla_turned_copied", 1)
        wait(pe, "taken_act", gv_taken)
        wait(pe, "norm_inverted", 27)
        for n in range(2):
            rows = META if n == 0 else P
            src = 2 if n == 0 else 0
            for h in range(GLA_HEADS):
                bank = 3 if h < 2 else 7
                mm = pe.matmul(ps[:, bank, (h % 2) * 256:(h % 2 + 1) * 256], kdecT[n][0:rows, h, :],
                               gv[0:rows, src, h * 256:(h + 1) * 256], start=True, stop=True)
            mm.then_inc(S("gla_state"), 1)
            wait(pe, "gla_state_kept", n + 1)
        wait(pe, "gla_kept", len(gla_steps))
        for t in range(NT):
            for h in range(GLA_HEADS):
                for e in range(2):
                    x = h * 2 + e
                    bank = [[4, 5], [6, 3]][t][x // 4]
                    dst = ps[:, bank, (x % 4) * P:(x % 4 + 1) * P]
                    pe.matmul(dst, gv[:, t, h * 256 + e * P:h * 256 + (e + 1) * P], amat[t][:, h, :], start=True, stop=False)
                    mm = pe.matmul(dst, state[t][:, h, e * P:(e + 1) * P], qdec[:, h, t * P:(t + 1) * P], start=False, stop=True)
                    if x % 4 == 3:
                        mm.then_inc(S("gla_o"), 1)

    def dve_gla_state(dve):
        for n in range(2):
            wait(dve, "gla_state", n + 1)
            for h in range(GLA_HEADS):
                bank = 3 if h < 2 else 7
                src = ps[:, bank, (h % 2) * 256:(h % 2 + 1) * 256]
                if n == 0:
                    ins = dve.tensor_copy(state[0][:, h, :], src)
                else:
                    ins = dve.scalar_tensor_tensor(state[1][:, h, :], state[0][:, h, :], blast[:, 1, h:h + 1], src,
                                                   ALU.mult, ALU.add)
            ins.then_inc(S("gla_state_kept"), 1)
            wait(dve, "gla_state_kept", n + 1)

    def act_gla_out(act):
        wait(act, "gla_turned", 1)
        act.copy(kdecT[0][0:META, :, :], ps[0:META, 3, :].rearrange("p (h d) -> p h d", h=GLA_HEADS))
        act.copy(kdecT[1], ps[:, 6, :].rearrange("p (h d) -> p h d", h=GLA_HEADS)).then_inc(S("gla_turned_copied"), 1)
        for m in range(4):
            t, half = m // 2, m % 2
            bank = [[4, 5], [6, 3]][t][half]
            wait(act, "gla_o", m + 1)
            act.copy(o_gla[:, half * 4:half * 4 + 4, t * P:(t + 1) * P],
                     ps[:, bank, :].rearrange("p (x i) -> p x i", x=4)).then_inc(S("o_gla_ready"), 1)

    def passes(pe, out_ap, w, m, start, stop):
        pe.matmul(out_ap, w[0], m[0], start=start, stop=False)
        pe.matmul(out_ap, w[1], m[0], start=False, stop=False)
        return pe.matmul(out_ap, w[0], m[1], start=False, stop=stop)

    UB = 4
    N_IT = P // UB
    TOPK_IT = NT * HEADS
    MID_IT = 8
    MID_END = TOPK_IT + MID_IT

    def halves(b, table):
        return ((b - 1) * 2 + table) * P * 2

    def peer_pe_scores(pe, b):
        wait(pe, "taken_act", wq_taken[b]["act"])
        wait(pe, "taken_dve", wq_taken[b]["dve"])
        wait(pe, f"keys_loaded{b}", 16)
        for t in range(NT):
            for j in range(16):
                bank = (4 if t == 0 else 0) + j // 4
                mm = pe.matmul(ps[:, bank, (j % 4) * P:(j % 4 + 1) * P],
                               q_area[:, j * T + t * P:j * T + (t + 1) * P], keys_area[:, j, :], start=True, stop=True)
                if j % 4 == 3:
                    mm.then_inc(S("peer_scored"), 1)

    def peer_act_scores(act, b):
        for m in range(8):
            t, n = m // 4, m % 4
            wait(act, "peer_scored", (b - 1) * 8 + m + 1)
            act.copy(s_area[:, t * 2048 + n * 512:t * 2048 + (n + 1) * 512],
                     ps[:, (4 if t == 0 else 0) + n, :]).then_inc(S("peer_s_copied"), 1)

    def u_unit(kind, eng, b, i, s, extra=None, first=False):
        unit = units[f"u{b}"][0] + s
        h0 = halves(b, 0) + 2 * s
        if kind == "pe":
            eng.wait_ge(S("u_bank_free"), i * UB + ((b - 1) * P + 4 * (b - 1) + s + 1))
        if kind == "act":
            eng.wait_ge(S(ring_full[unit % RING]), i * 16 + 16 * (unit // RING + 1))
        for half in range(2):
            hslot = (h0 + half) % HLRING
            raw = slot(unit)[:, half * HALF:(half + 1) * HALF]
            if kind == "pe":
                eng.wait_ge(S("split_hi"), i * 2 * UB + (h0 + half + 1))
                eng.wait_ge(S("split_lo"), i * 2 * UB + (h0 + half + 1))
                for n in range(KD // 2):
                    k = half * KD // 2 + n
                    w = [hl[:, hslot, x, n * P:(n + 1) * P] for x in range(2)]
                    m = [hsplit[:, x, k, :] for x in range(2)]
                    mm = passes(eng, ps[:, s, 0:T], w, m, k == 0, k == KD - 1)
                mm.then_inc(S("split_used"), 1)
            if kind == "act":
                eng.wait_ge(S("split_used"), i * 2 * UB + (h0 + half + HLRING * b - HLRING + 1))
                eng.copy(hl[:, hslot, 0, :], raw).then_inc(S("split_hi"), 1)
            if kind == "dve":
                eng.wait_ge(S("split_hi"), i * 2 * UB + (h0 + half + 1))
                eng.tensor_tensor(hl[:, hslot, 1, :], raw, hl[:, hslot, 0, :].bitcast(F32), ALU.subtract)\
                   .then_inc(S("split_lo"), 1)
                if extra:
                    extra(i, 2 * s + half)
        if kind == "act" and not (first and s < 2):
            gelu(eng, b, i, s - 2)

    def u_loop(kind, eng, b, it0, it1, extra=None):
        with eng.Fori(it0, it1) as i:
            for s in range(UB):
                u_unit(kind, eng, b, i, s, extra)

    def load_gelu(act, b):
        act.activation(small[:, 15 + b:16 + b], v_("sink"), ACT.Gelu)

    def gelu(eng, b, i, s):
        eng.wait_ge(S("split_used"), i * 2 * UB + (halves(b, 0) + HLRING * b + 2 * s + 2))
        eng.activation(acts[:, ds(i * (UB * T) + s * T, T)], ps[:, s % UB, 0:T], ACT.Gelu)\
           .then_inc(S("u_bank_free"), 1)

    def topk_step(eng):
        def part(i, n):
            halves_of = [(x, keybuf[:, x * P:(x + 1) * P], tmpbuf[:, x * P:(x + 1) * P]) for x in range(2)]
            if n == 0:
                eng.tensor_copy(keybuf[:, :], s_area[:, ds(i * 256, 256)])
                eng.drain()
                for x, keys, _ in halves_of:
                    eng.max(topbuf[:, x, 0:8], keys)
            if n == 1:
                for x, keys, rest in halves_of:
                    eng.max_index(idxbuf[:, x, 0:8], topbuf[:, x, 0:8], keys)
                    eng.match_replace(rest, topbuf[:, x, 0:8], keys, NEG)
            if n == 2:
                for x, _, rest in halves_of:
                    eng.max(topbuf[:, x, 8:16], rest)
            if n == 3:
                for x, _, rest in halves_of:
                    eng.max_index(idxbuf[:, x, 8:16], topbuf[:, x, 8:16], rest)
            if n == 4:
                eng.tensor_copy(index_f[:, :, ds(i * 16, 16)], idxbuf[:, :, :])
                eng.tensor_tensor(keybuf[:, :].rearrange("p (a b) -> p a b", a=TOPK),
                                  topbuf[:, 0, :].rearrange("p (a o) -> p a o", o=1).broadcast_to([P, TOPK, TOPK]),
                                  topbuf[:, 1, :].rearrange("p (o b) -> p o b", o=1).broadcast_to([P, TOPK, TOPK]),
                                  ALU.add)
            if n == 5:
                eng.max(bestbuf[:, 0:8], keybuf[:, :])
                eng.drain()
                eng.match_replace(tmpbuf[:, :], bestbuf[:, 0:8], keybuf[:, :], NEG)
            if n == 6:
                eng.max(bestbuf[:, 8:16], tmpbuf[:, :])
                eng.max_index(posbuf[:, 0:8], bestbuf[:, 0:8], keybuf[:, :])
            if n == 7:
                eng.max_index(posbuf[:, 8:16], bestbuf[:, 8:16], tmpbuf[:, :])
                eng.tensor_copy(sum_best[:, ds(i * 16, 16)], bestbuf[:, :])
                eng.drain()
                eng.tensor_copy(sum_pos[:, ds(i * 16, 16)], posbuf[:, :])
            eng.drain()
        return part

    index_f = gate_f[:, :, :, :].rearrange("p x t r -> p x (t r)")

    LOOKUPS = 2 * NT * 2
    EXP_UNIT, SOFTMAX, LOOK = 1, 9, 2
    TURN = (LOOK + 2 * 3 * LOOKUPS) // 2 + 1
    TAKE = 2 * TURN + 4

    ROUND = 1.5 * 2.0 ** 23

    def dve_gate_part(dve, b, n):
        r1, r2 = rank1.rearrange("p t r -> p (t r)"), rank2.rearrange("p t r -> p (t r)")
        if n == 0:
            best = sum_best.rearrange("p (m k) -> p m k", k=TOPK)
            dve.tensor_tensor(chosen[:, 2, :].rearrange("p (m k) -> p m k", k=TOPK), best,
                              best[:, :, 0:1].broadcast_to([P, NT * HEADS, TOPK]), ALU.subtract).then_inc(S("gates_shifted"), 1)
            chain(dve.tensor_scalar(r1, sum_pos, 1.0 / TOPK, -15.0 / 32, ALU.mult, ALU.add), dve)
        if n == 1:
            chain(dve.tensor_scalar(r1, r1, ROUND, ROUND, ALU.add, ALU.subtract), dve)
            chain(dve.scalar_tensor_tensor(r2, r1, -float(TOPK), sum_pos, ALU.mult, ALU.add), dve)
        gates = chosen[:, 2, :].rearrange("p (m k) -> p m k", k=TOPK)
        if n == SOFTMAX:
            wait(dve, "gates_exp", b)
            chain(dve.tensor_reduce(gate_sum[:, 0, :], gates, AX_X, ALU.add), dve)
            chain(dve.reciprocal(gate_sum[:, 1, :], gate_sum[:, 0, :]), dve)
            z = gate_sum[:, 1, :].rearrange("p (m o) -> p m o", o=1).broadcast_to([P, NT * HEADS, TOPK])
            chain(dve.tensor_tensor(gates, gates, z, ALU.mult), dve)
        if LOOK <= n < LOOK + 6 * LOOKUPS and n % 2 == 0:
            c, step = (n - LOOK) // 6, (n - LOOK) // 2 % 3
            x, t, half = c // 4, c // 2 % 2, c % 2
            rows = slice(half * 64, half * 64 + 64)
            hit = lookup[:, c % 2, :]
            rank = (rank1, rank2)[x][:, t, rows].rearrange("p (r o) -> p r o", o=1).broadcast_to([P, 64, TOPK])
            if step == 0:
                every = iota[:, 0:TOPK].rearrange("p (o a) -> p o a", o=1).broadcast_to([P, 64, TOPK])
                ins = dve.tensor_tensor(hit.rearrange("p (r a) -> p r a", a=TOPK), rank, every, ALU.is_equal)
            if step == 1:
                keys = gate_f[:, x, t, rows].rearrange("p (h o a) -> p h o a", h=4, o=1).broadcast_to([P, 4, TOPK, TOPK])
                h4 = hit.rearrange("p (h k a) -> p h k a", h=4, k=TOPK)
                ins = dve.tensor_tensor(h4, h4, keys, ALU.mult)
            if step == 2:
                at = t * P + half * 64
                ins = dve.tensor_reduce(chosen[:, x, at:at + 64], hit.rearrange("p (r a) -> p r a", a=TOPK), AX_X, ALU.add)
            if c == LOOKUPS - 1 and step == 2:
                ins.then_inc(S("experts_chosen"), 1)
            else:
                chain(ins, dve)
        if n == TAKE:
            wait(dve, "experts_turned", b)
            dve.tensor_copy(sel[:, 0:2, :], ps[:, 4, :].rearrange("p (c t) -> p c t", c=2))
            dve.tensor_copy(sel[:, 2, :], ps[:, 5, 0:T])
        if n == TAKE + 1:
            dve.tensor_scalar(sel[:, 3, :], ps[:, 4, T:2 * T], -1.0, None, ALU.mult)
            dve.tensor_scalar(sel[:, 4, :], ps[:, 5, 0:T], -1.0, None, ALU.mult).then_inc(S("sel_taken"), 1)

    def pe_gate_part(pe, b, n):
        if n == TURN:
            wait(pe, "experts_chosen", b)
            for c in range(3):
                for t in range(NT):
                    m = c * NT + t
                    mm = pe.transpose(ps[:, 4 + m // 4, m % 4 * P:m % 4 * P + P], chosen[:, c, t * P:(t + 1) * P], ident)
            mm.then_inc(S("experts_turned"), 1)

    def act_gate_part(act, b, n):
        if n == EXP_UNIT:
            wait(act, "gates_shifted", b)
            act.activation(chosen[:, 2, :], chosen[:, 2, :], ACT.Exp).then_inc(S("gates_exp"), 1)

    NG = T // 8
    HOT_AHEAD = 2

    def base(b):
        return (b - 1) * (NG + GRING)

    def dve_hots(dve, b, g, slot_):
        dve.wait_ge(S("e_ready"), g + (base(b) + 1))
        dve.tensor_copy(stage[slot_], sel[:, :, ds(g * 8, 8)]).then_inc(S("staged"), 1)
        dve.wait_ge(S("staged"), g + ((b - 1) * NG + 1))
        for t in range(8):
            ins = dve.tensor_scalar(hot1[:, slot_, t, :], iota, stage[slot_][:, 0, t:t + 1], None, ALU.is_equal)
        for t in range(ACT_HOT, 8):
            ins = dve.tensor_scalar(hot2[:, slot_, t, :], iota, stage[slot_][:, 1, t:t + 1],
                                    stage[slot_][:, 2, t:t + 1], ALU.is_equal, ALU.mult)
        ins.then_inc(S("hots_dve"), 1)

    def act_hots(act, b, g, slot_):
        act.wait_ge(S("staged"), g + ((b - 1) * NG + 1))
        st, dist = stage[slot_], hot_dist[slot_ % 2]
        for t in range(ACT_HOT):
            ins = act.activation(dist[:, t, :], iota, ACT.Abs, bias=st[:, 3, t:t + 1])
        ins.then_inc(S("hot_dist_ready"), 1)
        act.wait_ge(S("hot_dist_ready"), g + ((b - 1) * NG + 1))
        for t in range(ACT_HOT):
            ins = act.activation(hot2[:, slot_, t, :], dist[:, t, :], ACT.Relu, bias=st[:, 2, t:t + 1], scale=st[:, 4, t:t + 1])
        ins.then_inc(S("hots_act"), 1)

    def e_banks(slot_):
        return ps[:, 2 * slot_:2 * slot_ + 2, :].rearrange("p s n -> p (s n)")

    def pe_gates(pe, b, g, slot_):
        pe.wait_ge(S("hots_dve"), g + ((b - 1) * NG + 1))
        pe.wait_ge(S("hots_act"), g + ((b - 1) * NG + 1))
        pe.wait_ge(S("gated"), g + (base(b) + 1))
        for t in range(8):
            mm = pe.matmul(e_banks(slot_)[:, t * P:(t + 1) * P], hot1[:, slot_, t, :], hot2[:, slot_, t, :],
                           start=True, stop=True)
        mm.then_inc(S("e_ready"), 1)

    def dve_multiply(dve, b, g, slot_):
        dve.wait_ge(S("e_ready"), g + (base(b) + GRING + 1))
        a8 = acts[:, :].rearrange("p (i t) -> p i t", t=T)[:, :, ds(g * 8, 8)]
        src = e_banks(slot_).rearrange("p (t i) -> p i t", t=8)
        dve.tensor_tensor(a8, a8, src, ALU.mult).then_inc(S("gated"), 1)

    def ds(a, n):
        return bass.ds(a, n) if not isinstance(a, int) else slice(a, a + n)

    def v_loop(kind, eng, b):
        v_first = units[f"v{b}"][0]

        def body(i, first, last):
            for s in range(UB):
                unit = v_first + s
                cslot = s % CRING
                h0 = halves(b, 1) + 2 * s
                c = ds(i * (UB * T) + s * T, T)
                if kind == "act":
                    eng.wait_ge(S(ring_full[unit % RING]), i * 16 + 16 * (unit // RING + 1))
                for half in range(2):
                    hslot = (h0 + half) % HLRING
                    part = slice(half * HALF, (half + 1) * HALF)
                    if kind == "act":
                        eng.wait_ge(S("split_used"), i * 2 * UB + (h0 + half + HLRING * b - HLRING + 1))
                        if half == 0:
                            eng.copy(csplit[:, cslot, 0, :], acts[:, c]).then_inc(S("csplit_hi"), 1)
                        eng.copy(hl[:, hslot, 0, :], slot(unit)[:, part]).then_inc(S("split_hi"), 1)
                    if kind == "dve":
                        if half == 0:
                            eng.wait_ge(S("csplit_hi"), i * UB + ((b - 1) * P + s + 1))
                            eng.tensor_tensor(csplit[:, cslot, 1, :], acts[:, c], csplit[:, cslot, 0, :].bitcast(F32),
                                              ALU.subtract)
                        eng.wait_ge(S("split_hi"), i * 2 * UB + (h0 + half + 1))
                        eng.tensor_tensor(hl[:, hslot, 1, :], slot(unit)[:, part], hl[:, hslot, 0, :].bitcast(F32),
                                          ALU.subtract).then_inc(S("split_lo"), 1)
                    if kind == "pe":
                        eng.wait_ge(S("split_hi"), i * 2 * UB + (h0 + half + 1))
                        eng.wait_ge(S("split_lo"), i * 2 * UB + (h0 + half + 1))
                        for n in range(KD // 2):
                            w = [hl[:, hslot, x, n * P:(n + 1) * P] for x in range(2)]
                            m = [csplit[:, cslot, x, :] for x in range(2)]
                            mm = passes(eng, ps[:, half * KD // 2 + n, 0:T], w, m, first and s == 0, last and s == UB - 1)
                        mm.then_inc(S("split_used"), 1)

        body(0, True, False)
        with eng.Fori(1, N_IT - 1) as i:
            body(i, False, False)
        body(N_IT - 1, False, True)

    def peer_pe(pe, b):
        pe_tiles(pe, group_of[f"wq{b}"])
        peer_pe_scores(pe, b)
        pe.wait_ge(S("peer_s_copied"), 8 * b)
        pe.drain().then_inc(S("split_used"), HLRING)
        pe.wait_ge(S("hsplit_ready"), b)
        u_loop("pe", pe, b, 0, TOPK_IT)
        for n in range(MID_IT * UB):
            u_unit("pe", pe, b, TOPK_IT + n // UB, n % UB)
            pe_gate_part(pe, b, n)
        u_loop("pe", pe, b, MID_END, N_IT)
        pe.wait_ge(S("u_bank_free"), b * (P + 4))
        pe.wait_ge(S("sel_taken"), b)
        pe.drain().then_inc(S("e_ready"), GRING)
        pe.drain().then_inc(S("gated"), GRING)
        with pe.Fori(0, NG // GRING) as i:
            for n in range(GRING):
                pe_gates(pe, b, i * GRING + n, n)
        pe.wait_ge(S("gated"), b * (NG + GRING))
        v_loop("pe", pe, b)

    def peer_act(act, b):
        take_tiles("act", act, group_of[f"wq{b}"])
        peer_act_scores(act, b)
        act.wait_ge(S("peer_scored"), 8 * b)
        act.copy(hsplit[:, 0, :, :], h_full).then_inc(S("hsplit_hi"), 1)
        act.wait_ge(S("peer_s_copied"), 8 * b)
        act.drain().then_inc(S("u_bank_free"), 4)
        load_gelu(act, b)
        for s in range(UB):
            u_unit("act", act, b, 0, s, first=True)
        u_loop("act", act, b, 1, TOPK_IT)
        for n in range(MID_IT * UB):
            u_unit("act", act, b, TOPK_IT + n // UB, n % UB)
            act_gate_part(act, b, n)
        u_loop("act", act, b, MID_END, N_IT)
        gelu(act, b, N_IT, -2)
        gelu(act, b, N_IT, -1)
        with act.Fori(0, NG // GRING) as i:
            for n in range(GRING):
                act_hots(act, b, i * GRING + n, n)
        act.wait_ge(S("gated"), b * (NG + GRING))
        v_loop("act", act, b)

    def peer_dve(dve, b):
        take_tiles("dve", dve, group_of[f"wq{b}"])
        dve.wait_ge(S("hsplit_hi"), b)
        dve.tensor_tensor(hsplit[:, 1, :, :], h_full, hsplit[:, 0, :, :].bitcast(F32), ALU.subtract)\
           .then_inc(S("hsplit_ready"), 1)
        dve.wait_ge(S("peer_s_copied"), 8 * b)
        u_loop("dve", dve, b, 0, TOPK_IT, topk_step(dve))
        dve.drain().then_inc(S("topk_done"), 1)
        for n in range(MID_IT * UB):
            u_unit("dve", dve, b, TOPK_IT + n // UB, n % UB, extra=lambda i, part: dve_gate_part(dve, b, 2 * n + part % 2))
        u_loop("dve", dve, b, MID_END, N_IT)
        for g in range(HOT_AHEAD):
            dve_hots(dve, b, g, g)
        with dve.Fori(0, NG // GRING - 1) as i:
            for n in range(GRING):
                dve_hots(dve, b, i * GRING + (n + HOT_AHEAD), (n + HOT_AHEAD) % GRING)
                dve_multiply(dve, b, i * GRING + n, n)
        for g in range(NG - GRING, NG):
            if g + HOT_AHEAD < NG:
                dve_hots(dve, b, g + HOT_AHEAD, (g + HOT_AHEAD) % GRING)
            dve_multiply(dve, b, g, g % GRING)
        dve.wait_ge(S("gated"), b * (NG + GRING))
        v_loop("dve", dve, b)
        dve.wait_ge(S("split_used"), halves(b + 1, 0) + HLRING * b)
        for k in range(KD):
            if b == 1:
                ins = dve.scalar_tensor_tensor(resid[:, k, :], ps[:, k, 0:T], mod[:, 40 + k, 0:1], resid[:, k, :],
                                               ALU.mult, ALU.add)
            else:
                ins = dve.tensor_tensor(resid[:, k, :], ps[:, k, 0:T], resid[:, k, :], ALU.add)
        ins.then_inc(S("peer_out"), 1)

    with nc.Block() as block:
        @block.sync
        def _(sp):
            peer_units = {u: n for n, u in enumerate(units["u1"] + units["v1"] + units["u2"] + units["v2"])}

            def load(u):
                sp.dma_start(slot(u), stream[u, :, :]).then_inc(S(arrival(u)[0]), 16)

            u = 0
            while u < n_units:
                old = u - RING
                if u in peer_units and old in peer_units:
                    end = u
                    while end < n_units and end in peer_units:
                        end += 1
                    rounds = (end - u) // RING
                    n0 = peer_units[old]
                    with sp.Fori(0, rounds) as i:
                        for s in range(RING):
                            sp.wait_ge(S("split_lo"), i * 2 * RING + 2 * (n0 + s + 1))
                            sp.dma_start(slot(u + s), stream[bass.ds(i * RING + (u + s), 1), :, :]
                                         .rearrange("a p n -> (a p) n")).then_inc(S(ring_full[(u + s) % RING]), 16)
                    u += rounds * RING
                    while u < end:
                        wait(sp, "split_lo", 2 * (peer_units[u - RING] + 1))
                        load(u)
                        u += 1
                    continue
                if old in peer_units:
                    wait(sp, "split_lo", 2 * (peer_units[old] + 1))
                elif old >= 0:
                    wait(sp, "tile_done", last_tile[old] + 1)
                load(u)
                u += 1
            sp.wait_ge(S("peer_out"), 2)
            sp.dma_start(out, resid[:, :, :]).then_inc(S("out_stored"), 16)
            sp.wait_ge(S("out_stored"), 16)

        @block.gpsimd
        def _(pool):
            pool.memset(ones, 1.0).then_inc(S("ones_ready"), 1)

        @block.scalar
        def _(act):
            act.dma_start(vec[:, :], vectors).then_inc(S("vec_loaded"), 16)
            act.dma_start(xin[:, :, 0:T], xT).then_inc(S("x_loaded"), 16)
            act.dma_start(xin[:, :, T:], ctxT).then_inc(S("x_loaded"), 16)
            act.dma_start(resid[:, :, :], xT).then_inc(S("consts_loaded"), 16)
            act.dma_start(con[:, :], common).then_inc(S("consts_loaded"), 16)
            act.dma_start(con1, consts1).then_inc(S("consts_loaded"), 16)
            wait(act, "vec_loaded", 16)
            cond = vec[:, vec_at["cond"][0]:vec_at["cond"][0] + 16].rearrange("p (k c) -> p k c", k=KD)
            act.activation(silu_c, cond, ACT.Silu).then_inc(S("silu_ready"), 1)
            norm_x.act(act)
            wait(act, "consts_loaded", 48)
            take_tiles("act", act, group_of["kvq1"])
            att1.act(act)
            take_tiles("act", act, group_of["out1"])
            norm_h2.act(act)
            act.dma_start(keys_area, keys1).then_inc(S("keys_loaded1"), 16)
            peer_act(act, 1)
            wait(act, "peer_out", 1)
            act.dma_start(con2, consts2).then_inc(S("consts2_loaded"), 16)
            act.dma_start(hin[:, :, T:TM], metaT).then_inc(S("meta_loaded"), 16)
            act.dma_start(wa2_b[0:16, :], w_a2).then_inc(S("wa2_loaded"), 16)
            norm_final.act(act)
            norm_n2.act(act)
            for g in ("cq", "ckv", "kpe"):
                take_tiles("act", act, group_of[g])
            norm_cq.act(act)
            norm_ckv.act(act)
            norm_kpe.act(act)
            take_tiles("act", act, group_of["uq"])
            norm_qn.act(act)
            norm_qpe.act(act)
            take_tiles("act", act, group_of["ukv_k"])
            norm_kn.act(act)
            take_tiles("act", act, group_of["ukv_v"])
            wait(act, "consts2_loaded", 16)
            att2.act(act)
            act_gla_decay(act)
            act_gla_levels(act)
            act_gla_out(act)
            norm_gla.act(act)
            norm_ffn.act(act)
            wait(act, "peer_in", 2)
            act.dma_start(keys_area, keys2).then_inc(S("keys_loaded2"), 16)
            peer_act(act, 2)

        @block.vector
        def _(dve):
            dve_eng[0] = dve
            wait(dve, "vec_loaded", 16)
            take_tiles("dve", dve, group_of["mod_a"])
            wait(dve, "taken_dve", 16)
            for c in range(2):
                ins = dve.scalar_tensor_tensor(scale1[:, :, c], mod[:, 8:16, c], 1.0, v_("norm1", 0, 8), ALU.add, ALU.mult)
            chain(ins, dve)
            norm_x.dve(dve)
            wait(dve, "consts_loaded", 48)
            rope_q1.dve(dve)
            dve.tensor_copy(k_rot[:, T:T + CTX], k_raw[:, T:T + CTX]).then_inc(S("rope1_ready"), 1)
            att1.dve(dve)
            take_tiles("dve", dve, group_of["out1"])
            chain(dve.scalar_tensor_tensor(scale2[:, :], mod[:, 32:40, 0], 1.0, v_("norm2", 0, 8), ALU.add, ALU.mult), dve)
            norm_h2.dve(dve)
            peer_dve(dve, 1)
            norm_final.dve(dve)
            wait(dve, "x1_ready", 1)
            chain(dve.tensor_copy(resid[:, :, :], hin[:, :, 0:T]), dve)
            norm_n2.dve(dve)
            norm_cq.dve(dve)
            norm_ckv.dve(dve)
            norm_kpe.dve(dve)
            norm_qn.dve(dve)
            norm_qpe.dve(dve)
            norm_kn.dve(dve)
            wait(dve, "consts2_loaded", 16)
            rope_q2.dve(dve)
            rope_k2.dve(dve)
            att2.dve(dve)
            dve_gla_decay(dve)
            dve_gla_levels(dve)
            dve_gla_state(dve)
            norm_gla.dve(dve)
            wait(dve, "og_normed", 1)
            wait(dve, "taken_act", gates2_taken)
            dve.tensor_tensor(og_n, og_n, silu_g, ALU.mult).then_inc(S("gla_ready"), 1)
            for g in ("wo_mla", "wo_gla", "w_out"):
                take_tiles("dve", dve, group_of[g])
            norm_ffn.dve(dve)
            peer_dve(dve, 2)

        @block.tensor
        def _(pe):
            pe_tiles(pe, group_of["mod_a"])
            norm_x.pe(pe)
            pe_tiles(pe, group_of["kvq1"])
            wait(pe, "consts_loaded", 48)
            rope_q1.pe(pe)
            wait(pe, "rope1_ready", 2)
            att1.pe(pe)
            pe_tiles(pe, group_of["out1"])
            norm_h2.pe(pe)
            peer_pe(pe, 1)
            norm_final.pe(pe)
            norm_n2.pe(pe)
            for g in ("cq", "ckv", "kpe"):
                pe_tiles(pe, group_of[g])
            norm_cq.pe(pe)
            norm_ckv.pe(pe)
            norm_kpe.pe(pe)
            pe_tiles(pe, group_of["uq"])
            norm_qn.pe(pe)
            norm_qpe.pe(pe)
            pe_tiles(pe, group_of["ukv_k"])
            norm_kn.pe(pe)
            pe_tiles(pe, group_of["ukv_v"])
            wait(pe, "consts2_loaded", 16)
            rope_q2.pe(pe)
            rope_k2.pe(pe)
            att2.pe(pe)
            pe_gla_decay(pe)
            pe_gla_levels(pe)
            pe_gla_out(pe)
            norm_gla.pe(pe)
            for g in ("wo_mla", "wo_gla", "w_out"):
                pe_tiles(pe, group_of[g])
            norm_ffn.pe(pe)
            peer_pe(pe, 2)


def kernel(**inputs):
    import concourse.bacc as bacc
    from concourse.bass_utils import run_bass_kernel_spmd

    a = {k: np.asarray(v) for k, v in inputs.items()}
    common, consts1, consts2 = shape_constants()
    keys1 = a["peer_sub_keys"][0].reshape(16, P, P).transpose(2, 0, 1)
    keys2 = np.tile(a["peer_keys_2"][0].transpose(2, 0, 1)[:, None], (1, HEADS, 1, 1)).reshape(P, 16, P)
    arrays = {
        "stream": pack_stream(a), "xT": feature_major(a["x"][0]), "ctxT": feature_major(a["ctx"][0]),
        "metaT": feature_major(a["meta_2"]), "vectors": pack_vectors(a), "common": common,
        "consts1": consts1, "consts2": consts2, "keys1": keys1, "keys2": keys2, "w_a2": a["gla_w_a2_2"][0],
    }
    arrays = {k: np.ascontiguousarray(v) for k, v in arrays.items()}
    nc = bacc.Bacc("TRN2", target_bir_lowering=False, num_devices=1, dynamic_dma_scratch_size=1024)
    args = [nc.dram_tensor(k, v.shape, F32, kind="ExternalInput").ap() for k, v in arrays.items()]
    out = nc.dram_tensor("out", (P, KD, T), F32, kind="ExternalOutput").ap()
    build(nc, *args, out)
    result = run_bass_kernel_spmd(nc, [arrays], core_ids=[0]).results[0]["out"]
    return np.ascontiguousarray(np.asarray(result).transpose(2, 1, 0).reshape(1, T, D))
```

```python
import math

import numpy as np

import concourse.bass as bass
from concourse import mybir

F32 = mybir.dt.float32
F32R = mybir.dt.float32r
U32 = mybir.dt.uint32
ALU = mybir.AluOpType
ACT = mybir.ActivationFunctionType
AX_X = mybir.AxisListType.X

P = 128
D = 1024
KD = D // P
T = 256
NT = T // P
CTX = 256
META = 16
TM = T + META
EPS = 1e-6
NEG = -1.0e30
HEAD = 64
GROUP = 4
WINDOW = 128
HEADS = 8
TOPK = 16
TAU = 16.0
GLA_HEADS = 4
LEVELS = 7
RING = 4
UNIT = KD * P
HALF = UNIT // 2
HLRING = 4
CRING = 4
GRING = 4
ACT_HOT = 4
NPROJ = 3
B_STAT = (3, 7)
B_SCORE = (4, 5)
B_PT = 6
B_OUT = 7



def stream_order():
    order = [("mod_row", 16), ("in_kvq", 6)]
    mods, fills = 32, 28
    plan = [("fill1", 1)] * fills
    out = []
    for i, p in enumerate(plan):
        out.append(p)
        out += [("mod", 1)] * ((mods * (i + 1)) // fills - (mods * i) // fills)
    order += out
    order += [("attn_out", 4), ("conv_out", 4), ("mix_out", 8), ("wq1", 16), ("u1", 128), ("v1", 128),
              ("cq", 3), ("ckv", 2), ("kpe", 1), ("gq", 4), ("gk", 4), ("ga", 1),
              ("uq", 6), ("ukv_k", 2), ("ukv_v", 2), ("gv", 8), ("gg", 8), ("gate_a", 8), ("gate_b", 8),
              ("wo_mla", 8), ("wo_gla", 8), ("w_out", 8), ("wq2", 16), ("u2", 128), ("v2", 128)]
    return order


def unit_table():
    at, n = {}, 0
    for key, count in stream_order():
        at.setdefault(key, []).extend(range(n, n + count))
        n += count
    return at, n


def pack_stream(a):
    def std(w):
        n = w.shape[1] // P
        return w.reshape(KD, P, n, P).transpose(2, 1, 0, 3).reshape(n, P, UNIT)

    def short(w, per):
        k, n = w.shape[0] // P, w.shape[1] // P
        u = w.reshape(k, P, n // per, per, P).transpose(2, 1, 3, 0, 4).reshape(n // per, P, per * k * P)
        return np.concatenate([u, np.zeros((n // per, P, UNIT - per * k * P), np.float32)], axis=2)

    w_in = a["w_in"][0]
    q = w_in[:, :512].reshape(D, 2, GROUP, HEAD).transpose(0, 2, 1, 3).reshape(D, 512)
    k, v = w_in[:, 512:640], w_in[:, 640:768]
    gb, gc, u = w_in[:, 768:1280], w_in[:, 1280:1792], w_in[:, 1792:2304]
    ga, gv = w_in[:, 2304:3328], w_in[:, 3328:4352]
    attn_out = a["w_attn_out"][0].reshape(2, GROUP, HEAD, D).transpose(1, 0, 2, 3).reshape(512, D)
    w2 = a["w_in_2"][0]
    c = np.cumsum([0, 384, 256, 64, 512, 512, 1024, 16, 1024, 1024, 1024])
    part = lambda i: w2[:, c[i]:c[i + 1]]
    uq = a["mla_w_uq_2"][0].reshape(384, 8, 192)
    uq = np.concatenate([uq[:, :, :128].reshape(384, 1024), uq[:, :, 128:].reshape(384, 512)], axis=1)
    ukv = a["mla_w_ukv_2"][0].reshape(256, 8, 256)
    ukv_v = ukv[:, :, 128:].reshape(2, P, 2, 512).transpose(2, 1, 0, 3).reshape(2, P, UNIT)

    def peer_u(t):
        return t.reshape(P, P, KD, P).transpose(1, 3, 2, 0).reshape(P, P, UNIT)

    def peer_v(t):
        return t.reshape(P, P, D).transpose(1, 0, 2)

    parts = {
        "mod_row": a["w_mod"][0][:, :2048].reshape(4, 2, P, 4, 512).transpose(3, 0, 2, 1, 4).reshape(16, P, UNIT),
        "mod": std(a["w_mod"][0][:, 2048:]), "in_kvq": std(np.concatenate([k, v, q], axis=1)),
        "fill1": std(np.concatenate([gc, u, gb, ga, gv], axis=1)),
        "attn_out": short(attn_out, 2), "conv_out": short(a["w_conv_out"][0], 2),
        "mix_out": std(a["w_mix_out"][0]), "wq1": std(a["peer_w_q"][0]),
        "u1": peer_u(a["peer_u"][0]), "v1": peer_v(a["peer_v"][0]),
        "cq": std(part(0)), "ckv": std(part(1)), "kpe": std(np.concatenate([part(2), part(2)], axis=1)),
        "uq": short(uq, 2), "ukv_k": short(ukv[:, :, :128].reshape(256, 1024), 4), "ukv_v": ukv_v,
        "gq": std(part(3)), "gk": std(part(4)), "gv": std(part(5)),
        "ga": std(np.concatenate([part(6), np.zeros((D, P - 16), np.float32)], axis=1)),
        "gg": std(part(7)), "gate_a": std(part(8)), "gate_b": std(part(9)),
        "wo_mla": std(a["w_o_mla_2"][0]), "wo_gla": std(a["w_o_gla_2"][0]), "w_out": std(a["w_out_2"][0]),
        "wq2": std(a["peer_w_q_2"][0]), "u2": peer_u(a["peer_u_2"][0]), "v2": peer_v(a["peer_v_2"][0]),
    }
    at, n = unit_table()
    out = np.empty((n, P, UNIT), np.float32)
    for key, where in at.items():
        assert len(where) == len(parts[key]), (key, len(where), len(parts[key]))
        out[where] = parts[key]
    return out



VECS = [("b_mod", 48), ("norm1", 8), ("norm2", 8), ("final", 8), ("norm_mix", 8), ("q_norm", 3), ("kv_norm", 2),
        ("qn_nope", 1), ("qn_pe", 1), ("kn_nope", 1), ("kn_pe", 1), ("b_a", 4), ("gla_norm", 2), ("norm_ffn", 8),
        ("conv_w", 12), ("sink", 8), ("cond", 16)]
CONSTS = [("ident", 128), ("blk64", 128), ("iota", 128)]
CONSTS1 = [("rot", 128), ("cos", 256), ("sin", 256), ("mask", 1024)]
CONSTS2 = [("rot", 128), ("cos", 272), ("sin", 272), ("mask", 544), ("gla_mask", 128 * (LEVELS + 1))]


def offsets(table):
    at, n = {}, 0
    for key, size in table:
        at[key] = (n, size)
        n += size
    return at, n


def pack_vectors(a):
    col = lambda v: v.reshape(-1, P).T
    twice = lambda v: np.concatenate([v, v]).reshape(P, 1)
    parts = {
        "b_mod": col(a["b_mod"][0]), "norm1": col(a["norm1_g"][0]), "norm2": col(a["norm2_g"][0]),
        "final": col(a["final_g"]), "norm_mix": col(a["norm_mix_2"][0]), "q_norm": col(a["mla_q_norm_2"][0]),
        "kv_norm": col(a["mla_kv_norm_2"][0]), "qn_nope": col(a["qn_nope_2"][0]), "qn_pe": twice(a["qn_pe_2"][0]),
        "kn_nope": col(a["kn_nope_2"][0]), "kn_pe": twice(a["kn_pe_2"][0]), "b_a": col(a["gla_b_a_2"][0]),
        "gla_norm": col(a["gla_norm_2"][0]), "norm_ffn": col(a["norm_ffn_2"][0]),
        "conv_w": a["conv_w"][0].reshape(12, P).T, "sink": np.tile(a["attn_sink"][0], (P, 1)),
        "cond": np.stack([col(a["c"][0]), col(a["c_ctx"])], axis=2).reshape(P, 16),
    }
    return np.ascontiguousarray(np.concatenate([parts[k] for k, _ in VECS], axis=1))


def rotation(half):
    r = np.zeros((P, P), np.float32)
    for i in range(P):
        first = i % (2 * half) < half
        r[i, i + half if first else i - half] = -1.0 if first else 1.0
    return r.T


def shape_constants():
    i = np.arange(P)
    f32 = np.float32
    common = {
        "ident": np.eye(P), "blk64": i[:, None] // 64 == i[None, :] // 64,
        "iota": np.tile(np.arange(P), (P, 1)),
    }
    pos = np.arange(T)
    freq = (f32(10000.0) ** (-(np.arange(16, dtype=f32)) / f32(16))).astype(f32)
    place = np.where((i % HEAD < 32)[:, None], pos[None, :] // 64, pos[None, :] % 64).astype(f32)
    angle = (place * freq[i % 16][:, None]).astype(f32)
    mask = np.zeros((NT, P, 512))
    for t in range(NT):
        far = np.abs(t * P + i[:, None] - np.arange(T)[None, :]) > WINDOW
        mask[t, :, :T] = np.where(far, NEG, 0.0)
    first = {"rot": rotation(16), "cos": np.cos(angle), "sin": np.sin(angle),
             "mask": mask.transpose(1, 0, 2).reshape(P, -1)}
    where = np.concatenate([np.arange(META, TM), np.arange(META)]).astype(f32)
    freq = (f32(10000.0) ** (-(np.arange(32, dtype=f32)) / f32(32))).astype(f32)
    angle = (where[None, :] * freq[i % 32][:, None]).astype(f32)
    mask = np.zeros((NT, P, TM))
    for t in range(NT):
        later = np.arange(T)[None, :] // 64 > (t * P + i[:, None]) // 64
        mask[t, :, :T] = np.where(later, NEG, 0.0)
    levels = np.zeros((LEVELS + 1, P, P))
    for n in range(LEVELS):
        size = 1 << n
        j, q = i[:, None] // size, i[None, :] // size
        levels[n] = (j % 2 == 0) & (q == j + 1)
    levels[LEVELS] = np.eye(P)
    second = {"rot": rotation(32), "cos": np.cos(angle), "sin": np.sin(angle),
              "mask": mask.transpose(1, 0, 2).reshape(P, -1), "gla_mask": levels.transpose(1, 0, 2).reshape(P, -1)}
    join = lambda parts, table: np.ascontiguousarray(
        np.concatenate([np.asarray(parts[k], np.float32).reshape(P, n) for k, n in table], axis=1))
    return join(common, CONSTS), join(first, CONSTS1), join(second, CONSTS2)


def feature_major(x):
    return np.ascontiguousarray(x.T.reshape(-1, P, x.shape[0]).transpose(1, 0, 2))



class Tile:

    def __init__(self, unit, ready, pairs, rows, cols, engine, take):
        self.unit, self.ready, self.pairs, self.rows, self.cols = unit, ready, pairs, rows, cols
        self.engine, self.take = engine, take
        self.start, self.stop = True, True


def build(nc, stream, xT, ctxT, metaT, vectors, common, consts1, consts2, keys1, keys2, w_a2, out):
    units, n_units = unit_table()

    top = [(nc.sbuf_base + 31) // 32 * 8]

    def place(name, shape, dtype=F32, at=None):
        size = math.prod(shape[1:])
        where = top[0] if at is None else at
        t = nc.alloc_sbuf_tensor_at(name, shape, dtype, offset=4 * where)
        if at is None:
            top[0] += (size + 7) // 8 * 8
        return t, where

    ring, _ = place("ring", [P, RING, UNIT])
    resid, _ = place("resid", [P, KD, T])
    s_area, _ = place("s_area", [P, NT * HEADS * 2 * P])
    arena, _ = place("arena", [P, P * T])
    gbuf, gbuf_at = place("gbuf", [P, 10240])
    hl, _ = place("hl", [P, HLRING, 2, HALF], F32R, at=gbuf_at)
    hsplit, _ = place("hsplit", [P, 2, KD, T], F32R, at=gbuf_at + 2 * HLRING * HALF)
    csplit, _ = place("csplit", [P, CRING, 2, T], F32R, at=gbuf_at + 2 * HLRING * HALF + 2 * KD * T)
    vec_at, n_vec = offsets(VECS)
    con_at, n_con = offsets(CONSTS)
    vec, _ = place("vec", [P, n_vec])
    con, _ = place("con", [P, n_con])
    mod, _ = place("mod", [P, 48, 2])
    scale1, _ = place("scale1", [P, KD, 2])
    scale2, _ = place("scale2", [P, KD])
    small, _ = place("small", [P, 32])
    half_gate, _ = place("half_gate", [P, KD])
    gate_f, _ = place("gate_f", [P, 2, 2, P])
    onesbuf, _ = place("onesbuf", [P, P])
    topbuf, _ = place("topbuf", [P, 2, TOPK])
    idxbuf, _ = place("idxbuf", [P, 2, TOPK], U32)
    keybuf, _ = place("keybuf", [P, 2 * P])
    tmpbuf, _ = place("tmpbuf", [P, 2 * P])
    bestbuf, _ = place("bestbuf", [P, TOPK])
    posbuf, _ = place("posbuf", [P, TOPK], U32)
    assert top[0] * 4 <= nc.sbuf_usable_end, (top[0] * 4, nc.sbuf_usable_end)

    def v_(name, i=0, n=1):
        a = vec_at[name][0] + i
        return vec[:, a:a + n]

    def c_(name):
        a, n = con_at[name]
        return con[:, a:a + n]

    ident, blk64, iota, ones = c_("ident"), c_("blk64"), c_("iota"), onesbuf[:, :]

    class Space:

        def __init__(self, tensor, size):
            self.t, self.n, self.at = tensor, size, 0

        def take(self, *shape):
            n = math.prod(shape)
            a = self.at
            self.at += n
            assert self.at <= self.n, (self.at, self.n)
            ap = self.t[:, a:a + n]
            if len(shape) == 2:
                ap = ap.rearrange("p (a b) -> p a b", a=shape[0])
            if len(shape) == 3:
                ap = ap.rearrange("p (a b c) -> p a b c", a=shape[0], b=shape[1])
            return ap

    ps = nc.alloc_psum_tensor("ps", [P, 8, 512], F32)

    sems = {}

    def S(name):
        if name not in sems:
            sems[name] = nc.alloc_semaphore(name)
        return sems[name]

    def wait(eng, name, value):
        if value > 0:
            eng.wait_ge(S(name), value)

    ring_full = [f"ring_full{s}" for s in range(RING)]

    def arrival(unit):
        return ring_full[unit % RING], 16 * (unit // RING + 1)

    def slot(unit):
        return ring[:, unit % RING, :]

    A1 = Space(arena, P * T)
    xin = A1.take(KD, T + CTX)
    sq1 = A1.take(KD, T + CTX)
    h1 = A1.take(KD, T + CTX)
    q_raw, q_rot = A1.take(4, T), A1.take(4, T)
    k_raw, k_rot = A1.take(T + CTX), A1.take(T + CTX)
    rope_tmp = A1.take(TM)
    v_tok = A1.take(4, P)
    gc_b, z_b, conv_b, cg_b = A1.take(4, T), A1.take(4, T), A1.take(4, T), A1.take(4, T)
    sga, sgv, mixed = A1.take(KD, T), A1.take(KD, T), A1.take(KD, T)
    attn1 = A1.take(4, T)
    mod_row = A1.take(2048)
    mod_prod, mod_acc = A1.take(2, UNIT), A1.take(4, P)
    G1 = Space(gbuf, 10240)
    con1_at, n_con1 = offsets(CONSTS1)
    con1 = G1.take(n_con1)
    probs1, pt1 = G1.take(2, 512), G1.take(2, 512)
    rs1 = G1.take(2, 512)
    cprod = G1.take(2, T)
    silu_c = G1.take(KD, 2)

    A2 = Space(arena, P * T)
    starts2 = {}

    def arena_at(name):
        return starts2[name]

    def named(name, *shape):
        starts2[name] = A2.at
        return A2.take(*shape)
    hin, n2, sq2 = named("hin", KD, TM), A2.take(KD, TM), A2.take(KD, TM)
    cq_b, cqn, ckv_b, ckvn = named("cq", 3, T), A2.take(3, T), A2.take(2, TM), A2.take(2, TM)
    kpe_raw, kpe_n, kpe_rot = A2.take(TM), A2.take(TM), A2.take(TM)
    qnope, qnope_n = named("qnope", HEADS, T), named("qnope_n", HEADS, T)
    qpe, qpe_rot = named("qpe", 4, T), A2.take(4, T)
    knope, knope_n = named("knope", HEADS, TM), A2.take(HEADS, TM)
    v2_flat = A2.take(3 * D)
    v2 = v2_flat.rearrange("p (a d) -> p a d", a=3)
    attn2 = A2.take(HEADS, T)
    G2 = Space(gbuf, 10240)
    con2_at, n_con2 = offsets(CONSTS2)
    con2 = G2.take(n_con2)
    probs2, pt2 = G2.take(2, TM), G2.take(2, 3 * P)
    rs2 = G2.take(2, TM)
    ga_b, wa2_b = G2.take(TM), G2.take(512)
    la, lb = G2.take(GLA_HEADS, TM), G2.take(GLA_HEADS, TM)
    silu_g = G2.take(KD, T)
    SA = Space(s_area, NT * HEADS * 2 * P)
    sgate_a, sgate_b = SA.take(KD, T), SA.take(KD, T)
    gq, gk = A2.take(GLA_HEADS, T), A2.take(GLA_HEADS, TM)
    gv = A2.take(3, D)
    assert hin.shape[1] * TM >= 4 * GLA_HEADS * P and P == T // 2

    def over(first, *sizes):
        at = arena_at(first)
        out = []
        for shape in sizes:
            n = math.prod(shape)
            out.append(arena[:, at:at + n].rearrange("p (a b) -> p a b", a=shape[0]))
            at += n
        return out
    gd2_0, gd2_1, gqd_0, gqd_1 = over("hin", *[(GLA_HEADS, P)] * 4)
    gkd_0, gkd_1, amat_0, amat_1 = over("qnope", *[(GLA_HEADS, P)] * 4)
    gd2, gqd, gkd, amat = [gd2_0, gd2_1], [gqd_0, gqd_1], [gkd_0, gkd_1], [amat_0, amat_1]
    qdec, kdec_0, kdec_1, atmp, blast = over("cq", (GLA_HEADS, T), (GLA_HEADS, META), (GLA_HEADS, P), (GLA_HEADS, P),
                                             (2, GLA_HEADS))
    kdec = [kdec_0, kdec_1]
    kdecT = over("qpe", (GLA_HEADS, P), (GLA_HEADS, P))
    state = over("qnope_n", (GLA_HEADS, 256), (GLA_HEADS, 256))
    o_gla, og_n = over("knope", (KD, T), (KD, T))
    mixed2 = v2_flat[:, 0:KD * T].rearrange("p (k t) -> p k t", k=KD)

    def con1_(name):
        a, n = con1_at[name]
        return con1[:, a:a + n]

    def con2_(name):
        a, n = con2_at[name]
        return con2[:, a:a + n]

    q_area = arena[:, P * T - 16 * T:]
    keys_area = arena[:, P * T - 16 * T - 16 * P:P * T - 16 * T].rearrange("p (j n) -> p j n", j=16)
    acts = arena
    K = Space(gbuf, 10240)
    K.take(8192)
    sum_pos, sum_best = K.take(NT * P), K.take(NT * P)
    rank1, rank2 = K.take(NT, P), K.take(NT, P)
    chosen = K.take(3, NT * P)
    gate_sum = K.take(2, NT * HEADS)
    lookup = s_area[:, 0:2048].rearrange("p (c n) -> p c n", c=2)
    KINDS = 5
    sel = s_area[:, 2048:2048 + KINDS * T].rearrange("p (c t) -> p c t", c=KINDS)
    hot1 = gbuf[:, 0:GRING * 8 * P].rearrange("p (r t i) -> p r t i", r=GRING, t=8)
    hot2 = gbuf[:, GRING * 8 * P:2 * GRING * 8 * P].rearrange("p (r t i) -> p r t i", r=GRING, t=8)
    H = Space(gbuf, 10240)
    H.take(8192)
    stage = [H.take(KINDS, 8) for _ in range(GRING)]
    hot_dist = [H.take(ACT_HOT, P) for _ in range(2)]

    tiles = []
    taken = {"act": 0, "dve": 0}
    group_of = {}

    def tile(group, unit, ready, pairs, rows, cols, engine, take):
        t = Tile(unit, ready, pairs, rows, cols, engine, take)
        if engine:
            taken[engine] += 1
        t.n, t.seq, t.bank = len(tiles), taken.get(engine, 0), len(tiles) % NPROJ
        tiles.append(t)
        group_of.setdefault(group, []).append(t.n)

    def std_pairs(unit, rhs, k=KD, at=0):
        return [(slot(unit)[:, at + i * P:at + (i + 1) * P], rhs[:, i]) for i in range(k)]

    def take_copy(dst):
        def f(kind, eng, src):
            return eng.copy(dst, src) if kind == "act" else eng.tensor_copy(dst, src)
        return f

    def take_func(dst, func):
        def f(kind, eng, src):
            return eng.activation(dst, src, func)
        return f

    def take_gate(dst):
        def f(kind, eng, src):
            return eng.activation(dst, src, ACT.Tanh, scale=0.5)
        return f

    def take_times(dst, other, scalar=None):
        def f(kind, eng, src):
            if scalar is None:
                return eng.tensor_tensor(dst, src, other, ALU.mult)
            return eng.scalar_tensor_tensor(dst, src, scalar, other, ALU.mult, ALU.mult)
        return f

    MOD_BANKS = (4, 5, 6, 7)
    for i, u in enumerate(units["mod_row"]):
        group, pair = i // 4, i % 4
        pairs = [(silu_c[:, 2 * pair + j, :], slot(u)[:, j * 512:(j + 1) * 512]) for j in range(2)]
        tile("mod_a", u, ("silu_ready", 1), pairs, 2, 512, None, None)
        tiles[-1].bank, tiles[-1].start, tiles[-1].stop = MOD_BANKS[group], pair == 0, pair == 3

    mod_units = units["mod"]
    mod_prepared = {}

    def mod_tile(group, n):
        j = n - 16
        u = mod_units[j]
        tile(group, u, ("mod_weighed", j + 1), [(mod_acc[:, j % 4, :], ones[:, 0:1])], P, 1, "dve",
             lambda kind, eng, src: eng.tensor_scalar(mod[:, n, 0:1], src, v_("b_mod", n), None, ALU.add))
        mod_prepared[len(tiles) - 1] = j

    def weigh_mod(kind, eng, n):
        j = mod_prepared[n]
        u = mod_units[j]
        if kind == "act":
            eng.wait_ge(S(arrival(u)[0]), arrival(u)[1])
            wait(eng, "mod_weighed", j - 1)
            for k in range(KD):
                ins = eng.activation(mod_prod[:, j % 2, k * P:(k + 1) * P], slot(u)[:, k * P:(k + 1) * P], ACT.Copy,
                                     scale=silu_c[:, k, 0:1])
            ins.then_inc(S("mod_products"), 1)
            return
        eng.wait_ge(S("mod_products"), j + 1)
        if j >= 4:
            old = [m for m in mod_prepared if mod_prepared[m] == j - 4][0]
            eng.wait_ge(S("tile_done"), old + 1)
        eng.tensor_reduce(mod_acc[:, j % 4, :], mod_prod[:, j % 2, :].rearrange("p (k m) -> p m k", k=KD),
                          AX_X, ALU.add).then_inc(S("mod_weighed"), 1)

    u0 = units["in_kvq"]
    tile("kvq1", u0[0], ("h1_ready", 2), std_pairs(u0[0], h1), P, T + CTX, "act", take_copy(k_raw))

    def v_pairs(u, src, t, n):
        return [(src[:, k, t:t + n], slot(u)[:, k * P:(k + 1) * P]) for k in range(KD)]

    for t in range(4):
        tile("kvq1", u0[1], ("h1_ready", 2), v_pairs(u0[1], h1, t * P, P), P, P, "act", take_copy(v_tok[:, t, :]))
    for j in range(4):
        tile("kvq1", u0[2 + j], ("h1_ready", 2), std_pairs(u0[2 + j], h1[:, :, 0:T]), P, T, "act",
             take_copy(q_raw[:, j, :]))
    kv1_taken = taken["act"]

    next_mod = 16
    f1 = units["fill1"]

    def conv_take(i):
        def f(kind, eng, src):
            chain(eng.tensor_tensor(z_b[:, i, :], src, gc_b[:, i, :], ALU.mult), eng)
            w = lambda tap: v_("conv_w", tap * 4 + i)
            chain(eng.tensor_scalar(conv_b[:, i, :], z_b[:, i, :], w(1), None, ALU.mult), eng)
            chain(eng.scalar_tensor_tensor(conv_b[:, i, 1:T], z_b[:, i, 0:T - 1], w(0), conv_b[:, i, 1:T],
                                           ALU.mult, ALU.add), eng)
            return eng.scalar_tensor_tensor(conv_b[:, i, 0:T - 1], z_b[:, i, 1:T], w(2), conv_b[:, i, 0:T - 1],
                                            ALU.mult, ALU.add)
        return f

    for i in range(28):
        u = f1[i]
        pairs = std_pairs(u, h1[:, :, 0:T])
        if i < 4:
            tile("fill1", u, None, pairs, P, T, "dve", take_copy(gc_b[:, i, :]))
        elif i < 8:
            tile("fill1", u, None, pairs, P, T, "dve", conv_take(i - 4))
        elif i < 12:
            tile("fill1", u, None, pairs, P, T, "dve", take_times(cg_b[:, i - 8, :], conv_b[:, i - 8, :]))
        elif i < 20:
            tile("fill1", u, None, pairs, P, T, "act", take_gate(sga[:, i - 12, :]))
        else:
            tile("fill1", u, None, pairs, P, T, "act", take_gate(sgv[:, i - 20, :]))
        while next_mod < 48 and (i == 27 or mod_units[next_mod - 16] < f1[i + 1]):
            mod_tile("fill1", next_mod)
            next_mod += 1
    assert next_mod == 48

    sig1_taken = taken["act"]

    def ao_take(n):
        def f(kind, eng, src):
            if n == 0:
                eng.wait_ge(S("taken_act"), sig1_taken)
            return eng.scalar_tensor_tensor(mixed[:, n, :], sga[:, n, :], 1.0, src, ALU.add, ALU.mult)
        return f

    def add_take(dst, gate, tmp):
        def f(kind, eng, src):
            chain(eng.scalar_tensor_tensor(tmp, gate, 1.0, src, ALU.add, ALU.mult), eng)
            return eng.tensor_tensor(dst, dst, tmp, ALU.add)
        return f

    for i, u in enumerate(units["attn_out"]):
        for s in range(2):
            tile("out1", u, ("attn_out_ready", 4), std_pairs(u, attn1, 4, at=s * 4 * P), P, T, "dve", ao_take(2 * i + s))
    for i, u in enumerate(units["conv_out"]):
        for s in range(2):
            n = 2 * i + s
            tile("out1", u, ("taken_dve", "conv"), std_pairs(u, cg_b, 4, at=s * 4 * P), P, T, "dve",
                 add_take(mixed[:, n, :], sgv[:, n, :], cprod[:, n % 2, :]))
    mixed_taken = taken["dve"]

    def resid_take(n, scalar):
        def f(kind, eng, src):
            dst = resid[:, n, :]
            if scalar is None:
                return eng.scalar_tensor_tensor(dst, src, 0.5, dst, ALU.mult, ALU.add)
            return eng.scalar_tensor_tensor(dst, src, scalar(n), dst, ALU.mult, ALU.add)
        return f

    for n, u in enumerate(units["mix_out"]):
        tile("out1", u, ("taken_dve", mixed_taken), std_pairs(u, mixed), P, T, "dve",
             resid_take(n, lambda n: half_gate[:, n:n + 1]))

    h_full = gbuf[:, 8192:10240].rearrange("p (k t) -> p k t", k=KD)

    def group2(key, dst, ready, rhs, n, engine="act", k=KD, per=1, make=take_copy, width=None):
        for i, u in enumerate(units[key]):
            for s in range(per):
                m = i * per + s
                tile(key, u, ready, std_pairs(u, rhs, k, at=s * k * P), P, n, engine, make(dst[:, m, :]))

    nT = n2[:, :, 0:T]
    group2("cq", cq_b, ("n2_ready", 1), nT, T)
    group2("ckv", ckv_b, ("n2_ready", 1), n2, TM)
    tile("kpe", units["kpe"][0], ("n2_ready", 1), std_pairs(units["kpe"][0], n2), P, TM, "act", take_copy(kpe_raw))
    c_taken = taken["act"]
    def gq_take(dst):
        return lambda kind, eng, src: eng.activation(dst, src, ACT.Copy, scale=float(P) ** -0.5)
    group2("gq", gq, None, nT, T, make=gq_take)
    group2("gk", gk, None, n2, TM)
    tile("ga", units["ga"][0], None, std_pairs(units["ga"][0], n2), P, TM, "act", take_copy(ga_b))
    ga_taken = taken["act"]
    for i, u in enumerate(units["uq"]):
        for s in range(2):
            m = 2 * i + s
            dst = qnope[:, m, :] if m < HEADS else qpe[:, m - HEADS, :]
            tile("uq", u, ("cq_ready", 1), std_pairs(u, cqn, 3, at=s * 3 * P), P, T, "act", take_copy(dst))
    uq_taken = taken["act"]
    group2("ukv_k", knope, ("ckv_ready", 1), ckvn, TM, k=2, per=4)
    uk_taken = taken["act"]
    KT2 = [(0, P), (P, P), (T, META)]
    for half, u in enumerate(units["ukv_v"]):
        for t, (a, n) in enumerate(KT2):
            pairs = [(ckvn[:, k, a:a + n], slot(u)[:, k * 512:(k + 1) * 512]) for k in range(2)]
            tile("ukv_v", u, None, pairs, n, 512, "act", take_copy(v2[0:n, t, half * 512:(half + 1) * 512]))
    v2_taken = taken["act"]

    for i, u in enumerate(units["gv"]):
        for t, (a, n) in enumerate(KT2):
            tile("gv", u, None, v_pairs(u, n2, a, n), n, P, "act", take_copy(gv[0:n, t, i * P:(i + 1) * P]))
    gv_taken = taken["act"]
    group2("gg", silu_g, None, nT, T, make=lambda d: take_func(d, ACT.Silu))
    group2("gate_a", sgate_a, None, nT, T, make=take_gate)
    group2("gate_b", sgate_b, None, nT, T, make=take_gate)
    gates2_taken = taken["act"]

    def wo_mla_take(n):
        def f(kind, eng, src):
            if n == 0:
                eng.wait_ge(S("taken_act"), gates2_taken)
            return eng.scalar_tensor_tensor(mixed2[:, n, :], sgate_a[:, n, :], 1.0, src, ALU.add, ALU.mult)
        return f
    for n, u in enumerate(units["wo_mla"]):
        tile("wo_mla", u, ("attn_out_ready", 4 + HEADS), std_pairs(u, attn2), P, T, "dve", wo_mla_take(n))
    for n, u in enumerate(units["wo_gla"]):
        tile("wo_gla", u, ("gla_ready", 1), std_pairs(u, og_n), P, T, "dve",
             add_take(mixed2[:, n, :], sgate_b[:, n, :], rs2[:, n % 2, 0:T]))
    mixed2_taken = taken["dve"]
    for n, u in enumerate(units["w_out"]):
        tile("w_out", u, ("taken_dve", mixed2_taken), std_pairs(u, mixed2), P, T, "dve", resid_take(n, None))

    conv_taken = max(tiles[n].seq for n in group_of["fill1"] if tiles[n].engine == "dve" and tiles[n].cols == T)
    for t in tiles:
        if t.ready and t.ready[1] == "conv":
            t.ready = (t.ready[0], conv_taken)
    last_tile = {t.unit: t.n for t in tiles}

    chained = {}

    def chain(ins, eng):
        key = "dve_chain" if eng is dve_eng[0] else "act_chain"
        chained[key] = chained.get(key, 0) + 1
        ins.then_inc(S(key), 1)
        eng.wait_ge(S(key), chained[key])

    dve_eng = [None]

    def pe_tiles(pe, numbers):
        for n in numbers:
            t = tiles[n]
            pe.wait_ge(S(arrival(t.unit)[0]), arrival(t.unit)[1])
            if t.ready:
                wait(pe, *t.ready)
            before = tiles[n - NPROJ] if n >= NPROJ else t
            if before.engine and n >= NPROJ:
                wait(pe, "taken_" + before.engine, before.seq)
            last = len(t.pairs) - 1
            for i, (lhs, rhs) in enumerate(t.pairs):
                mm = pe.matmul(ps[0:t.rows, t.bank, 0:t.cols], lhs, rhs, start=(t.start and i == 0),
                               stop=(t.stop and i == last))
            mm.then_inc(S("tile_done"), 1)

    WEIGH_AHEAD = 2
    weigh_at = {}
    for m in sorted(mod_prepared):
        weigh_at.setdefault(max(m - WEIGH_AHEAD, group_of["fill1"][0]), []).append(m)

    def take_tiles(kind, eng, numbers):
        for n in numbers:
            t = tiles[n]
            for m in weigh_at.get(n, ()):
                weigh_mod(kind, eng, m)
            if t.engine == kind:
                eng.wait_ge(S("tile_done"), n + 1)
                t.take(kind, eng, ps[0:t.rows, t.bank, 0:t.cols]).then_inc(S("taken_" + kind), 1)

    def pieces(group, parts):
        n = group_of[group] if isinstance(group, str) else [m for g in group for m in g]
        return [n[len(n) * i // parts:len(n) * (i + 1) // parts] for i in range(parts)]

    norm_count = [0, 0, 0]

    class Norm:

        def __init__(self, src, squares, n, cols, groups, lhs, width, root, ready, gain, dst=None, done=None, apply=None, fill=None,
                     each=None, done_each=None):
            self.fill = fill
            self.done_each = done_each
            self.each = each
            self.src = src
            self.squares = squares
            self.n = n
            self.cols = cols
            self.groups = groups
            self.lhs = lhs
            self.width = width
            self.root = root
            self.ready = ready
            self.gain = gain
            self.dst = dst
            self.done = done
            self.apply = apply
            self.id, self.g0, self.s0 = norm_count
            self.steps = n if each else 1
            norm_count[0] += 1
            norm_count[1] += len(groups)
            norm_count[2] += self.steps

        def act(self, eng):
            for r in self.ready:
                wait(eng, *r)
            for k in range(self.steps):
                a = slice(k, k + 1) if self.each else slice(0, self.n)
                if self.each:
                    wait(eng, *self.each(k))
                eng.activation(self.squares[:, a, 0:self.cols], self.src[:, a, :], ACT.Square).then_inc(S("norm_squared"), 1)
            for g in range(len(self.groups)):
                eng.wait_ge(S("norm_inverted"), self.g0 + g + 1)
                r = self.root[:, (self.g0 + g) % 2, 0:self.cols]
                eng.sqrt(r, r).then_inc(S("norm_rooted"), 1)
                if self.fill:
                    take_tiles("act", eng, self.fill[g])

        def pe(self, eng):
            if not self.each:
                eng.wait_ge(S("norm_squared"), self.s0 + 1)
            for g, group in enumerate(self.groups):
                wait(eng, "norm_inverted", self.g0 + g - 1)
                bank = B_STAT[(self.g0 + g) % 2]
                for i, k in enumerate(group):
                    if self.each:
                        eng.wait_ge(S("norm_squared"), self.s0 + k + 1)
                    mm = eng.matmul(ps[:, bank, 0:self.cols], self.lhs, self.squares[:, k, 0:self.cols],
                                    start=(i == 0), stop=(i == len(group) - 1))
                mm.then_inc(S("norm_summed"), 1)
                if self.fill:
                    pe_tiles(eng, self.fill[g])

        def dve(self, eng):
            def invert(g):
                r = self.root[:, (self.g0 + g) % 2, 0:self.cols]
                eng.wait_ge(S("norm_summed"), self.g0 + g + 1)
                chain(eng.tensor_scalar(r, ps[:, B_STAT[(self.g0 + g) % 2], 0:self.cols], 1.0 / self.width, EPS,
                                        ALU.mult, ALU.add), eng)
                eng.reciprocal(r, r).then_inc(S("norm_inverted"), 1)

            for r in self.ready:
                wait(eng, *r)
            n = len(self.groups)
            invert(0)
            for g in range(n):
                if g + 1 < n:
                    invert(g + 1)
                eng.wait_ge(S("norm_rooted"), self.g0 + g + 1)
                root = self.root[:, (self.g0 + g) % 2, 0:self.cols]
                if self.apply:
                    self.apply(eng, root)
                    continue
                for k in self.groups[g]:
                    ins = eng.scalar_tensor_tensor(self.dst(k), self.src[:, k, :], self.gain(k), root, ALU.mult, ALU.mult)
                    if self.done_each:
                        ins.then_inc(S(self.done_each), 1)
                if self.done_each:
                    continue
                if g == n - 1 and self.done:
                    ins.then_inc(S(self.done), 1)
                else:
                    chain(ins, eng)

    def flat_groups(n):
        return [[k] for k in range(n)]

    def take_mod_row(dve, g):
        dve.wait_ge(S("tile_done"), 4 * (g + 1))
        dve.tensor_copy(mod_row[0:2, g * 512:(g + 1) * 512], ps[0:2, MOD_BANKS[g], :]).then_inc(S("mod_row_taken"), 1)

    def apply_h1(eng, root):
        rb = root.rearrange("p (o t) -> p o t", o=1).broadcast_to([P, KD, T + CTX])
        eng.tensor_tensor(xin, xin, rb, ALU.mult)
        take_mod_row(eng, 2)
        take_mod_row(eng, 3)
        eng.wait_ge(S("mod_turned"), 1)
        b = v_("b_mod", 0, 16).rearrange("p (n o) -> p n o", o=1).broadcast_to([P, 16, 2])
        chain(eng.tensor_tensor(mod[:, 0:16, :], ps[:, MOD_BANKS[0], 0:32].rearrange("p (n c) -> p n c", n=16), b, ALU.add), eng)
        g = v_("norm1", 0, 8).rearrange("p (n o) -> p n o", o=1).broadcast_to([P, 8, 2])
        chain(eng.scalar_tensor_tensor(scale1[:, :, :], mod[:, 8:16, :], 1.0, g, ALU.add, ALU.mult), eng)
        eng.drain().then_inc(S("scale1_ready"), 1)
        for k in range(KD):
            ins = eng.tensor_scalar(h1[:, k, 0:T], xin[:, k, 0:T], scale1[:, k, 0:1], mod[:, k, 0:1], ALU.mult, ALU.add)
        ins.then_inc(S("h1_ready"), 1)

    def act_h1_context(act):
        act.wait_ge(S("scale1_ready"), 1)
        for k in range(KD):
            ins = act.activation(h1[:, k, T:], xin[:, k, T:], ACT.Identity, bias=mod[:, k, 1:2], scale=scale1[:, k, 1:2])
        ins.then_inc(S("h1_ready"), 1)

    def apply_h2(eng, root):
        for k in range(KD):
            ins = eng.scalar_tensor_tensor(h_full[:, k, :], resid[:, k, :], scale2[:, k:k + 1], root, ALU.mult, ALU.mult)
        chain(ins, eng)
        for k in range(KD):
            ins = eng.tensor_scalar(h_full[:, k, :], h_full[:, k, :], mod[:, 24 + k, 0:1], None, ALU.add)
        ins.then_inc(S("peer_in"), 1)

    norm_x = Norm(xin, sq1, KD, T + CTX, [list(range(KD))], ones, D, rs1,
                  [("x_loaded", 32), ("ones_ready", 1)], None, apply=apply_h1)
    out1_taken = tiles[group_of["out1"][-1]].seq
    norm_h2 = Norm(resid[:, :, :], sq1, KD, T, [list(range(KD))], ones, D, rs1, [], None,
                   apply=apply_h2, each=lambda k: ("taken_dve", out1_taken - KD + k + 1))
    norm_final = Norm(resid[:, :, :], sq2, KD, T, [list(range(KD))], ones, D, rs2, [],
                      lambda k: v_("final", k), dst=lambda k: hin[:, k, 0:T], done_each="x1_ready",
                      each=lambda k: ("peer_out", k + 1))
    norm_n2 = Norm(hin, sq2, KD, TM, [list(range(KD))], ones, D, rs2, [("meta_loaded", 16), ("norm_summed", 3)],
                   lambda k: v_("norm_mix", k), dst=lambda k: n2[:, k, :], done="n2_ready",
                   each=lambda k: ("x1_ready", k + 1))
    norm_cq = Norm(cq_b, sq2, 3, T, [[0, 1, 2]], ones, 384, rs2, [("taken_act", c_taken)],
                   lambda k: v_("q_norm", k), dst=lambda k: cqn[:, k, :], done="cq_ready")
    norm_ckv = Norm(ckv_b, sq2, 2, TM, [[0, 1]], ones, 256, rs2, [("norm_summed", 5)],
                    lambda k: v_("kv_norm", k), dst=lambda k: ckvn[:, k, :], done="ckv_ready")
    kpe3 = kpe_raw.rearrange("p (a t) -> p a t", a=1)
    norm_kpe = Norm(kpe3, sq2, 1, TM, [[0]], blk64, 64, rs2, [("norm_summed", 6)],
                    lambda k: v_("kn_pe"), dst=lambda k: kpe_n, done="kpe_ready")
    norm_qn = Norm(qnope, sq2, HEADS, T, flat_groups(HEADS), ones, P, rs2, [("taken_act", uq_taken), ("norm_summed", 7)],
                   lambda k: v_("qn_nope"), dst=lambda k: qnope_n[:, k, :], done="qn_ready", fill=pieces("gv", 12)[:HEADS])
    norm_qpe = Norm(qpe, sq2, 4, T, flat_groups(4), blk64, 64, rs2, [("norm_summed", 15)],
                    lambda k: v_("qn_pe"), dst=lambda k: qpe[:, k, :], done="qpe_ready", fill=pieces("gv", 12)[HEADS:])
    norm_kn = Norm(knope, sq2, HEADS, TM, flat_groups(HEADS), ones, P, rs2, [("taken_act", uk_taken), ("norm_summed", 19)],
                   lambda k: v_("kn_nope"), dst=lambda k: knope_n[:, k, :], done="kn_ready", fill=pieces([group_of["gg"][4:], group_of["gate_a"][:4]], HEADS))
    norm_gla = Norm(o_gla, sq2, KD, T, [[2 * h, 2 * h + 1] for h in range(GLA_HEADS)], ones, 256, rs2,
                    [("o_gla_ready", 4), ("norm_summed", 27)], lambda k: v_("gla_norm", k % 2),
                    dst=lambda k: og_n[:, k, :], done="og_normed")
    ffn_taken = tiles[group_of["w_out"][-1]].seq
    norm_ffn = Norm(resid[:, :, :], sq2, KD, T, [list(range(KD))], ones, D, rs2, [],
                    lambda k: v_("norm_ffn", k), dst=lambda k: h_full[:, k, :], done="peer_in",
                    each=lambda k: ("taken_dve", ffn_taken - KD + k + 1))

    rope_count = [0]

    class Rope:

        def __init__(self, items, n, rot, cos, sin, ready, tmp, done):
            self.items = items
            self.n = n
            self.rot = rot
            self.cos = cos
            self.sin = sin
            self.ready = ready
            self.tmp = tmp
            self.done = done
            self.r0 = rope_count[0]
            rope_count[0] += len(items)

        def pe(self, eng):
            for r in self.ready:
                wait(eng, *r)
            for i, (src, _) in enumerate(self.items):
                m = self.r0 + i
                wait(eng, "rope_read", m - 1)
                eng.matmul(ps[:, B_STAT[m % 2], 0:self.n], self.rot, src, start=True, stop=True).then_inc(S("rope_swapped"), 1)

        def dve(self, eng):
            for r in self.ready:
                wait(eng, *r)
            for i, (src, dst) in enumerate(self.items):
                m = self.r0 + i
                eng.tensor_tensor(dst, src, self.cos, ALU.mult)
                eng.wait_ge(S("rope_swapped"), m + 1)
                ins = eng.tensor_tensor(self.tmp, ps[:, B_STAT[m % 2], 0:self.n], self.sin, ALU.mult)
                ins.then_inc(S("rope_read"), 1)
                eng.wait_ge(S("rope_read"), m + 1)
                ins = eng.tensor_tensor(dst, dst, self.tmp, ALU.add)
                if i == len(self.items) - 1:
                    ins.then_inc(S(self.done), 1)
                else:
                    chain(ins, eng)

    rope_q1 = Rope([(k_raw[:, 0:T], k_rot[:, 0:T])] + [(q_raw[:, j, :], q_rot[:, j, :]) for j in range(4)], T,
                   con1_("rot"), con1_("cos"), con1_("sin"), [("taken_act", kv1_taken), ("norm_inverted", 1)],
                   rope_tmp[:, 0:T], "rope1_ready")
    rope_q2 = Rope([(qpe[:, j, :], qpe_rot[:, j, :]) for j in range(4)], T, con2_("rot"),
                   con2_("cos")[:, 0:T], con2_("sin")[:, 0:T], [("qpe_ready", 1), ("norm_inverted", 27), ("kn_ready", 1)],
                   rs2[:, 0, 0:T], "rope2_ready")
    rope_k2 = Rope([(kpe_n, kpe_rot)], TM, con2_("rot"), con2_("cos"), con2_("sin"), [("kpe_ready", 1)],
                   rs2[:, 1, :], "rope2_ready")

    att_count = [0, 0]

    class Attention:

        def __init__(self, items, n_keys, key_tiles, scale, probs, pt, fill, ready, outs, step=None):
            self.step = step
            self.items = items
            self.n_keys = n_keys
            self.key_tiles = key_tiles
            self.scale = scale
            self.probs = probs
            self.pt = pt
            self.fill = fill
            self.ready = ready
            self.outs = outs
            self.i0, self.o0 = att_count
            att_count[0] += len(items)
            att_count[1] += len(outs)

        def pe(self, eng):
            for r in self.ready:
                wait(eng, *r)
            n = len(self.items)

            def scores_of(i):
                it, m = self.items[i], self.i0 + i
                wait(eng, "att_masked", m - 1)
                for x, (lhs, rhs) in enumerate(it["scores"]):
                    mm = eng.matmul(ps[:, B_SCORE[m % 2], 0:self.n_keys], lhs, rhs, start=(x == 0),
                                    stop=(x == len(it["scores"]) - 1))
                mm.then_inc(S("att_scored"), 1)

            scores_of(0)
            scores_of(1)
            for i, it in enumerate(self.items):
                m = self.i0 + i
                if self.step:
                    self.step["pe"](eng, i)
                pe_tiles(eng, self.fill[i])
                eng.wait_ge(S("att_prob"), m + 1)
                wait(eng, "att_pt", m)
                for x, (a, w) in enumerate(self.key_tiles):
                    mm = eng.transpose(ps[0:w, B_PT, x * P:x * P + P], self.probs[:, m % 2, a:a + w], ident)
                mm.then_inc(S("att_turned"), 1)
                if i + 2 < n:
                    scores_of(i + 2)
                eng.wait_ge(S("att_pt"), m + 1)
                if it["wait_out"] > 0:
                    eng.wait_ge(S("attn_out_ready"), self.o0 + it["wait_out"])
                for x, (a, w) in enumerate(self.key_tiles):
                    mm = eng.matmul(it["out"], it["v"](x), self.pt[0:w, m % 2, x * P:(x + 1) * P], start=(x == 0),
                                    stop=(x == len(self.key_tiles) - 1))
                mm.then_inc(S("att_summed"), 1)

        def dve(self, eng):
            n = len(self.items)
            for r in self.ready:
                wait(eng, *r)

            def mask(i):
                it, m = self.items[i], self.i0 + i
                p = self.probs[:, m % 2, 0:self.n_keys]
                b = (m % 2) * 8
                eng.wait_ge(S("att_scored"), m + 1)
                wait(eng, "att_turned", m - 1)
                ins = eng.scalar_tensor_tensor(p, ps[:, B_SCORE[m % 2], 0:self.n_keys], self.scale, it["mask"],
                                               ALU.mult, ALU.add)
                ins.then_inc(S("att_masked"), 1)
                eng.wait_ge(S("att_masked"), m + 1)
                chain(eng.tensor_reduce(small[:, b:b + 1], p, AX_X, ALU.max), eng)
                if it["sink"] is None:
                    ins = eng.tensor_scalar(small[:, b + 1:b + 2], small[:, b:b + 1], -1.0, None, ALU.mult)
                else:
                    ins = eng.tensor_scalar(small[:, b + 1:b + 2], small[:, b:b + 1], v_("sink", it["sink"]), -1.0,
                                            ALU.max, ALU.mult)
                ins.then_inc(S("att_max"), 1)

            def normalise(i):
                it, m = self.items[i], self.i0 + i
                b = (m % 2) * 8
                p = self.probs[:, m % 2, 0:self.n_keys]
                eng.wait_ge(S("att_exp"), m + 1)
                if it["sink"] is not None:
                    chain(eng.tensor_tensor(small[:, b + 2:b + 3], small[:, b + 2:b + 3], small[:, b + 3:b + 4], ALU.add), eng)
                chain(eng.reciprocal(small[:, b + 4:b + 5], small[:, b + 2:b + 3]), eng)
                eng.tensor_scalar(p, p, small[:, b + 4:b + 5], None, ALU.mult).then_inc(S("att_prob"), 1)

            mask(0)
            for i in range(n):
                normalise(i)
                if i + 1 < n:
                    mask(i + 1)
                if self.step:
                    self.step["dve"](eng, i)
                take_tiles("dve", eng, self.fill[i])

        def act(self, eng):
            for i, it in enumerate(self.items):
                m = self.i0 + i
                b = (m % 2) * 8
                p = self.probs[:, m % 2, 0:self.n_keys]
                eng.wait_ge(S("att_max"), m + 1)
                if it["sink"] is not None:
                    eng.activation(small[:, b + 3:b + 4], v_("sink", it["sink"]), ACT.Exp, bias=small[:, b + 1:b + 2])
                eng.activation(p, p, ACT.Exp, bias=small[:, b + 1:b + 2],
                               accum_out=small[:, b + 2:b + 3]).then_inc(S("att_exp"), 1)
                take_tiles("act", eng, self.fill[i])
                eng.wait_ge(S("att_turned"), m + 1)
                wait(eng, "att_summed", m - 1)
                w = len(self.key_tiles) * P
                full = [x for x, (_, k) in enumerate(self.key_tiles) if k == P]
                ins = eng.copy(self.pt[:, m % 2, 0:len(full) * P], ps[:, B_PT, 0:len(full) * P])
                if len(full) < len(self.key_tiles):
                    k = self.key_tiles[-1][1]
                    ins = eng.copy(self.pt[0:k, m % 2, len(full) * P:w], ps[0:k, B_PT, len(full) * P:w])
                ins.then_inc(S("att_pt"), 1)
                if self.step:
                    self.step["act"](eng, i)
                if it["copy"] is not None:
                    eng.wait_ge(S("att_summed"), m + 1)
                    src, dst = self.outs[it["copy"]]
                    eng.copy(dst, src).then_inc(S("attn_out_ready"), 1)

    def region(x):
        return ps[:, B_OUT, (x % 2) * T:(x % 2 + 1) * T]

    items1, outs1 = [], []
    for j in range(4):
        outs1.append((region(j), attn1[:, j, :]))
        for g in range(2):
            for t in range(NT):
                rows = slice(g * HEAD, (g + 1) * HEAD)
                last = g == 1 and t == NT - 1
                items1.append(dict(
                    scores=[(q_rot[rows, j, t * P:(t + 1) * P], k_rot[rows, :])],
                    mask=con1_("mask")[:, t * 512:(t + 1) * 512], sink=g * GROUP + j,
                    v=lambda x, g=g: v_tok[:, x, g * HEAD:(g + 1) * HEAD],
                    out=ps[rows, B_OUT, (j % 2) * T + t * P:(j % 2) * T + (t + 1) * P],
                    copy=j if last else None, wait_out=j - 1))
    att1 = Attention(items1, T + CTX, [(i * P, P) for i in range(4)], HEAD ** -0.5, probs1, pt1,
                     pieces("fill1", len(items1)), [("rope1_ready", 1)], outs1)
    items2, outs2 = [], []
    for h in range(HEADS):
        outs2.append((region(h), attn2[:, h, :]))
        rows = slice((h % 2) * 64, (h % 2) * 64 + 64)
        for t in range(NT):
            q = slice(t * P, (t + 1) * P)
            items2.append(dict(
                scores=[(qnope_n[:, h, q], knope_n[:, h, :]), (qpe_rot[rows, h // 2, q], kpe_rot[rows, :])],
                mask=con2_("mask")[:, t * TM:(t + 1) * TM], sink=None,
                v=lambda x, h=h: v2[0:KT2[x][1], x, h * P:(h + 1) * P],
                out=ps[:, B_OUT, (h % 2) * T + t * P:(h % 2) * T + (t + 1) * P],
                copy=h if t == NT - 1 else None, wait_out=h - 1))
    att2 = Attention(items2, TM, KT2, 192 ** -0.5, probs2, pt2,
                     pieces([group_of["gate_a"][4:], group_of["gate_b"]], len(items2)),
                     [("kn_ready", 1), ("rope2_ready", 2), ("taken_act", v2_taken)], outs2,
                     step=dict(pe=lambda eng, i: pe_gla_level(eng, i - 1), dve=lambda eng, i: dve_gla_level(eng, i),
                               act=lambda eng, i: act_gla_level(eng, i + 1)))

    GLA_BANK = 3

    def pe_gla_decay(pe):
        pe.wait_ge(S("taken_act"), ga_taken)
        pe.wait_ge(S("wa2_loaded"), 16)
        for h in range(GLA_HEADS):
            if h == 3:
                pe.wait_ge(S("gla_logit_taken"), 1)
            pe.matmul(ps[:, 4 + h % 3, 0:TM], wa2_b[0:16, h * P:(h + 1) * P], ga_b[0:16, :], start=True,
                      stop=True).then_inc(S("gla_logit"), 1)

    def dve_gla_decay(dve):
        dve.wait_ge(S("taken_act"), ga_taken)
        for h in range(GLA_HEADS):
            dve.wait_ge(S("gla_logit"), h + 1)
            dve.tensor_scalar(la[:, h, :], ps[:, 4 + h % 3, 0:TM], v_("b_a", h), None, ALU.add)\
               .then_inc(S("gla_logit_taken"), 1)
        dve.wait_ge(S("gla_logit_taken"), GLA_HEADS)
        dve.scalar_tensor_tensor(lb, la, -1.0, la, ALU.mult, ALU.max).then_inc(S("gla_abs"), 1)
        dve.wait_ge(S("gla_log"), 1)
        chain(dve.tensor_scalar(la, la, 0.0, None, ALU.min), dve)
        chain(dve.tensor_tensor(la, la, lb, ALU.subtract), dve)
        chain(dve.tensor_scalar(la, la, 1.0 / TAU, None, ALU.mult), dve)
        for h in range(GLA_HEADS):
            for a, w in KT2:
                ins = dve.tensor_tensor_scan(lb[:, h, a:a + w], ones[:, 0:w], la[:, h, a:a + w], 0.0, ALU.mult, ALU.add)
        chain(ins, dve)
        for n, (a, w) in enumerate([KT2[2], KT2[0]]):
            dve.tensor_tensor(kdec[n], lb[:, :, a + w - 1:a + w].broadcast_to([P, GLA_HEADS, w]), lb[:, :, a:a + w], ALU.subtract)
        dve.tensor_copy(blast[:, 1, :], lb[:, :, P - 1]).then_inc(S("gla_ends"), 1)
        dve.wait_ge(S("gla_ends_exp"), 1)
        for n, (a, w) in enumerate([KT2[2], KT2[0]]):
            dve.tensor_tensor(kdec[n], kdec[n], gk[:, :, a:a + w], ALU.mult)
        dve.tensor_tensor(qdec, qdec, gq, ALU.mult).then_inc(S("gla_dec"), 1)

    def act_gla_decay(act):
        act.wait_ge(S("gla_abs"), 1)
        act.activation(lb, lb, ACT.Exp, scale=-1.0).then_inc(S("gla_e"), 1)
        act.wait_ge(S("gla_e"), 1)
        act.activation(lb, lb, ACT.Ln, bias=1.0).then_inc(S("gla_log"), 1)
        take_tiles("act", act, group_of["gg"][:2])
        act.wait_ge(S("gla_ends"), 1)
        act.activation(qdec, lb[:, :, 0:T], ACT.Exp)
        act.activation(kdec[0], kdec[0], ACT.Exp)
        act.activation(kdec[1], kdec[1], ACT.Exp)
        act.activation(blast[:, 1, :], blast[:, 1, :], ACT.Exp).then_inc(S("gla_ends_exp"), 1)
        take_tiles("act", act, group_of["gg"][2:4])

    gla_steps = [(t, n) for t in range(NT) for n in range(LEVELS + 1)]

    def dve_gla_level(dve, m):
        dve_gla_fade(dve, m)
        if m:
            collect(dve, m - 1)
        if m + 1 < len(gla_steps):
            dve_gla_distance(dve, m + 1)

    def dve_gla_distance(dve, m):
        t, n = gla_steps[m]
        a = t * P
        gd = gd2[(t * LEVELS + n) % 2]
        if n < LEVELS:
            size = 1 << n
            for h in range(GLA_HEADS):
                bh = lb[:, h, a:a + P].rearrange("p (m s) -> p m s", s=2 * size)
                dh = gd[:, h, :].rearrange("p (m s) -> p m s", s=2 * size)
                r = bh[:, :, size - 1:size].broadcast_to([P, P // (2 * size), 2 * size])
                ins = dve.tensor_tensor(dh, bh, r, ALU.subtract)
            chain(ins, dve)
            dve.scalar_tensor_tensor(gd, gd, -1.0, gd, ALU.mult, ALU.max).then_inc(S("gla_dist"), 1)

    def dve_gla_fade(dve, m):
        t, n = gla_steps[m]
        a = t * P
        dist = t * LEVELS + n
        gd = gd2[dist % 2]
        wait(dve, "gla_pair", m - 1)
        if n < LEVELS:
            dve.wait_ge(S("gla_fade"), dist + 1)
            dve.tensor_tensor(gqd[m % 2], gd, gq[:, :, a:a + P], ALU.mult)
            ins = dve.tensor_tensor(gkd[m % 2], gd, gk[:, :, a:a + P], ALU.mult)
        else:
            dve.tensor_copy(gqd[m % 2], gq[:, :, a:a + P])
            ins = dve.tensor_copy(gkd[m % 2], gk[:, :, a:a + P])
        ins.then_inc(S("gla_faded"), 1)

    def collect(dve, m):
        t, n = gla_steps[m]
        dve.wait_ge(S("gla_pair"), m + 1)
        mask = con2_("gla_mask")[:, n * P:(n + 1) * P].rearrange("p (a i) -> p a i", a=1).broadcast_to([P, GLA_HEADS, P])
        src = ps[:, GLA_BANK, :].rearrange("p (h i) -> p h i", h=GLA_HEADS)
        if n == 0:
            dve.tensor_tensor(amat[t], src, mask, ALU.mult).then_inc(S("gla_kept"), 1)
            return
        ins = dve.tensor_tensor(atmp, src, mask, ALU.mult)
        chain(ins, dve)
        dve.tensor_tensor(amat[t], amat[t], atmp, ALU.add).then_inc(S("gla_kept"), 1)
        dve.wait_ge(S("gla_kept"), m + 1)

    def act_gla_level(act, m):
        if m == len(gla_steps):
            return
        t, n = gla_steps[m]
        if n < LEVELS:
            dist = t * LEVELS + n
            act.wait_ge(S("gla_dist"), dist + 1)
            gd = gd2[dist % 2]
            act.activation(gd, gd, ACT.Exp, scale=-1.0).then_inc(S("gla_fade"), 1)

    def pe_gla_level(pe, m):
        if m < 0:
            return
        pe.wait_ge(S("gla_faded"), m + 1)
        wait(pe, "gla_kept", m)
        for h in range(GLA_HEADS):
            mm = pe.matmul(ps[:, GLA_BANK, h * P:(h + 1) * P], gkd[m % 2][:, h, :], gqd[m % 2][:, h, :],
                           start=True, stop=True)
        mm.then_inc(S("gla_pair"), 1)

    def pe_gla_out(pe):
        pe.wait_ge(S("gla_dec"), 1)
        pe.wait_ge(S("gla_kept"), len(gla_steps))
        pe.wait_ge(S("att_pt"), len(items1) + len(items2))
        for h in range(GLA_HEADS):
            pe.transpose(ps[0:META, 3, h * P:(h + 1) * P], kdec[0][:, h, :], ident)
        for h in range(GLA_HEADS):
            mm = pe.transpose(ps[:, 6, h * P:(h + 1) * P], kdec[1][:, h, :], ident)
        mm.then_inc(S("gla_turned"), 1)
        pe_tiles(pe, group_of["wo_mla"][1:2])
        pe.wait_ge(S("gla_turned_copied"), 1)
        pe.wait_ge(S("taken_act"), gv_taken)
        pe.wait_ge(S("norm_inverted"), 27)
        for n in range(2):
            rows = META if n == 0 else P
            src = 2 if n == 0 else 0
            for h in range(GLA_HEADS):
                bank = 3 if h < 2 else 7
                mm = pe.matmul(ps[:, bank, (h % 2) * 256:(h % 2 + 1) * 256], kdecT[n][0:rows, h, :],
                               gv[0:rows, src, h * 256:(h + 1) * 256], start=True, stop=True)
            mm.then_inc(S("gla_state"), 1)
            pe_tiles(pe, group_of["wo_mla"][2 + n:3 + n])
            pe.wait_ge(S("gla_state_kept"), n + 1)
        pe.wait_ge(S("gla_kept"), len(gla_steps))
        for t in range(NT):
            for h in range(GLA_HEADS):
                for e in range(2):
                    x = h * 2 + e
                    bank = [[4, 5], [6, 3]][t][x // 4]
                    dst = ps[:, bank, (x % 4) * P:(x % 4 + 1) * P]
                    pe.matmul(dst, gv[:, t, h * 256 + e * P:h * 256 + (e + 1) * P], amat[t][:, h, :], start=True, stop=False)
                    mm = pe.matmul(dst, state[t][:, h, e * P:(e + 1) * P], qdec[:, h, t * P:(t + 1) * P], start=False, stop=True)
                    if x % 4 == 3:
                        mm.then_inc(S("gla_o"), 1)

    def dve_gla_state(dve):
        for n in range(2):
            take_tiles("dve", dve, group_of["wo_mla"][n:n + 1])
            dve.wait_ge(S("gla_state"), n + 1)
            for h in range(GLA_HEADS):
                bank = 3 if h < 2 else 7
                src = ps[:, bank, (h % 2) * 256:(h % 2 + 1) * 256]
                if n == 0:
                    ins = dve.tensor_copy(state[0][:, h, :], src)
                else:
                    ins = dve.scalar_tensor_tensor(state[1][:, h, :], state[0][:, h, :], blast[:, 1, h:h + 1], src,
                                                   ALU.mult, ALU.add)
            ins.then_inc(S("gla_state_kept"), 1)
            dve.wait_ge(S("gla_state_kept"), n + 1)

    def act_gla_out(act):
        act.wait_ge(S("gla_turned"), 1)
        act.copy(kdecT[0][0:META, :, :], ps[0:META, 3, :].rearrange("p (h d) -> p h d", h=GLA_HEADS))
        act.copy(kdecT[1], ps[:, 6, :].rearrange("p (h d) -> p h d", h=GLA_HEADS)).then_inc(S("gla_turned_copied"), 1)
        for m in range(4):
            t, half = m // 2, m % 2
            bank = [[4, 5], [6, 3]][t][half]
            act.wait_ge(S("gla_o"), m + 1)
            act.copy(o_gla[:, half * 4:half * 4 + 4, t * P:(t + 1) * P],
                     ps[:, bank, :].rearrange("p (x i) -> p x i", x=4)).then_inc(S("o_gla_ready"), 1)

    def passes(pe, out_ap, w, m, start, stop):
        pe.matmul(out_ap, w[0], m[0], start=start, stop=False)
        pe.matmul(out_ap, w[1], m[0], start=False, stop=False)
        return pe.matmul(out_ap, w[0], m[1], start=False, stop=stop)

    UB = 4
    N_IT = P // UB
    TOPK_UB = 20
    TOPK_IT = NT * HEADS // 4
    MID_UNITS = 32
    MID_AT = TOPK_UB * TOPK_IT
    MID_END = MID_AT + MID_UNITS

    NQ = 16
    BEFORE = {"wq": 0, "u": NQ, "v": NQ + P}
    PER_BLOCK = NQ + 2 * P

    def halves(b, table):
        return ((b - 1) * PER_BLOCK + BEFORE[table]) * 2

    def banks_freed(b, table):
        return (b - 1) * (NQ + P + 4) + BEFORE[table]

    def peer_pe_scores(pe, b):
        pe.wait_ge(S("u_bank_free"), banks_freed(b, "u") + 4)
        pe.wait_ge(S(f"keys_loaded{b}"), 16)
        for t in range(NT):
            for j in range(16):
                bank = (4 if t == 0 else 0) + j // 4
                mm = pe.matmul(ps[:, bank, (j % 4) * P:(j % 4 + 1) * P],
                               q_area[:, j * T + t * P:j * T + (t + 1) * P], keys_area[:, j, :], start=True, stop=True)
                if j % 4 == 3:
                    mm.then_inc(S("peer_scored"), 1)

    def peer_act_scores(act, b):
        for m in range(8):
            t, n = m // 4, m % 4
            act.wait_ge(S("peer_scored"), (b - 1) * 8 + m + 1)
            act.copy(s_area[:, t * 2048 + n * 512:t * 2048 + (n + 1) * 512],
                     ps[:, (4 if t == 0 else 0) + n, :]).then_inc(S("peer_s_copied"), 1)

    def u_unit(kind, eng, b, i, s, per=4, extra=None, first=False, table="u"):
        unit = units[f"{table}{b}"][0] + s
        h0 = halves(b, table) + 2 * s
        if kind == "pe":
            eng.wait_ge(S("u_bank_free"), i * per + (banks_freed(b, table) + s + 1))
        if kind == "act":
            eng.wait_ge(S(ring_full[unit % RING]), i * (16 * per // RING) + 16 * (unit // RING + 1))
        for half in range(2):
            hslot = (h0 + half) % HLRING
            raw = slot(unit)[:, half * HALF:(half + 1) * HALF]
            if kind == "pe":
                eng.wait_ge(S("split_hi"), i * 2 * per + (h0 + half + 1))
                eng.wait_ge(S("split_lo"), i * 2 * per + (h0 + half + 1))
                for n in range(KD // 2):
                    k = half * KD // 2 + n
                    w = [hl[:, hslot, x, n * P:(n + 1) * P] for x in range(2)]
                    m = [hsplit[:, x, k, :] for x in range(2)]
                    mm = passes(eng, ps[:, s % 4, 0:T], w, m, k == 0, k == KD - 1)
                mm.then_inc(S("split_used"), 1)
            if kind == "act":
                eng.wait_ge(S("split_used"), i * 2 * per + (h0 + half + HLRING * b - HLRING + 1))
                eng.copy(hl[:, hslot, 0, :], raw).then_inc(S("split_hi"), 1)
            if kind == "dve":
                eng.wait_ge(S("split_hi"), i * 2 * per + (h0 + half + 1))
                eng.tensor_tensor(hl[:, hslot, 1, :], raw, hl[:, hslot, 0, :].bitcast(F32), ALU.subtract)\
                   .then_inc(S("split_lo"), 1)
                if extra:
                    extra(i, s, half)
        if kind == "act" and not (first and s < 2):
            take_unit(eng, b, i, s - 2, per, table)

    def u_loop(kind, eng, b, it0, it1, table="u"):
        with eng.Fori(it0, it1) as i:
            for s in range(UB):
                u_unit(kind, eng, b, i, s, table=table)

    def load_gelu(act, b):
        act.activation(small[:, 15 + b:16 + b], v_("sink"), ACT.Gelu)

    def take_unit(eng, b, i, s, per=4, table="u"):
        eng.wait_ge(S("split_used"), i * 2 * per + (halves(b, table) + HLRING * b + 2 * s + 2))
        dst, func = (acts, ACT.Gelu) if table == "u" else (q_area, ACT.Copy)
        eng.activation(dst[:, ds(i * (per * T) + s * T, T)], ps[:, s % 4, 0:T], func).then_inc(S("u_bank_free"), 1)

    def topk_part(eng, i, s, half):
        q, n = divmod(2 * s + half, 10)
        at = i * (4 * TOPK) + q * TOPK
        halves_of = [(x, keybuf[:, x * P:(x + 1) * P], tmpbuf[:, x * P:(x + 1) * P]) for x in range(2)]
        if n == 0:
            eng.tensor_copy(keybuf[:, :], s_area[:, ds(i * 1024 + q * 256, 256)])
            eng.drain()
            for x, keys, _ in halves_of:
                eng.max(topbuf[:, x, 0:8], keys)
        if n == 1:
            for x, keys, rest in halves_of:
                eng.max_index(idxbuf[:, x, 0:8], topbuf[:, x, 0:8], keys)
        if n == 2:
            for x, keys, rest in halves_of:
                eng.match_replace(rest, topbuf[:, x, 0:8], keys, NEG)
        if n == 3:
            for x, _, rest in halves_of:
                eng.max(topbuf[:, x, 8:16], rest)
        if n == 4:
            for x, _, rest in halves_of:
                eng.max_index(idxbuf[:, x, 8:16], topbuf[:, x, 8:16], rest)
        if n == 5:
            eng.tensor_copy(index_f[:, :, ds(at, TOPK)], idxbuf[:, :, :])
            eng.tensor_tensor(keybuf[:, :].rearrange("p (a b) -> p a b", a=TOPK),
                              topbuf[:, 0, :].rearrange("p (a o) -> p a o", o=1).broadcast_to([P, TOPK, TOPK]),
                              topbuf[:, 1, :].rearrange("p (o b) -> p o b", o=1).broadcast_to([P, TOPK, TOPK]),
                              ALU.add)
        if n == 6:
            eng.max(bestbuf[:, 0:8], keybuf[:, :])
            eng.drain()
            eng.match_replace(tmpbuf[:, :], bestbuf[:, 0:8], keybuf[:, :], NEG)
        if n == 7:
            eng.max(bestbuf[:, 8:16], tmpbuf[:, :])
            eng.max_index(posbuf[:, 0:8], bestbuf[:, 0:8], keybuf[:, :])
        if n == 8:
            eng.max_index(posbuf[:, 8:16], bestbuf[:, 8:16], tmpbuf[:, :])
        if n == 9:
            eng.tensor_copy(sum_best[:, ds(at, TOPK)], bestbuf[:, :])
            eng.tensor_copy(sum_pos[:, ds(at, TOPK)], posbuf[:, :])
        eng.drain()

    index_f = gate_f[:, :, :, :].rearrange("p x t r -> p x (t r)")

    LOOKUPS = 2 * NT * 2
    EXP_UNIT, SOFTMAX, LOOK = 1, 9, 2
    TURN = (LOOK + 2 * 3 * LOOKUPS) // 2 + 1
    TAKE = 2 * TURN + 4

    ROUND = 1.5 * 2.0 ** 23

    def dve_gate_part(dve, b, n):
        r1, r2 = rank1.rearrange("p t r -> p (t r)"), rank2.rearrange("p t r -> p (t r)")
        if n == 0:
            best = sum_best.rearrange("p (m k) -> p m k", k=TOPK)
            dve.tensor_tensor(chosen[:, 2, :].rearrange("p (m k) -> p m k", k=TOPK), best,
                              best[:, :, 0:1].broadcast_to([P, NT * HEADS, TOPK]), ALU.subtract).then_inc(S("gates_shifted"), 1)
            chain(dve.tensor_scalar(r1, sum_pos, 1.0 / TOPK, -15.0 / 32, ALU.mult, ALU.add), dve)
        if n == 1:
            chain(dve.tensor_scalar(r1, r1, ROUND, ROUND, ALU.add, ALU.subtract), dve)
            chain(dve.scalar_tensor_tensor(r2, r1, -float(TOPK), sum_pos, ALU.mult, ALU.add), dve)
        gates = chosen[:, 2, :].rearrange("p (m k) -> p m k", k=TOPK)
        if n == SOFTMAX:
            dve.wait_ge(S("gates_exp"), b)
            chain(dve.tensor_reduce(gate_sum[:, 0, :], gates, AX_X, ALU.add), dve)
            chain(dve.reciprocal(gate_sum[:, 1, :], gate_sum[:, 0, :]), dve)
            z = gate_sum[:, 1, :].rearrange("p (m o) -> p m o", o=1).broadcast_to([P, NT * HEADS, TOPK])
            chain(dve.tensor_tensor(gates, gates, z, ALU.mult), dve)
        if LOOK <= n < LOOK + 6 * LOOKUPS and n % 2 == 0:
            c, step = (n - LOOK) // 6, (n - LOOK) // 2 % 3
            x, t, half = c // 4, c // 2 % 2, c % 2
            rows = slice(half * 64, half * 64 + 64)
            hit = lookup[:, c % 2, :]
            rank = (rank1, rank2)[x][:, t, rows].rearrange("p (r o) -> p r o", o=1).broadcast_to([P, 64, TOPK])
            if step == 0:
                every = iota[:, 0:TOPK].rearrange("p (o a) -> p o a", o=1).broadcast_to([P, 64, TOPK])
                ins = dve.tensor_tensor(hit.rearrange("p (r a) -> p r a", a=TOPK), rank, every, ALU.is_equal)
            if step == 1:
                keys = gate_f[:, x, t, rows].rearrange("p (h o a) -> p h o a", h=4, o=1).broadcast_to([P, 4, TOPK, TOPK])
                h4 = hit.rearrange("p (h k a) -> p h k a", h=4, k=TOPK)
                ins = dve.tensor_tensor(h4, h4, keys, ALU.mult)
            if step == 2:
                at = t * P + half * 64
                ins = dve.tensor_reduce(chosen[:, x, at:at + 64], hit.rearrange("p (r a) -> p r a", a=TOPK), AX_X, ALU.add)
            if c == LOOKUPS - 1 and step == 2:
                ins.then_inc(S("experts_chosen"), 1)
            else:
                chain(ins, dve)
        if n == TAKE:
            dve.wait_ge(S("experts_turned"), b)
            dve.tensor_copy(sel[:, 0:2, :], ps[:, 4, :].rearrange("p (c t) -> p c t", c=2))
            dve.tensor_copy(sel[:, 2, :], ps[:, 5, 0:T])
        if n == TAKE + 1:
            dve.tensor_scalar(sel[:, 3, :], ps[:, 4, T:2 * T], -1.0, None, ALU.mult)
            dve.tensor_scalar(sel[:, 4, :], ps[:, 5, 0:T], -1.0, None, ALU.mult).then_inc(S("sel_taken"), 1)

    def pe_gate_part(pe, b, n):
        if n == TURN:
            pe.wait_ge(S("experts_chosen"), b)
            for c in range(3):
                for t in range(NT):
                    m = c * NT + t
                    mm = pe.transpose(ps[:, 4 + m // 4, m % 4 * P:m % 4 * P + P], chosen[:, c, t * P:(t + 1) * P], ident)
            mm.then_inc(S("experts_turned"), 1)

    def act_gate_part(act, b, n):
        if n == EXP_UNIT:
            act.wait_ge(S("gates_shifted"), b)
            act.activation(chosen[:, 2, :], chosen[:, 2, :], ACT.Exp).then_inc(S("gates_exp"), 1)

    NG = T // 8
    HOT_AHEAD = 2

    def base(b):
        return (b - 1) * (NG + GRING)

    def dve_hots(dve, b, g, slot_):
        dve.wait_ge(S("e_ready"), g + (base(b) + 1))
        dve.tensor_copy(stage[slot_], sel[:, :, ds(g * 8, 8)]).then_inc(S("staged"), 1)
        dve.wait_ge(S("staged"), g + ((b - 1) * NG + 1))
        dve.tensor_tensor(hot1[:, slot_, :, :], stage[slot_][:, 0, :].rearrange("p (t o) -> p t o", o=1).broadcast_to([P, 8, P]),
                          iota.rearrange("p (o i) -> p o i", o=1).broadcast_to([P, 8, P]), ALU.is_equal)
        for t in range(ACT_HOT, 8):
            ins = dve.tensor_scalar(hot2[:, slot_, t, :], iota, stage[slot_][:, 1, t:t + 1],
                                    stage[slot_][:, 2, t:t + 1], ALU.is_equal, ALU.mult)
        ins.then_inc(S("hots_dve"), 1)

    def act_hots(act, b, g, slot_):
        act.wait_ge(S("staged"), g + ((b - 1) * NG + 1))
        st, dist = stage[slot_], hot_dist[slot_ % 2]
        for t in range(ACT_HOT):
            ins = act.activation(dist[:, t, :], iota, ACT.Abs, bias=st[:, 3, t:t + 1])
        ins.then_inc(S("hot_dist_ready"), 1)
        act.wait_ge(S("hot_dist_ready"), g + ((b - 1) * NG + 1))
        for t in range(ACT_HOT):
            ins = act.activation(hot2[:, slot_, t, :], dist[:, t, :], ACT.Relu, bias=st[:, 2, t:t + 1], scale=st[:, 4, t:t + 1])
        ins.then_inc(S("hots_act"), 1)

    def e_banks(slot_):
        return ps[:, 2 * slot_:2 * slot_ + 2, :].rearrange("p s n -> p (s n)")

    def pe_gates(pe, b, g, slot_):
        pe.wait_ge(S("hots_dve"), g + ((b - 1) * NG + 1))
        pe.wait_ge(S("hots_act"), g + ((b - 1) * NG + 1))
        pe.wait_ge(S("gated"), g + (base(b) + 1))
        for t in range(8):
            mm = pe.matmul(e_banks(slot_)[:, t * P:(t + 1) * P], hot1[:, slot_, t, :], hot2[:, slot_, t, :],
                           start=True, stop=True)
        mm.then_inc(S("e_ready"), 1)

    def dve_multiply(dve, b, g, slot_):
        dve.wait_ge(S("e_ready"), g + (base(b) + GRING + 1))
        a8 = acts[:, :].rearrange("p (i t) -> p i t", t=T)[:, :, ds(g * 8, 8)]
        src = e_banks(slot_).rearrange("p (t i) -> p i t", t=8)
        dve.tensor_tensor(a8, a8, src, ALU.mult).then_inc(S("gated"), 1)

    def ds(a, n):
        return bass.ds(a, n) if not isinstance(a, int) else slice(a, a + n)

    def v_loop(kind, eng, b):
        v_first = units[f"v{b}"][0]

        def body(i, first, last):
            for s in range(UB):
                unit = v_first + s
                cslot = s % CRING
                h0 = halves(b, "v") + 2 * s
                c = ds(i * (UB * T) + s * T, T)
                if kind == "act":
                    eng.wait_ge(S(ring_full[unit % RING]), i * 16 + 16 * (unit // RING + 1))
                for half in range(2):
                    hslot = (h0 + half) % HLRING
                    part = slice(half * HALF, (half + 1) * HALF)
                    if kind == "act":
                        eng.wait_ge(S("split_used"), i * 2 * UB + (h0 + half + HLRING * b - HLRING + 1))
                        if half == 0:
                            eng.copy(csplit[:, cslot, 0, :], acts[:, c]).then_inc(S("csplit_hi"), 1)
                        eng.copy(hl[:, hslot, 0, :], slot(unit)[:, part]).then_inc(S("split_hi"), 1)
                    if kind == "dve":
                        if half == 0:
                            eng.wait_ge(S("csplit_hi"), i * UB + ((b - 1) * P + s + 1))
                            eng.tensor_tensor(csplit[:, cslot, 1, :], acts[:, c], csplit[:, cslot, 0, :].bitcast(F32),
                                              ALU.subtract)
                        eng.wait_ge(S("split_hi"), i * 2 * UB + (h0 + half + 1))
                        eng.tensor_tensor(hl[:, hslot, 1, :], slot(unit)[:, part], hl[:, hslot, 0, :].bitcast(F32),
                                          ALU.subtract).then_inc(S("split_lo"), 1)
                    if kind == "pe":
                        eng.wait_ge(S("split_hi"), i * 2 * UB + (h0 + half + 1))
                        eng.wait_ge(S("split_lo"), i * 2 * UB + (h0 + half + 1))
                        for n in range(KD // 2):
                            w = [hl[:, hslot, x, n * P:(n + 1) * P] for x in range(2)]
                            m = [csplit[:, cslot, x, :] for x in range(2)]
                            mm = passes(eng, ps[:, half * KD // 2 + n, 0:T], w, m, first and s == 0, last and s == UB - 1)
                        mm.then_inc(S("split_used"), 1)

        body(0, True, False)
        with eng.Fori(1, N_IT - 1) as i:
            body(i, False, False)
        body(N_IT - 1, False, True)

    def peer_pe(pe, b):
        pe.wait_ge(S("peer_in"), b)
        pe.drain().then_inc(S("split_used"), HLRING)
        pe.wait_ge(S("hsplit_ready"), b)
        u_loop("pe", pe, b, 0, NQ // UB, table="wq")
        peer_pe_scores(pe, b)
        pe.wait_ge(S("peer_s_copied"), 8 * b)
        with pe.Fori(0, TOPK_IT) as i:
            for s in range(TOPK_UB):
                u_unit("pe", pe, b, i, s, TOPK_UB)
        for n in range(MID_UNITS):
            u_unit("pe", pe, b, 0, MID_AT + n)
            pe_gate_part(pe, b, n)
        u_loop("pe", pe, b, MID_END // UB, N_IT)
        pe.wait_ge(S("u_bank_free"), banks_freed(b + 1, "wq"))
        pe.wait_ge(S("sel_taken"), b)
        pe.drain().then_inc(S("e_ready"), GRING)
        pe.drain().then_inc(S("gated"), GRING)
        with pe.Fori(0, NG // GRING) as i:
            for n in range(GRING):
                pe_gates(pe, b, i * GRING + n, n)
        pe.wait_ge(S("gated"), b * (NG + GRING))
        v_loop("pe", pe, b)

    def peer_act(act, b):
        act.wait_ge(S("peer_in"), b)
        act.copy(hsplit[:, 0, :, :], h_full).then_inc(S("hsplit_hi"), 1)
        act.drain().then_inc(S("u_bank_free"), 4)
        for s in range(UB):
            u_unit("act", act, b, 0, s, first=True, table="wq")
        u_loop("act", act, b, 1, NQ // UB, table="wq")
        take_unit(act, b, NQ // UB, -2, table="wq")
        take_unit(act, b, NQ // UB, -1, table="wq")
        peer_act_scores(act, b)
        load_gelu(act, b)
        for s in range(UB):
            u_unit("act", act, b, 0, s, first=True)
        u_loop("act", act, b, 1, MID_AT // UB)
        for n in range(MID_UNITS):
            u_unit("act", act, b, 0, MID_AT + n)
            act_gate_part(act, b, n)
        u_loop("act", act, b, MID_END // UB, N_IT)
        take_unit(act, b, N_IT, -2)
        take_unit(act, b, N_IT, -1)
        with act.Fori(0, NG // GRING) as i:
            for n in range(GRING):
                act_hots(act, b, i * GRING + n, n)
        act.wait_ge(S("gated"), b * (NG + GRING))
        v_loop("act", act, b)

    def peer_dve(dve, b):
        dve.wait_ge(S("hsplit_hi"), b)
        dve.tensor_tensor(hsplit[:, 1, :, :], h_full, hsplit[:, 0, :, :].bitcast(F32), ALU.subtract)\
           .then_inc(S("hsplit_ready"), 1)
        u_loop("dve", dve, b, 0, NQ // UB, table="wq")
        dve.wait_ge(S("peer_s_copied"), 8 * b)
        with dve.Fori(0, TOPK_IT) as i:
            for s in range(TOPK_UB):
                u_unit("dve", dve, b, i, s, TOPK_UB, extra=lambda i, s, half: topk_part(dve, i, s, half))
        for n in range(MID_UNITS):
            u_unit("dve", dve, b, 0, MID_AT + n, extra=lambda i, s, half: dve_gate_part(dve, b, 2 * (s - MID_AT) + half))
        u_loop("dve", dve, b, MID_END // UB, N_IT)
        for g in range(HOT_AHEAD):
            dve_hots(dve, b, g, g)
        with dve.Fori(0, NG // GRING - 1) as i:
            for n in range(GRING):
                dve_hots(dve, b, i * GRING + (n + HOT_AHEAD), (n + HOT_AHEAD) % GRING)
                dve_multiply(dve, b, i * GRING + n, n)
        for g in range(NG - GRING, NG):
            if g + HOT_AHEAD < NG:
                dve_hots(dve, b, g + HOT_AHEAD, (g + HOT_AHEAD) % GRING)
            dve_multiply(dve, b, g, g % GRING)
        dve.wait_ge(S("gated"), b * (NG + GRING))
        v_loop("dve", dve, b)
        dve.wait_ge(S("split_used"), halves(b + 1, "wq") + HLRING * b)
        for k in range(KD):
            if b == 1:
                ins = dve.scalar_tensor_tensor(resid[:, k, :], ps[:, k, 0:T], mod[:, 40 + k, 0:1], resid[:, k, :],
                                               ALU.mult, ALU.add)
            else:
                ins = dve.tensor_tensor(resid[:, k, :], ps[:, k, 0:T], resid[:, k, :], ALU.add)
            ins.then_inc(S("peer_out"), 1)

    with nc.Block() as block:
        @block.sync
        def _(sp):
            peer_units = {u: n for n, u in enumerate(m for key in ("wq1", "u1", "v1", "wq2", "u2", "v2") for m in units[key])}

            def load(u):
                sp.dma_start(slot(u), stream[u, :, :]).then_inc(S(arrival(u)[0]), 16)

            u = 0
            while u < n_units:
                old = u - RING
                if u in peer_units and old in peer_units:
                    end = u
                    while end < n_units and end in peer_units:
                        end += 1
                    rounds = (end - u) // RING
                    n0 = peer_units[old]
                    with sp.Fori(0, rounds) as i:
                        for s in range(RING):
                            sp.wait_ge(S("split_lo"), i * 2 * RING + 2 * (n0 + s + 1))
                            sp.dma_start(slot(u + s), stream[bass.ds(i * RING + (u + s), 1), :, :]
                                         .rearrange("a p n -> (a p) n")).then_inc(S(ring_full[(u + s) % RING]), 16)
                    u += rounds * RING
                    while u < end:
                        sp.wait_ge(S("split_lo"), 2 * (peer_units[u - RING] + 1))
                        load(u)
                        u += 1
                    continue
                if old in peer_units:
                    sp.wait_ge(S("split_lo"), 2 * (peer_units[old] + 1))
                elif old >= 0:
                    sp.wait_ge(S("tile_done"), last_tile[old] + 1)
                load(u)
                u += 1
            sp.wait_ge(S("peer_out"), 2 * KD)
            sp.dma_start(out, resid[:, :, :]).then_inc(S("out_stored"), 16)
            sp.wait_ge(S("out_stored"), 16)

        @block.gpsimd
        def _(pool):
            pool.memset(ones, 1.0).then_inc(S("ones_ready"), 1)

        @block.scalar
        def _(act):
            act.dma_start(vec[:, :], vectors).then_inc(S("vec_loaded"), 16)
            act.dma_start(xin[:, :, 0:T], xT).then_inc(S("x_loaded"), 16)
            act.dma_start(xin[:, :, T:], ctxT).then_inc(S("x_loaded"), 16)
            act.dma_start(con[:, :], common).then_inc(S("common_loaded"), 16)
            act.wait_ge(S("vec_loaded"), 16)
            cond = vec[:, vec_at["cond"][0]:vec_at["cond"][0] + 16].rearrange("p (k c) -> p k c", k=KD)
            act.activation(silu_c, cond, ACT.Silu).then_inc(S("silu_ready"), 1)
            norm_x.act(act)
            act_h1_context(act)
            act.dma_start(con1, consts1).then_inc(S("consts_loaded"), 16)
            act.dma_start(resid[:, :, :], xT).then_inc(S("consts_loaded"), 16)
            act.wait_ge(S("consts_loaded"), 32)
            take_tiles("act", act, group_of["kvq1"])
            att1.act(act)
            take_tiles("act", act, group_of["out1"])
            norm_h2.act(act)
            act.dma_start(keys_area, keys1).then_inc(S("keys_loaded1"), 16)
            peer_act(act, 1)
            act.wait_ge(S("peer_out"), 1)
            act.dma_start(con2, consts2).then_inc(S("consts2_loaded"), 16)
            act.dma_start(hin[:, :, T:TM], metaT).then_inc(S("meta_loaded"), 16)
            act.dma_start(wa2_b[0:16, :], w_a2).then_inc(S("wa2_loaded"), 16)
            norm_final.act(act)
            norm_n2.act(act)
            for g in ("cq", "ckv", "kpe", "gq"):
                take_tiles("act", act, group_of[g])
            norm_cq.act(act)
            take_tiles("act", act, group_of["gk"][:2])
            norm_ckv.act(act)
            take_tiles("act", act, group_of["gk"][2:])
            norm_kpe.act(act)
            for g in ("ga", "uq", "ukv_k", "ukv_v"):
                take_tiles("act", act, group_of[g])
            norm_qn.act(act)
            norm_qpe.act(act)
            act_gla_decay(act)
            norm_kn.act(act)
            act.wait_ge(S("consts2_loaded"), 16)
            act_gla_level(act, 0)
            att2.act(act)
            act_gla_out(act)
            norm_gla.act(act)
            norm_ffn.act(act)
            act.wait_ge(S("peer_in"), 2)
            act.dma_start(keys_area, keys2).then_inc(S("keys_loaded2"), 16)
            peer_act(act, 2)

        @block.vector
        def _(dve):
            dve_eng[0] = dve
            dve.wait_ge(S("vec_loaded"), 16)
            for g in range(2):
                take_mod_row(dve, g)
            norm_x.dve(dve)
            dve.wait_ge(S("consts_loaded"), 32)
            rope_q1.dve(dve)
            dve.tensor_copy(k_rot[:, T:T + CTX], k_raw[:, T:T + CTX]).then_inc(S("rope1_ready"), 1)
            att1.dve(dve)
            chain(dve.tensor_scalar(half_gate[:, :], mod[:, 16:24, 0], 0.5, None, ALU.mult), dve)
            take_tiles("dve", dve, group_of["out1"])
            chain(dve.scalar_tensor_tensor(scale2[:, :], mod[:, 32:40, 0], 1.0, v_("norm2", 0, 8), ALU.add, ALU.mult), dve)
            norm_h2.dve(dve)
            peer_dve(dve, 1)
            norm_final.dve(dve)
            dve.wait_ge(S("x1_ready"), KD)
            chain(dve.tensor_copy(resid[:, :, :], hin[:, :, 0:T]), dve)
            norm_n2.dve(dve)
            norm_cq.dve(dve)
            norm_ckv.dve(dve)
            norm_kpe.dve(dve)
            norm_qn.dve(dve)
            norm_qpe.dve(dve)
            dve_gla_decay(dve)
            norm_kn.dve(dve)
            dve.wait_ge(S("consts2_loaded"), 16)
            rope_q2.dve(dve)
            rope_k2.dve(dve)
            dve_gla_distance(dve, 0)
            att2.dve(dve)
            collect(dve, len(gla_steps) - 1)
            dve_gla_state(dve)
            take_tiles("dve", dve, group_of["wo_mla"][2:6])
            norm_gla.dve(dve)
            dve.wait_ge(S("og_normed"), 1)
            dve.wait_ge(S("taken_act"), gates2_taken)
            dve.tensor_tensor(og_n, og_n, silu_g, ALU.mult).then_inc(S("gla_ready"), 1)
            take_tiles("dve", dve, group_of["wo_mla"][6:])
            for g in ("wo_gla", "w_out"):
                take_tiles("dve", dve, group_of[g])
            norm_ffn.dve(dve)
            peer_dve(dve, 2)

        @block.tensor
        def _(pe):
            pe_tiles(pe, group_of["mod_a"][:8])
            norm_x.pe(pe)
            pe_tiles(pe, group_of["mod_a"][8:])
            pe.wait_ge(S("mod_row_taken"), 4)
            pe.wait_ge(S("common_loaded"), 16)
            for n in range(16):
                mm = pe.transpose(ps[:, MOD_BANKS[0], 2 * n:2 * n + 2], mod_row[0:2, n * P:(n + 1) * P], ident[0:2, 0:2])
            mm.then_inc(S("mod_turned"), 1)
            pe_tiles(pe, group_of["kvq1"])
            pe.wait_ge(S("consts_loaded"), 32)
            rope_q1.pe(pe)
            pe.wait_ge(S("rope1_ready"), 2)
            att1.pe(pe)
            pe_tiles(pe, group_of["out1"])
            norm_h2.pe(pe)
            peer_pe(pe, 1)
            pe.wait_ge(S("peer_out"), B_STAT[norm_final.g0 % 2] + 1)
            norm_final.pe(pe)
            norm_n2.pe(pe)
            for g in ("cq", "ckv", "kpe", "gq"):
                pe_tiles(pe, group_of[g])
            norm_cq.pe(pe)
            pe_tiles(pe, group_of["gk"][:2])
            norm_ckv.pe(pe)
            pe_tiles(pe, group_of["gk"][2:])
            norm_kpe.pe(pe)
            for g in ("ga", "uq", "ukv_k", "ukv_v"):
                pe_tiles(pe, group_of[g])
            norm_qn.pe(pe)
            norm_qpe.pe(pe)
            pe_gla_decay(pe)
            pe_tiles(pe, group_of["gg"][:4])
            norm_kn.pe(pe)
            pe.wait_ge(S("consts2_loaded"), 16)
            rope_q2.pe(pe)
            rope_k2.pe(pe)
            att2.pe(pe)
            pe_gla_level(pe, len(gla_steps) - 1)
            pe_tiles(pe, group_of["wo_mla"][:1])
            pe_gla_out(pe)
            pe_tiles(pe, group_of["wo_mla"][4:6])
            norm_gla.pe(pe)
            pe_tiles(pe, group_of["wo_mla"][6:])
            for g in ("wo_gla", "w_out"):
                pe_tiles(pe, group_of[g])
            norm_ffn.pe(pe)
            peer_pe(pe, 2)


def kernel(**inputs):
    import concourse.bacc as bacc
    from concourse.bass_utils import run_bass_kernel_spmd

    a = {k: np.asarray(v) for k, v in inputs.items()}
    common, consts1, consts2 = shape_constants()
    keys1 = a["peer_sub_keys"][0].reshape(16, P, P).transpose(2, 0, 1)
    keys2 = np.tile(a["peer_keys_2"][0].transpose(2, 0, 1)[:, None], (1, HEADS, 1, 1)).reshape(P, 16, P)
    arrays = {
        "stream": pack_stream(a), "xT": feature_major(a["x"][0]), "ctxT": feature_major(a["ctx"][0]),
        "metaT": feature_major(a["meta_2"]), "vectors": pack_vectors(a), "common": common,
        "consts1": consts1, "consts2": consts2, "keys1": keys1, "keys2": keys2, "w_a2": a["gla_w_a2_2"][0],
    }
    arrays = {k: np.ascontiguousarray(v) for k, v in arrays.items()}
    nc = bacc.Bacc("TRN2", target_bir_lowering=False, num_devices=1, dynamic_dma_scratch_size=1024)
    args = [nc.dram_tensor(k, v.shape, F32, kind="ExternalInput").ap() for k, v in arrays.items()]
    out = nc.dram_tensor("out", (P, KD, T), F32, kind="ExternalOutput").ap()
    build(nc, *args, out)
    result = run_bass_kernel_spmd(nc, [arrays], core_ids=[0]).results[0]["out"]
    return np.ascontiguousarray(np.asarray(result).transpose(2, 1, 0).reshape(1, T, D))
```
